# Optimizing a Trainium2 kernel written in Bass

```python
import jax, jax.numpy as jnp
from jax import lax
import numpy as np

D_MODEL = 1024
BATCH = 1
SEQ = 256
DEPTH = 2

CHUNK = 64
LOOKBACK_CHUNKS = 8
BAND = (LOOKBACK_CHUNKS + 1) * CHUNK
N_MIXERS = 2
N_HEADS = 16
HEAD_DIM = D_MODEL // N_HEADS
MAX_REL = 128
N_REL = 2 * MAX_REL + 1
SSM_GROUP = 16
SSM_GROUPS = D_MODEL // SSM_GROUP
SSM_STATE = 64
DT_MIN = 1e-3
DT_MAX = 1e-1
N_EXPERT_GROUPS = 4
EXPERTS_PER_GROUP = 8
N_EXPERTS = N_EXPERT_GROUPS * EXPERTS_PER_GROUP
TOP_K = 2
D_EXPERT = D_MODEL // 4
RMS_EPS = 1e-6
NEG_BIG = -1e30

kernel_name = "interleaved_chunkattn_s5_hiermoe"

def rms_norm(x, g):
    x32 = x.astype(jnp.float32)
    y = x32 * lax.rsqrt(jnp.mean(x32 * x32, axis=-1, keepdims=True) + RMS_EPS)
    return (y * g.astype(jnp.float32)).astype(x.dtype)

def chunked_rel_attention(h, w_qkv, w_o, rel_bias):
    b, s, _ = h.shape
    nc = s // CHUNK
    q, k, v = jnp.split(h @ w_qkv, 3, axis=-1)
    q = q.reshape(b, nc, CHUNK, N_HEADS, HEAD_DIM)
    pad = ((0, 0), (LOOKBACK_CHUNKS * CHUNK, 0), (0, 0))

    def gather_band(t):
        t = jnp.pad(t, pad).reshape(b, nc + LOOKBACK_CHUNKS, CHUNK, N_HEADS, HEAD_DIM)
        return jnp.concatenate([t[:, j:j + nc] for j in range(LOOKBACK_CHUNKS + 1)], axis=2)

    kb, vb = gather_band(k), gather_band(v)
    scores = jnp.einsum('bcqhd,bckhd->bhcqk', q, kb).astype(jnp.float32) * (HEAD_DIM ** -0.5)
    q_pos = LOOKBACK_CHUNKS * CHUNK + jnp.arange(CHUNK)
    dist = q_pos[:, None] - jnp.arange(BAND)[None, :]
    rel_idx = jnp.clip(dist, -MAX_REL, MAX_REL) + MAX_REL
    bias = rel_bias[:, rel_idx].astype(jnp.float32)
    key_chunk = jnp.arange(nc)[:, None] - LOOKBACK_CHUNKS + jnp.arange(BAND)[None, :] // CHUNK
    valid = key_chunk >= 0
    scores = jnp.where(valid[None, None, :, None, :], scores + bias[None, :, None], NEG_BIG)
    p = jax.nn.softmax(scores, axis=-1).astype(vb.dtype)
    o = jnp.einsum('bhcqk,bckhd->bcqhd', p, vb).reshape(b, s, D_MODEL)
    return o @ w_o

def _complex_affine_combine(e1, e2):
    a1r, a1i, b1r, b1i = e1
    a2r, a2i, b2r, b2i = e2
    ar = a2r * a1r - a2i * a1i
    ai = a2r * a1i + a2i * a1r
    br = a2r * b1r - a2i * b1i + b2r
    bi = a2r * b1i + a2i * b1r + b2i
    return (ar, ai, br, bi)

def s5_mixer(h, lambda_re, lambda_im, log_step, b_re, b_im, c_re, c_im, d_skip, w_out):
    bsz, s, _ = h.shape
    h32 = h.astype(jnp.float32)
    u = h32.reshape(bsz, s, SSM_GROUPS, SSM_GROUP)
    lam_re = jnp.minimum(lambda_re.astype(jnp.float32), -1e-4)
    lam_im = lambda_im.astype(jnp.float32)
    step = jnp.exp(log_step.astype(jnp.float32))[:, None]
    decay = jnp.exp(lam_re * step)
    ang = lam_im * step
    abar_re = decay * jnp.cos(ang)
    abar_im = decay * jnp.sin(ang)
    denom = lam_re * lam_re + lam_im * lam_im
    num_re = abar_re - 1.0
    f_re = ((num_re * lam_re + abar_im * lam_im) / denom)[..., None]
    f_im = ((abar_im * lam_re - num_re * lam_im) / denom)[..., None]
    br = b_re.astype(jnp.float32)
    bi = b_im.astype(jnp.float32)
    bbar_re = f_re * br - f_im * bi
    bbar_im = f_re * bi + f_im * br
    bu_re = jnp.einsum('blgc,gpc->blgp', u, bbar_re)
    bu_im = jnp.einsum('blgc,gpc->blgp', u, bbar_im)
    a_re = jnp.broadcast_to(abar_re, bu_re.shape)
    a_im = jnp.broadcast_to(abar_im, bu_im.shape)
    _, _, x_re, x_im = lax.associative_scan(_complex_affine_combine, (a_re, a_im, bu_re, bu_im), axis=1)
    y = (jnp.einsum('blgp,gcp->blgc', x_re, c_re.astype(jnp.float32))
         - jnp.einsum('blgp,gcp->blgc', x_im, c_im.astype(jnp.float32)))
    y = y.reshape(bsz, s, D_MODEL) + d_skip.astype(jnp.float32) * h32
    y = jax.nn.gelu(y).astype(h.dtype)
    a, g = jnp.split(y @ w_out, 2, axis=-1)
    return a * jax.nn.sigmoid(g)

def hierarchical_moe(h, w_group_router, b_group_router, w_expert_router, b_expert_router,
                     w_gate, w_up, w_down):
    bsz, s, d = h.shape
    t = h.reshape(-1, d)
    group_logits = (t @ w_group_router).astype(jnp.float32) + b_group_router.astype(jnp.float32)
    group_prob = jax.nn.softmax(group_logits, axis=-1)
    g_prob, g_idx = lax.top_k(group_prob, 1)
    exp_logits = (jnp.einsum('td,gde->tge', t, w_expert_router).astype(jnp.float32)
                  + b_expert_router.astype(jnp.float32))
    sel_logits = jnp.take_along_axis(exp_logits, g_idx[:, :, None], axis=1)[:, 0]
    top_logits, e_idx = lax.top_k(sel_logits, TOP_K)
    e_w = jax.nn.softmax(top_logits, axis=-1) * g_prob
    global_idx = g_idx * EXPERTS_PER_GROUP + e_idx
    gates = jnp.sum(jax.nn.one_hot(global_idx, N_EXPERTS, dtype=jnp.float32) * e_w[..., None], axis=1)
    out = jnp.zeros(t.shape, jnp.float32)
    for e in range(N_EXPERTS):
        hid = jax.nn.silu(t @ w_gate[e]) * (t @ w_up[e])
        out = out + gates[:, e:e + 1] * (hid @ w_down[e]).astype(jnp.float32)
    return out.astype(h.dtype).reshape(bsz, s, d)

def setup_inputs(seed: int = 0) -> dict:
    key = jax.random.key(seed)
    ks = jax.random.split(key, 24)
    n_attn = (DEPTH + 1) // 2
    n_ssm = DEPTH // 2
    D, F = D_MODEL, D_EXPERT
    nrm = jax.random.normal
    f32 = jnp.float32
    log_step = jax.random.uniform(ks[5], (n_ssm, SSM_GROUPS), f32,
                                  float(np.log(DT_MIN)), float(np.log(DT_MAX)))
    lam_im_base = jnp.pi * jnp.arange(SSM_STATE, dtype=f32)
    return {
        "x": nrm(ks[0], (BATCH, SEQ, D), f32),
        "norm_mix": 1.0 + 0.02 * nrm(ks[1], (DEPTH, D), f32),
        "norm_ffn": 1.0 + 0.02 * nrm(ks[2], (DEPTH, D), f32),
        "norm_final": 1.0 + 0.02 * nrm(ks[3], (D,), f32),
        "attn_w_qkv": nrm(ks[4], (n_attn, D, 3 * D), f32) * D ** -0.5,
        "attn_w_o": nrm(ks[6], (n_attn, D, D), f32) * D ** -0.5,
        "attn_rel_bias": 0.1 * nrm(ks[7], (n_attn, N_HEADS, N_REL), f32),
        "ssm_lambda_re": -0.5 + 0.01 * nrm(ks[8], (n_ssm, SSM_GROUPS, SSM_STATE), f32),
        "ssm_lambda_im": lam_im_base + 0.01 * nrm(ks[9], (n_ssm, SSM_GROUPS, SSM_STATE), f32),
        "ssm_log_step": log_step,
        "ssm_b_re": nrm(ks[10], (n_ssm, SSM_GROUPS, SSM_STATE, SSM_GROUP), f32) * (2 * SSM_GROUP) ** -0.5,
        "ssm_b_im": nrm(ks[11], (n_ssm, SSM_GROUPS, SSM_STATE, SSM_GROUP), f32) * (2 * SSM_GROUP) ** -0.5,
        "ssm_c_re": nrm(ks[12], (n_ssm, SSM_GROUPS, SSM_GROUP, SSM_STATE), f32) * SSM_STATE ** -0.5,
        "ssm_c_im": nrm(ks[13], (n_ssm, SSM_GROUPS, SSM_GROUP, SSM_STATE), f32) * SSM_STATE ** -0.5,
        "ssm_d": nrm(ks[14], (n_ssm, D), f32),
        "ssm_w_out": nrm(ks[15], (n_ssm, D, 2 * D), f32) * D ** -0.5,
        "moe_w_group_router": nrm(ks[16], (DEPTH, D, N_EXPERT_GROUPS), f32) * D ** -0.5,
        "moe_b_group_router": 0.01 * nrm(ks[17], (DEPTH, N_EXPERT_GROUPS), f32),
        "moe_w_expert_router": nrm(ks[18], (DEPTH, N_EXPERT_GROUPS, D, EXPERTS_PER_GROUP), f32) * D ** -0.5,
        "moe_b_expert_router": 0.01 * nrm(ks[19], (DEPTH, N_EXPERT_GROUPS, EXPERTS_PER_GROUP), f32),
        "moe_w_gate": nrm(ks[20], (DEPTH, N_EXPERTS, D, F), f32) * D ** -0.5,
        "moe_w_up": nrm(ks[21], (DEPTH, N_EXPERTS, D, F), f32) * D ** -0.5,
        "moe_w_down": nrm(ks[22], (DEPTH, N_EXPERTS, F, D), f32) * F ** -0.5,
    }

def reference(x, norm_mix, norm_ffn, norm_final, attn_w_qkv, attn_w_o, attn_rel_bias,
              ssm_lambda_re, ssm_lambda_im, ssm_log_step, ssm_b_re, ssm_b_im, ssm_c_re, ssm_c_im,
              ssm_d, ssm_w_out, moe_w_group_router, moe_b_group_router, moe_w_expert_router,
              moe_b_expert_router, moe_w_gate, moe_w_up, moe_w_down):
    h = x
    for i in range(DEPTH):
        j = i // N_MIXERS
        hn = rms_norm(h, norm_mix[i])
        if i % N_MIXERS == 0:
            mix = chunked_rel_attention(hn, attn_w_qkv[j], attn_w_o[j], attn_rel_bias[j])
        else:
            mix = s5_mixer(hn, ssm_lambda_re[j], ssm_lambda_im[j], ssm_log_step[j],
                           ssm_b_re[j], ssm_b_im[j], ssm_c_re[j], ssm_c_im[j],
                           ssm_d[j], ssm_w_out[j])
        h = h + mix
        hn = rms_norm(h, norm_ffn[i])
        h = h + hierarchical_moe(hn, moe_w_group_router[i], moe_b_group_router[i],
                                 moe_w_expert_router[i], moe_b_expert_router[i],
                                 moe_w_gate[i], moe_w_up[i], moe_w_down[i])
    return rms_norm(h, norm_final)


_drawn_inputs = setup_inputs


def setup_inputs(seed=0):
    import zlib

    import numpy as np

    out = dict(_drawn_inputs(seed))
    spreads = {}
    factors = {}
    for name, (base, spread) in spreads.items():
        noise = np.random.default_rng([zlib.crc32(name.encode()), seed]).standard_normal(out[name].shape)
        drawn = base * np.exp(spread * noise) if base else spread * noise
        out[name] = __import__('jax').numpy.asarray(drawn.astype(out[name].dtype))
    for name, factor in factors.items():
        out[name] = (out[name] * factor).astype(out[name].dtype)
    return out
```

```python
from contextlib import ExitStack

import numpy as np

import concourse.bass as bass
from concourse import mybir

F32 = mybir.dt.float32
F32R = mybir.dt.float32r
I32 = mybir.dt.int32
ALU = mybir.AluOpType
ACT = mybir.ActivationFunctionType
AX = mybir.AxisListType

P = 128
D = 1024
T = 256
TT = T // P
KT = D // P
H, HD = 16, 64
HP = H // 2
CH = 64
MAXREL = 128
NREL = 2 * MAXREL + 1
G, GC, NS = 64, 16, 64
ST = G * NS // P
NCH = T // CH
EG, EPG = 4, 8
E = EG * EPG
F = D // 4
FT = F // P
CAP = 64
WINDOWS = T // CAP
QUAD = 4
QS = QUAD * CAP
NQ = E // QUAD
NR = EG + E
EPS = 1e-6
NEG = -1e30
RING = 4
SLOT = 3 * D * F // P
REV = 2 * T - 1 - P
QCOL = 3 * D // RING
WCOL = D // RING
VCOL = 256


def trunk_program(nc, a, out):
    ctx = ExitStack()
    with ctx:
        base = (nc.sbuf_base + 63) // 64 * 64
        where = [base]

        def fixed(name, shape, dt=F32):
            n = int(np.prod(shape[1:])) * 4
            t = nc.alloc_sbuf_tensor_at(name, shape, dt, offset=where[0])
            where[0] += (n + 63) // 64 * 64
            return t

        def sem(name):
            return ctx.enter_context(nc.semaphore(name))

        ring = fixed("ring", [P, RING, SLOT])
        x = fixed("x", [P, TT, D])
        normw = fixed("normw", [P, D])
        xnT = fixed("xnT", [P, KT, T])
        bT = fixed("bT", [P, 2, KT, P])
        cT = fixed("cT", [P, 3, ST, 2 * GC])
        par = fixed("par", [P, 5, ST])
        router_w = fixed("router_w", [P, 2, KT, NR])
        router_b = fixed("router_b", [P, 2, NR])
        ident = fixed("ident", [P, P])
        before = fixed("before", [P, P])
        ones = fixed("ones", [P, P])
        slot_iota = fixed("slot_iota", [P, CAP])
        rev_e = fixed("rev_e", [P, E])
        rev_g = fixed("rev_g", [P, EG])
        small = fixed("small", [P, 12, TT])
        lam = fixed("lam", [ST, 2, P])
        logstep = fixed("logstep", [ST, 2])
        dskip = fixed("dskip", [P, KT])
        rank = fixed("rank", [P, TT, E])
        gates = fixed("gates", [P, TT, E])
        route = fixed("route", [P, 6, TT, E])
        glog = fixed("glog", [P, TT, NR])
        sel = fixed("sel", [P, TT, E])
        count_i = fixed("count_i", [P, 2], I32)
        arena = where[0]

        def at(name, shape, off, dt=F32):
            return nc.alloc_sbuf_tensor_at(name, shape, dt, offset=arena + 4 * off)

        qkT = at("qkT", [P, 2 * HP, T], 0)
        v = at("v", [P, TT, D], 4096)
        bias = at("bias", [P, H, 3 * P], 6144)
        s_sb = at("s_sb", [P, 2, 2, 3 * P], 12288)
        pT = at("pT", [P, 2, 3 * P], 13824)
        oT = xnT
        stat = at("stat", [P, 3, 2, 2, 2], 14592)
        b_raw = at("b_raw", [P, 2, ST, GC], 6144)
        b_blk = at("b_blk", [P, 2, ST, 2 * GC], 7168)
        b_tmp = at("b_tmp", [P, 2, ST, GC], 9216)
        c_raw = at("c_raw", [P, 2, KT, 2, NS], 10240)
        disc = at("disc", [ST, 24, P], 3072)
        rb_row = at("rb_row", [H, NREL], 12288)
        rb_rev = at("rb_rev", [H, REV], 12288 + 320)
        xn = at("xn", [P, TT, D], 0)
        xg = at("xg", [P, KT, QS], 0)
        xh = at("xh", [P, TT, D], 2048, F32R)
        xl = at("xl", [P, TT, D], 4096, F32R)
        yh = at("yh", [P, 2, D], 6144, F32R)
        yl = at("yl", [P, 2, D], 8192, F32R)
        pick = at("pick", [P, TT, QUAD, CAP], 10240, F32R)
        pickT = at("pickT", [P, 2, T], 10752, F32R)
        sg = at("sg", [P, 2, F], 11264)
        hid = at("hid", [P, 2, F], 11776)
        hidT = at("hidT", [P, 2, FT, P], 12288)
        gq = at("gq", [P, TT, QUAD], 12800)
        gslot = at("gslot", [P, 2], 12816)
        cosT = at("cosT", [P, ST, CH], 0 + 2048)
        sinT = at("sinT", [P, ST, CH], 4096)
        decayT = at("decayT", [P, 4, 4, 2, CH], 6144)
        tb = at("tb", [P, 4, 512], 8192)
        db = at("db", [P, 2, 512], 10240)
        zb = at("zb", [P, 2, 512], 11264)
        qb = at("qb", [P, 4, 512], 12288)
        yT = at("yT", [P, KT, T], 0)
        sc = at("sc", [P, 16, ST], 14336)
        dtmp = tb[:, 0, :]
        sig = at("sig", [P, 2, WCOL], 4096)
        assert arena + 4 * 14848 <= nc.sbuf_usable_end, (arena, nc.sbuf_usable_end)

        ps = ctx.enter_context(nc.psum_tensor("ps", [P, 8, 512], F32))
        rev_dram = nc.dram_tensor("rev_bias", (H, REV), F32).ap()

        x_loaded, small_loaded = sem("x_loaded"), sem("small_loaded")
        braw_loaded, craw_loaded = sem("braw_loaded"), sem("craw_loaded")
        rb_loaded, rev_ready, rev_stored, bias_loaded = (sem(n) for n in ("rb_loaded", "rev_ready", "rev_stored", "bias_loaded"))
        normw_loaded = sem("normw_loaded")
        const_ready, pool_chain = sem("const_ready"), sem("pool_chain")
        dve_chain = sem("dve_chain")
        slot_full = [sem(f"slot_full{s}") for s in range(RING)]
        slot_free = [sem(f"slot_free{s}") for s in range(RING)]
        ms_ready, rms_ready, xn_ready = sem("ms_ready"), sem("rms_ready"), sem("xn_ready")
        xh_ready, xl_ready = sem("xh_ready"), sem("xl_ready")
        tr_done, tr_evac = sem("tr_done"), sem("tr_evac")
        qkv_done, qkv_evac = sem("qkv_done"), sem("qkv_evac")
        step_ready, step_exp, ang_ready, ang_sin = (sem(n) for n in ("step_ready", "step_exp", "ang_ready", "ang_sin"))
        par_ready, par_turned, c_turned, b_ready, b_turned, prep_done = (
            sem(n) for n in ("par_ready", "par_turned", "c_turned", "b_ready", "b_turned", "prep_done"))
        s_done, nmax_ready, exp_done, p_ready, pt_done, pt_evac_a = (
            sem(n) for n in ("s_done", "nmax_ready", "exp_done", "p_ready", "pt_done", "pt_evac_a"))
        o_done, o_evac = sem("o_done"), sem("o_evac")
        proj_done, proj_added = sem("proj_done"), sem("proj_added")
        logit_done, sel_ready, rank_done = (sem(n) for n in ("logit_done", "sel_ready", "rank_done"))
        glog_ready, gexp_done, e2_ready, e2_done = (sem(n) for n in ("glog_ready", "gexp_done", "e2_ready", "e2_done"))
        count_ready = sem("count_ready")
        bu_done, bu_used, q_ready, q_used, y_done, y_used, gelu_in, gelu_done = (
            sem(n) for n in ("bu_done", "bu_used", "q_ready", "q_used", "y_done", "y_used", "gelu_in", "gelu_done"))
        glu_done, sig_done, glu_added = sem("glu_done"), sem("sig_done"), sem("glu_added")
        out_stored = sem("out_stored")
        xnT_free = sem("xnT_free")

        class MoeSems:

            def __init__(self, tag):
                self.pick_ready = sem(f"pick_ready_{tag}")
                self.gath_done = sem(f"gath_done_{tag}")
                self.xg_evac = sem(f"xg_evac_{tag}")
                self.turn_done = sem(f"turn_done_{tag}")
                self.pt_evac = sem(f"pt_evac_{tag}")
                self.gslot_ready = sem(f"gslot_ready_{tag}")
                self.gu_done = sem(f"gu_done_{tag}")
                self.silu_done = sem(f"silu_done_{tag}")
                self.hid_ready = sem(f"hid_ready_{tag}")
                self.hT_done = sem(f"hT_done_{tag}")
                self.hT_evac = sem(f"hT_evac_{tag}")
                self.down_done = sem(f"down_done_{tag}")
                self.yh_done = sem(f"yh_done_{tag}")
                self.yl_done = sem(f"yl_done_{tag}")
                self.comb_done = sem(f"comb_done_{tag}")
                self.x_added = sem(f"x_added_{tag}")
                self.chain = sem(f"chain_{tag}")
                self.window = sem(f"window_{tag}")
                self.ring_passed = sem(f"ring_passed_{tag}")
                self.full = None

        main = [MoeSems(f"l{i}") for i in range(2)]
        more = [MoeSems(f"more{i}") for i in range(2)]
        for i in range(2):
            more[i].full = [sem(f"more_full{i}_{s}") for s in range(RING)]

        def full_before(layer):
            return 32 + layer * (NQ * 48 + 32)

        block = ctx.enter_context(nc.Block())

        class Chain:

            def __init__(self, eng, s, start=0):
                self.eng, self.s, self.start, self.n = eng, s, start, 0

            def __call__(self, ins):
                self.n += 1
                ins.then_inc(self.s, 1)
                self.eng.wait_ge(self.s, self.start + self.n)

        @block.sync
        def _(sp):
            sp.dma_start(x[:], a["x"][0].rearrange("(t p) d -> p t d", p=P)).then_inc(x_loaded, 16)
            wqkv = a["attn_w_qkv"][0].rearrange("(k p) n -> p k n", p=P)
            wo = a["attn_w_o"][0].rearrange("(k p) n -> p k n", p=P)
            wout = a["ssm_w_out"][0].rearrange("(k p) n -> p k n", p=P)
            for s in range(RING):
                sp.dma_start(ring[:, s, :].rearrange("p (k n) -> p k n", k=KT),
                             wqkv[:, :, s * QCOL:(s + 1) * QCOL]).then_inc(slot_full[s], 16)
            for s in range(RING):
                sp.wait_ge(slot_free[s], 1)
                sp.dma_start(ring[:, s, 0:KT * WCOL].rearrange("p (k n) -> p k n", k=KT),
                             wo[:, :, s * WCOL:(s + 1) * WCOL]).then_inc(slot_full[s], 16)

            def expert(layer, e, s, full):
                r = E * layer + e
                sl = ring[:, s, :]
                wg = a["moe_w_gate"].rearrange("l e (p c) f -> p (l e) (c f)", p=P)
                wu = a["moe_w_up"].rearrange("l e (p c) f -> p (l e) (c f)", p=P)
                wd = a["moe_w_down"].rearrange("l e (p j) d -> p (l e) (j d)", p=P)
                n = D * F // P
                for i, w in enumerate((wg, wu, wd)):
                    src = w[:, bass.ds(r, 1), :].rearrange("p o n -> p (o n)")
                    sp.dma_start(sl[:, i * n:(i + 1) * n], src).then_inc(full[s], 16)

            def experts(layer):
                S = main[layer]
                for s in range(QUAD):
                    sp.wait_ge(slot_free[s], 2 + layer)
                    expert(layer, s, s, slot_full)
                with sp.Fori(1, NQ) as it:
                    for s in range(QUAD):
                        sp.wait_ge(S.down_done, 2 * it - 1 + s // 2)
                        expert(layer, QUAD * it + s, s, slot_full)
                sp.wait_ge(count_ready, layer + 1)
                most = sp.value_load(count_i[0:1, layer:layer + 1], min_val=0, max_val=T)
                R = more[layer]
                with sp.If(most > CAP):
                    sp.wait_ge(S.down_done, 2 * NQ)
                    with sp.Fori(0, WINDOWS - 1) as w:
                        with sp.Fori(0, NQ) as it:
                            for s in range(QUAD):
                                sp.wait_ge(R.ring_passed, NQ * w + it + 1)
                                expert(layer, QUAD * it + s, s, R.full)
                    sp.wait_ge(R.down_done, 2 * NQ * (WINDOWS - 1))
                sp.nop()

            experts(0)
            for s in range(RING):
                sp.wait_ge(main[0].down_done, 2 * NQ - 1 + s // 2)
                dst = ring[:, s, 0:KT * 2 * WCOL].rearrange("p (k h n) -> p k h n", k=KT, h=2)
                for h in range(2):
                    sp.dma_start(dst[:, :, h, :], wout[:, :, h * D + s * WCOL:h * D + (s + 1) * WCOL])\
                      .then_inc(slot_full[s], 16)
            experts(1)
            for tt in range(TT):
                sp.wait_ge(xn_ready, 2 * 4 + tt + 1)
                sp.dma_start(out[0, tt * P:(tt + 1) * P, :], xn[:, tt, :]).then_inc(out_stored, 16)
            sp.wait_ge(out_stored, 16 * TT)

        @block.gpsimd
        def _(pool):
            pc = Chain(pool, pool_chain)
            norms = [a["norm_mix"][0], a["norm_ffn"][0], a["norm_mix"][1], a["norm_ffn"][1], a["norm_final"]]

            def load_normw(i):
                if i:
                    pool.wait_ge(xn_ready, 2 * i)
                pool.dma_start(normw[:], norms[i].rearrange("(o d) -> o d", o=1).to_broadcast([P, D]))\
                    .then_inc(normw_loaded, 16)

            load_normw(0)
            nc.gpsimd.memset(ones[:], 1.0).then_inc(const_ready, 1)
            pc(nc.gpsimd.memset(ident[:], 0.0))
            pc(nc.gpsimd.memset(before[:], 1.0))
            nc.gpsimd.affine_select(out=ident[:], in_=ident[:], compare_op=ALU.not_equal, fill=1.0, base=0,
                                    pattern=[[-1, P]], channel_multiplier=1).then_inc(const_ready, 1)
            nc.gpsimd.affine_select(out=before[:], in_=before[:], compare_op=ALU.is_gt, fill=0.0, base=0,
                                    pattern=[[1, P]], channel_multiplier=-1).then_inc(const_ready, 1)
            nc.gpsimd.iota(slot_iota[:], pattern=[[1, CAP]], base=0, channel_multiplier=0,
                           allow_small_or_imprecise_dtypes=True).then_inc(const_ready, 1)
            nc.gpsimd.iota(rev_e[:], pattern=[[-1, E]], base=E, channel_multiplier=0,
                           allow_small_or_imprecise_dtypes=True).then_inc(const_ready, 1)
            nc.gpsimd.iota(rev_g[:], pattern=[[-1, EG]], base=EG, channel_multiplier=0,
                           allow_small_or_imprecise_dtypes=True).then_inc(const_ready, 1)
            nc.gpsimd.memset(b_blk[:], 0.0).then_inc(const_ready, 1)
            nc.gpsimd.memset(cT[:], 0.0).then_inc(const_ready, 1)
            load_normw(1)
            pool.wait_ge(rev_ready, 1)
            pool.dma_start(rev_dram, rb_rev[:]).then_inc(rev_stored, 16)
            pool.wait_ge(rev_stored, 16)
            pool.wait_ge(prep_done, 1)
            ap = rev_dram
            lo = bass.AP(tensor=ap.tensor, offset=T - P, ap=[[1, P], [REV, H], [1, P]])
            hi = bass.AP(tensor=ap.tensor, offset=0, ap=[[1, P], [REV, H], [1, 2 * P]])
            pool.dma_start(bias[:, :, 0:P], lo).then_inc(bias_loaded, 16)
            pool.dma_start(bias[:, :, P:3 * P], hi).then_inc(bias_loaded, 16)
            for i in range(2, 5):
                load_normw(i)

        @block.scalar
        def _(act):
            n = 0
            lre = a["ssm_lambda_re"][0].rearrange("(s g) p -> s (g p)", g=2)
            lim = a["ssm_lambda_im"][0].rearrange("(s g) p -> s (g p)", g=2)
            act.dma_start(lam[:, 0, :], lre).then_inc(small_loaded, 16)
            act.dma_start(lam[:, 1, :], lim).then_inc(small_loaded, 16)
            act.dma_start(logstep[:], a["ssm_log_step"][0].rearrange("(s g) -> s g", g=2)).then_inc(small_loaded, 16)
            act.dma_start(rb_row[:], a["attn_rel_bias"][0]).then_inc(rb_loaded, 16)
            for r, name in enumerate(("ssm_c_re", "ssm_c_im")):
                for dup in range(2):
                    act.dma_start(c_raw[:, r, :, dup, :], a[name][0].rearrange("(i g) c p -> (g c) i p", g=P // GC))\
                       .then_inc(craw_loaded, 16)
            for r, name in enumerate(("ssm_b_re", "ssm_b_im")):
                for g2 in range(2):
                    src = a[name][0].rearrange("(s g) p c -> g p s c", g=2)[g2]
                    act.dma_start(b_raw[NS * g2:NS * (g2 + 1), r], src).then_inc(braw_loaded, 16)
            for layer in range(2):
                wr = router_w[:, layer]
                act.dma_start(wr[:, :, 0:EG], a["moe_w_group_router"][layer].rearrange("(k p) g -> p k g", p=P))\
                   .then_inc(small_loaded, 16)
                for g in range(EG):
                    act.dma_start(wr[:, :, EG + g * EPG:EG + (g + 1) * EPG],
                                  a["moe_w_expert_router"][layer, g].rearrange("(k p) e -> p k e", p=P))\
                       .then_inc(small_loaded, 16)
                act.dma_start(router_b[:, layer, 0:EG],
                              a["moe_b_group_router"][layer].rearrange("(o g) -> o g", o=1).to_broadcast([P, EG]))\
                   .then_inc(small_loaded, 16)
                act.dma_start(router_b[:, layer, EG:],
                              a["moe_b_expert_router"][layer].rearrange("(o g) e -> o (g e)", o=1).to_broadcast([P, E]))\
                   .then_inc(small_loaded, 16)
            act.dma_start(dskip[:], a["ssm_d"][0].rearrange("(k p) -> p k", p=P),
                          allow_slow_non_contiguous=True).then_inc(small_loaded, 16)

            def norm_root(i):
                act.wait_ge(ms_ready, i + 1)
                nc.scalar.activation(small[:, 2, :], small[:, 1, :], ACT.Sqrt).then_inc(rms_ready, 1)

            def turn_evac(i):
                for g in range(4):
                    act.wait_ge(tr_done, 4 * i + g + 1)
                    nc.scalar.copy(xnT[:, 2 * g:2 * g + 2, :], ps[:, g % 2, :].rearrange("p (k t) -> p k t", k=2))\
                      .then_inc(tr_evac, 1)

            norm_root(0)
            turn_evac(0)

            def qkv_evacs(u0, u1):
                for u in range(u0, u1):
                    act.wait_ge(qkv_done, u + 1)
                    if u < 16:
                        dst = qkT[:, u, :]
                    else:
                        c, tt = divmod(u - 16, 2)
                        dst = v[:, tt, c * VCOL:(c + 1) * VCOL]
                    if u == 12:
                        act.wait_ge(par_ready, 1)
                        act.wait_ge(par_turned, 1)
                    src = ps[:, u % 3, 0:VCOL]
                    if u < HP:
                        dst = dst.rearrange("p (t q) -> p t q", t=TT)
                        src = src.rearrange("p (t q) -> p t q", t=TT)[:, :, ::-1]
                    nc.scalar.copy(dst, src).then_inc(qkv_evac, 1)

            act.wait_ge(step_ready, 1)
            nc.scalar.activation(disc[:, 0, 0:2], logstep[:], ACT.Exp).then_inc(step_exp, 1)
            act.wait_ge(step_ready, 2)
            nc.scalar.activation(disc[:, 2, :], disc[:, 1, :], ACT.Exp).then_inc(step_exp, 1)
            act.wait_ge(ang_ready, 1)
            nc.scalar.activation(disc[:, 8:10, :], disc[:, 6:8, :], ACT.Sin).then_inc(ang_sin, 1)
            qkv_evacs(0, 24)

            def att_evac(hp):
                act.wait_ge(pt_done, hp + 1)
                nc.scalar.copy(pT[:], ps[:, 4:6, 0:3 * P]).then_inc(pt_evac_a, 1)
                act.wait_ge(o_done, hp + 1)
                nc.scalar.copy(oT[:, hp, :].rearrange("p (t q) -> p t q", t=TT),
                               ps[:, 6 + hp % 2, 0:T].rearrange("p (t q) -> p t q", t=TT)[:, :, ::-1]).then_inc(o_evac, 1)

            for hp in range(HP):
                act.wait_ge(nmax_ready, hp + 1)
                for h in range(2):
                    for qt in range(2):
                        w = slice(0, P) if qt == 0 else slice(P, 3 * P)
                        sl = s_sb[:, hp % 2, h, w]
                        ins = nc.scalar.activation(sl, sl, ACT.Exp, bias=stat[:, 0, hp % 2, h, qt:qt + 1],
                                                   accum_out=stat[:, 1, hp % 2, h, qt:qt + 1])
                        ins.then_inc(exp_done, 1)
                if hp:
                    att_evac(hp - 1)
            att_evac(HP - 1)

            def moe_act(S, n):
                for u in range(4):
                    act.wait_ge(S.gath_done, 4 * n + u + 1)
                    nc.scalar.copy(xg[:, 2 * u:2 * u + 2, :], ps[:, u % 2, :].rearrange("p (c s) -> p c s", c=2))\
                      .then_inc(S.xg_evac, 1)
                act.wait_ge(S.turn_done, n + 1)
                nc.scalar.copy(pickT[:], ps[:, 5, :].rearrange("p (r t) -> p r t", r=2)).then_inc(S.pt_evac, 1)
                for r in range(2):
                    act.wait_ge(S.gu_done, 2 * n + r + 1)
                    nc.scalar.activation(sg[:, r, :], ps[:, 2 + r, 0:F], ACT.Silu).then_inc(S.silu_done, 1)
                for r in range(2):
                    act.wait_ge(S.hT_done, 2 * n + r + 1)
                    nc.scalar.copy(hidT[:, r], ps[:, 4, 0:F].rearrange("p (j s) -> p j s", j=FT)).then_inc(S.hT_evac, 1)
                    act.wait_ge(S.down_done, 2 * n + r + 1)
                    act.wait_ge(S.gslot_ready, 2 * n + 2)
                    nc.scalar.activation(yh[:, r, :].rearrange("p (b n) -> p b n", b=2), ps[:, 6:8, :], ACT.Copy,
                                         scale=gslot[:, r:r + 1]).then_inc(S.yh_done, 1)

            def layer_moe(layer):
                i = 2 * layer + 1
                norm_root(i)
                for tt in range(TT):
                    act.wait_ge(xn_ready, 2 * i + tt + 1)
                    nc.scalar.copy(xh[:, tt, :], xn[:, tt, :]).then_inc(xh_ready, 1)
                turn_evac(i)
                act.wait_ge(glog_ready, layer + 1)
                nc.scalar.activation(route[:, 0, :, 0:EG], route[:, 1, :, 0:EG], ACT.Exp).then_inc(gexp_done, 1)
                act.wait_ge(e2_ready, layer + 1)
                nc.scalar.activation(small[:, 9, :], small[:, 8, :], ACT.Exp).then_inc(e2_done, 1)
                with act.Fori(0, NQ) as it:
                    moe_act(main[layer], it)
                act.wait_ge(count_ready, layer + 1)
                most = act.value_load(count_i[0:1, layer:layer + 1], min_val=0, max_val=T)
                with act.If(most > CAP):
                    with act.Fori(0, WINDOWS - 1) as w:
                        with act.Fori(0, NQ) as it:
                            moe_act(more[layer], w * NQ + it)
                act.nop()

            layer_moe(0)
            norm_root(2)
            turn_evac(2)
            for k in range(NCH):
                act.wait_ge(gelu_in, k + 1)
                nc.scalar.activation(yT[:, :, k * CH:(k + 1) * CH],
                                     tb[:, 1, :].rearrange("p (i t) -> p i t", i=KT), ACT.Gelu_apprx_tanh)\
                  .then_inc(gelu_done, 1)
            for u in range(2 * RING):
                act.wait_ge(glu_done, u + 1)
                if u >= 2:
                    act.wait_ge(glu_added, u - 1)
                nc.scalar.activation(sig[:, u % 2, :], ps[:, u % 2, WCOL:2 * WCOL], ACT.Sigmoid).then_inc(sig_done, 1)
            layer_moe(1)
            norm_root(4)

        @block.vector
        def _(dve):
            lk = Chain(dve, dve_chain)
            V = nc.vector

            def norm(i):
                ss, ms, rt, r0, t0, t1, rs = (small[:, j, :] for j in (0, 1, 2, 3, 4, 5, 6))
                for tt in range(TT):
                    lk(V.tensor_tensor_reduce(out=xn[:, tt, :], in0=x[:, tt, :], in1=x[:, tt, :], scale=1.0, scalar=0.0,
                                              op0=ALU.mult, op1=ALU.add, accum_out=ss[:, tt:tt + 1]))
                V.tensor_scalar(ms, ss, 1.0 / D, EPS, ALU.mult, ALU.add).then_inc(ms_ready, 1)
                dve.wait_ge(rms_ready, i + 1)
                lk(V.reciprocal(r0, rt))
                lk(V.tensor_tensor(t0, r0, r0, ALU.mult))
                lk(V.tensor_tensor(t1, t0, ms, ALU.mult))
                lk(V.tensor_scalar(t0, t1, -0.5, 1.5, ALU.mult, ALU.add))
                lk(V.tensor_tensor(rs, r0, t0, ALU.mult))
                dve.wait_ge(normw_loaded, 16 * (i + 1))
                for tt in range(TT):
                    V.scalar_tensor_tensor(out=xn[:, tt, :], in0=x[:, tt, :], scalar=rs[:, tt:tt + 1], in1=normw[:],
                                           op0=ALU.mult, op1=ALU.mult).then_inc(xn_ready, 1)

            dve.wait_ge(x_loaded, 16)
            norm(0)

            dve.wait_ge(rb_loaded, 16)
            far = REV - 2 * MAXREL
            lk(V.tensor_copy(rb_rev[:, far:], rb_row[:, NREL - 1:0:-1]))
            V.tensor_copy(rb_rev[:, 0:far], rb_row[:, NREL - 1:NREL].to_broadcast([H, far])).then_inc(rev_ready, 1)

            dve.wait_ge(small_loaded, 16 * 18)
            d = disc
            step = d[:, 0, 0:2]
            lr, li, dec = d[:, 3, :], lam[:, 1, :], d[:, 2, :]

            def by_group(ap):
                return ap.rearrange("s (g p) -> s g p", g=2)

            lk(V.tensor_scalar(lr, lam[:, 0, :], -1e-4, None, ALU.min))
            lk(V.tensor_copy(d[:, 4, 0:2], logstep[:]))
            V.memset(d[:, 0, 2:4], 0.0).then_inc(step_ready, 1)
            dve.wait_ge(step_exp, 1)
            stepb = step.unsqueeze(2).to_broadcast([ST, 2, NS])
            V.tensor_tensor(by_group(d[:, 1, :]), by_group(lr), stepb, ALU.mult).then_inc(step_ready, 1)
            ang, cyc, t1, t2 = d[:, 5, :], d[:, 10, :], d[:, 11, :], d[:, 12, :]
            lk(V.tensor_tensor(by_group(ang), by_group(li), stepb, ALU.mult))
            MAGIC = float(1.5 * 2 ** 23)
            c1 = 6.28125
            c2 = float(np.float32(np.round((2 * np.pi - c1) * 2 ** 24) / 2 ** 24))
            c3 = float(2 * np.pi - c1 - c2)
            lk(V.tensor_scalar(cyc, ang, float(1 / (2 * np.pi)), None, ALU.mult))
            lk(V.tensor_scalar(t1, cyc, MAGIC, None, ALU.add))
            lk(V.tensor_scalar(cyc, t1, MAGIC, None, ALU.subtract))
            lk(V.scalar_tensor_tensor(out=t1, in0=cyc, scalar=-c1, in1=ang, op0=ALU.mult, op1=ALU.add))
            lk(V.scalar_tensor_tensor(out=t2, in0=cyc, scalar=-c2, in1=t1, op0=ALU.mult, op1=ALU.add))
            lk(V.scalar_tensor_tensor(out=t1, in0=cyc, scalar=-c3, in1=t2, op0=ALU.mult, op1=ALU.add))
            PI = float(np.nextafter(np.float32(np.pi), np.float32(0)))
            lk(V.tensor_scalar(d[:, 6, :], t1, -PI, PI, ALU.max, ALU.min))
            lk(V.tensor_scalar(t2, d[:, 6, :], -1.0, None, ALU.mult))
            lk(V.tensor_tensor(t1, d[:, 6, :], t2, ALU.max))
            V.tensor_scalar(d[:, 7, :], t1, -1.0, float(np.pi / 2), ALU.mult, ALU.add).then_inc(ang_ready, 1)
            dve.wait_ge(ang_sin, 1)
            dve.wait_ge(step_exp, 2)
            sin, cos = d[:, 8, :], d[:, 9, :]
            are, aim, den, nre = d[:, 13, :], d[:, 14, :], d[:, 15, :], d[:, 16, :]
            lk(V.tensor_tensor(are, dec, cos, ALU.mult))
            lk(V.tensor_tensor(aim, dec, sin, ALU.mult))
            lk(V.tensor_scalar(nre, are, -1.0, None, ALU.add))
            lk(V.tensor_tensor(t1, lr, lr, ALU.mult))
            lk(V.tensor_tensor(t2, li, li, ALU.mult))
            lk(V.tensor_tensor(den, t1, t2, ALU.add))
            lk(V.reciprocal(d[:, 17, :], den))
            lk(V.tensor_tensor(t1, nre, lr, ALU.mult))
            lk(V.tensor_tensor(t2, aim, li, ALU.mult))
            lk(V.tensor_tensor(den, t1, t2, ALU.add))
            lk(V.tensor_tensor(d[:, 18, :], den, d[:, 17, :], ALU.mult))
            lk(V.tensor_tensor(t1, aim, lr, ALU.mult))
            lk(V.tensor_tensor(t2, nre, li, ALU.mult))
            lk(V.tensor_tensor(den, t1, t2, ALU.subtract))
            V.tensor_tensor(d[:, 19, :], den, d[:, 17, :], ALU.mult).then_inc(par_ready, 1)

            dve.wait_ge(const_ready, 8)
            dve.wait_ge(c_turned, 1)
            for r in range(2):
                for half in range(2):
                    for g2 in range(2):
                        part = slice(NS * g2, NS * (g2 + 1))
                        src = ps[part, 4 + 2 * r + half, :].rearrange("p (s g c) -> p s g c", g=2, c=GC)[:, :, g2, :]
                        rows = slice(16 * half, 16 * (half + 1))
                        cols = slice(GC * g2, GC * (g2 + 1))
                        if r == 0:
                            V.tensor_copy(cT[part, 0, rows, cols], src)
                            lk(V.tensor_scalar(cT[part, 1, rows, cols], src, -1.0, None, ALU.mult))
                        else:
                            lk(V.tensor_scalar(cT[part, 2, rows, cols], src, -1.0, None, ALU.mult))
            dve.wait_ge(par_turned, 1)
            lk(V.tensor_copy(par[:], ps[:, 3, 0:5 * ST].rearrange("p (j s) -> p j s", j=5)))
            dve.wait_ge(braw_loaded, 64)
            fre = par[:, 0, :].unsqueeze(2).to_broadcast([P, ST, GC])
            fim = par[:, 1, :].unsqueeze(2).to_broadcast([P, ST, GC])
            for r, (fa, fb, op) in enumerate(((fre, fim, ALU.subtract), (fim, fre, ALU.add))):
                lk(V.tensor_tensor(b_tmp[:, 0], b_raw[:, 0], fa, ALU.mult))
                lk(V.tensor_tensor(b_tmp[:, 1], b_raw[:, 1], fb, ALU.mult))
                for g2 in range(2):
                    part = slice(NS * g2, NS * (g2 + 1))
                    ins = V.tensor_tensor(b_blk[part, r, :, GC * g2:GC * (g2 + 1)], b_tmp[part, 0], b_tmp[part, 1], op)
                    if r == 1 and g2 == 1:
                        ins.then_inc(b_ready, 1)
                    else:
                        lk(ins)
            dve.wait_ge(b_turned, 1)
            lk(V.tensor_copy(bT[:], ps[:, 4:8, :].rearrange("p (r h) (i q) -> p r (h i) q", r=2, q=P)))
            lk(V.memset(sc[:, 15, :], 0.0))
            V.memset(sc[:, 14, :], 0.0).then_inc(prep_done, 1)

            dve.wait_ge(bias_loaded, 32)
            for col in (P - CH, 3 * P - CH):
                lk(V.memset(bias[P - CH:P, :, col:col + CH], NEG))

            def att_norm(hp):
                b = hp % 2
                dve.wait_ge(exp_done, 4 * hp + 4)
                lk(V.reciprocal(stat[:, 2, b], stat[:, 1, b]))
                for qt, w in ((0, slice(0, P)), (1, slice(P, 3 * P))):
                    n = w.stop - w.start
                    V.tensor_tensor(s_sb[:, b, :, w], s_sb[:, b, :, w],
                                    stat[:, 2, b, :, qt:qt + 1].to_broadcast([P, 2, n]), ALU.mult).then_inc(p_ready, 1)

            for hp in range(HP):
                b = hp % 2
                dve.wait_ge(s_done, hp + 1)
                if hp >= 2:
                    dve.wait_ge(pt_done, hp - 1)
                lk(V.scalar_tensor_tensor(out=s_sb[:, b], in0=ps[:, 2 * b:2 * b + 2, 0:3 * P], scalar=HD ** -0.5,
                                          in1=bias[:, 2 * hp:2 * hp + 2, :], op0=ALU.mult, op1=ALU.add))
                lk(V.tensor_reduce(stat[:, 0, b, :, 0:1], s_sb[:, b, :, 0:P], AX.X, ALU.max, negate=True))
                V.tensor_reduce(stat[:, 0, b, :, 1:2], s_sb[:, b, :, P:3 * P], AX.X, ALU.max, negate=True)\
                 .then_inc(nmax_ready, 1)
                if hp:
                    att_norm(hp - 1)
            att_norm(HP - 1)

            for u in range(2 * RING):
                s, tt = divmod(u, 2)
                dve.wait_ge(proj_done, u + 1)
                xs = x[:, tt, s * WCOL:(s + 1) * WCOL]
                V.tensor_tensor(xs, xs, ps[:, u % 2, 0:WCOL], ALU.add).then_inc(proj_added, 1)
            dve.wait_ge(proj_added, 2 * RING)

            def routing(layer):
                def bc(ap, n):
                    return ap.unsqueeze(2).to_broadcast([P, TT, n])

                r0, r1, r2, r3, r4, r5 = (route[:, j] for j in range(6))
                v0, v1, v2, v3 = (small[:, j, :] for j in (7, 8, 9, 10))
                m1 = small[:, 11, :]
                gl, el = glog[:, :, 0:EG], glog[:, :, EG:]
                dve.wait_ge(logit_done, layer + 1)
                lk(V.tensor_tensor(glog[:], ps[:, 2, 0:TT * NR].rearrange("p (t n) -> p t n", t=TT),
                                   router_b[:, layer].unsqueeze(1).to_broadcast([P, TT, NR]), ALU.add))
                lk(V.tensor_reduce(v0.unsqueeze(2), gl, AX.X, ALU.max))
                V.tensor_tensor(r1[:, :, 0:EG], gl, bc(v0, EG), ALU.subtract).then_inc(glog_ready, 1)
                lk(V.tensor_tensor(r2[:, :, 0:EG], gl, bc(v0, EG), ALU.is_equal))
                lk(V.tensor_tensor(r3[:, :, 0:EG], r2[:, :, 0:EG], rev_g[:].unsqueeze(1).to_broadcast([P, TT, EG]), ALU.mult))
                lk(V.tensor_reduce(v1.unsqueeze(2), r3[:, :, 0:EG], AX.X, ALU.max))
                lk(V.tensor_tensor(r2[:, :, 0:EG], rev_g[:].unsqueeze(1).to_broadcast([P, TT, EG]), bc(v1, EG), ALU.is_equal))
                dve.wait_ge(gexp_done, layer + 1)
                lk(V.tensor_reduce(v1.unsqueeze(2), r0[:, :, 0:EG], AX.X, ALU.add))
                lk(V.reciprocal(v3, v1))
                lk(V.tensor_scalar(r3[:, :, 0:EG], r2[:, :, 0:EG], 1.0, -NEG, ALU.subtract, ALU.mult))
                for tt in range(TT):
                    hot = r2[:, tt, 0:EG].unsqueeze(2).to_broadcast([P, EG, EPG])
                    low = r3[:, tt, 0:EG].unsqueeze(2).to_broadcast([P, EG, EPG])
                    e4 = r4[:, tt, :].rearrange("p (g e) -> p g e", g=EG)
                    lk(V.tensor_tensor(e4, el[:, tt, :].rearrange("p (g e) -> p g e", g=EG), hot, ALU.mult))
                    lk(V.tensor_tensor(e4, e4, low, ALU.add))
                reve = rev_e[:].unsqueeze(1).to_broadcast([P, TT, E])

                def first_max(src, top, hot):
                    lk(V.tensor_reduce(top.unsqueeze(2), src, AX.X, ALU.max))
                    lk(V.tensor_tensor(r3, src, bc(top, E), ALU.is_equal))
                    lk(V.tensor_tensor(r1, r3, reve, ALU.mult))
                    lk(V.tensor_reduce(v0.unsqueeze(2), r1, AX.X, ALU.max))
                    lk(V.tensor_tensor(hot, reve, bc(v0, E), ALU.is_equal))

                first_max(r4, m1, r5)
                lk(V.scalar_tensor_tensor(out=r0, in0=r5, scalar=2.0 * NEG, in1=r4, op0=ALU.mult, op1=ALU.add))
                first_max(r0, v2, r2)
                V.tensor_tensor(v1, v2, m1, ALU.subtract).then_inc(e2_ready, 1)
                V.tensor_tensor(sel[:], r5, r2, ALU.add).then_inc(sel_ready, 1)
                dve.wait_ge(e2_done, layer + 1)
                lk(V.tensor_scalar(v0, v2, 1.0, None, ALU.add))
                lk(V.reciprocal(m1, v0))
                lk(V.tensor_tensor(v0, m1, v3, ALU.mult))
                lk(V.tensor_tensor(v1, v0, v2, ALU.mult))
                lk(V.tensor_tensor(r0, r5, bc(v0, E), ALU.mult))
                lk(V.tensor_tensor(r1, r2, bc(v1, E), ALU.mult))
                lk(V.tensor_tensor(gates[:], r0, r1, ALU.add))
                dve.wait_ge(rank_done, layer + 1)
                lk(V.tensor_scalar(r0, ps[:, 3, 0:TT * E].rearrange("p (t e) -> p t e", t=TT), 1.0, None, ALU.add))
                lk(V.tensor_tensor(r1, r0, sel[:], ALU.mult))
                lk(V.tensor_scalar(rank[:], r1, -1.0, None, ALU.add))
                lk(V.tensor_reduce(r0[:, 0, 0:1], ps[:, 3, TT * E:(TT + 1) * E], AX.X, ALU.max))
                V.tensor_copy(count_i[:, layer:layer + 1], r0[:, 0, 0:1]).then_inc(count_ready, 1)
                dve.wait_ge(count_ready, layer + 1)

            def moe_dve(S, n, it, w=None):
                CHAIN = 2
                c = Chain(dve, S.chain, CHAIN * n)
                c(V.tensor_copy(gq[:], gates[:, :, bass.ds(QUAD * it, QUAD)]))
                if w is not None:
                    dve.wait_ge(S.window, w + 1)
                for tt in range(TT):
                    rk = rank[:, tt, bass.ds(QUAD * it, QUAD)].unsqueeze(2).to_broadcast([P, QUAD, CAP])
                    V.tensor_tensor(pick[:, tt], slot_iota[:].unsqueeze(1).to_broadcast([P, QUAD, CAP]), rk,
                                    ALU.is_equal).then_inc(S.pick_ready, 1)
                dve.wait_ge(S.turn_done, n + 1)
                for h in range(2):
                    part = slice(CAP * h, CAP * (h + 1))
                    V.tensor_copy(gslot[part, :], ps[part, 4, 256:256 + 2 * QUAD].rearrange("p (r e) -> p r e", r=2)
                                  [:, :, :].rearrange("p r e -> p (r e)")[:, h:h + 7:6]).then_inc(S.gslot_ready, 1)
                for r in range(2):
                    dve.wait_ge(S.silu_done, 2 * n + r + 1)
                    V.tensor_tensor(hid[:, r, :], sg[:, r, :], ps[:, 2 + r, F:2 * F], ALU.mult).then_inc(S.hid_ready, 1)
                for r in range(2):
                    dve.wait_ge(S.yh_done, 2 * n + r + 1)
                    dve.wait_ge(S.gslot_ready, 2 * n + 2)
                    V.scalar_tensor_tensor(out=yl[:, r, :].rearrange("p (b n) -> p b n", b=2), in0=ps[:, 6:8, :],
                                           scalar=gslot[:, r:r + 1],
                                           in1=yh[:, r, :].bitcast(F32).rearrange("p (b n) -> p b n", b=2),
                                           op0=ALU.mult, op1=ALU.subtract).then_inc(S.yl_done, 1)
                for u in range(4):
                    tt, h = divmod(u, 2)
                    dve.wait_ge(S.comb_done, 4 * n + u + 1)
                    xs = x[:, tt, 512 * h:512 * (h + 1)]
                    V.tensor_tensor(xs, xs, ps[:, u % 2, :], ALU.add).then_inc(S.x_added, 1)
                c(V.tensor_copy(small[:, 7, :], small[:, 6, :]))
                dve.wait_ge(S.x_added, 4 * n + 4)
                assert c.n == CHAIN

            def layer_moe(layer):
                i = 2 * layer + 1
                norm(i)
                for tt in range(TT):
                    dve.wait_ge(xh_ready, 2 * layer + tt + 1)
                    V.tensor_tensor(xl[:, tt, :], xn[:, tt, :], xh[:, tt, :].bitcast(F32), ALU.subtract).then_inc(xl_ready, 1)
                routing(layer)
                with dve.Fori(0, NQ) as it:
                    moe_dve(main[layer], it, it)
                most = dve.value_load(count_i[0:1, layer:layer + 1], min_val=0, max_val=T)
                with dve.If(most > CAP):
                    with dve.Fori(0, WINDOWS - 1) as w:
                        V.tensor_scalar(rank[:], rank[:], float(CAP), None, ALU.subtract)\
                         .then_inc(more[layer].window, 1)
                        with dve.Fori(0, NQ) as it:
                            moe_dve(more[layer], w * NQ + it, it, w)
                dve.nop()

            layer_moe(0)

            norm(2)
            dec_s, c1s, s1s = par[:, 2, :], par[:, 3, :], par[:, 4, :]
            wc, ws, u1, u2, u3, u4 = (sc[:, j, :] for j in range(6))
            dve.wait_ge(tr_done, 12)
            lk(V.memset(cosT[:, :, 0:1], 1.0))
            lk(V.memset(sinT[:, :, 0:1], 0.0))
            lk(V.tensor_copy(wc, c1s))
            lk(V.tensor_copy(ws, s1s))
            m = 1
            while m <= CH:
                if m < CH:
                    n_el = ST * m
                    ta = tb[:, 0:2, :].rearrange("p a b -> p (a b)")[:, 0:n_el].rearrange("p (s m) -> p s m", m=m)
                    td = tb[:, 2:4, :].rearrange("p a b -> p (a b)")[:, 0:n_el].rearrange("p (s m) -> p s m", m=m)
                    wcb = wc.unsqueeze(2).to_broadcast([P, ST, m])
                    wsb = ws.unsqueeze(2).to_broadcast([P, ST, m])
                    c0, s0 = cosT[:, :, 0:m], sinT[:, :, 0:m]
                    lk(V.tensor_tensor(ta, c0, wcb, ALU.mult))
                    lk(V.tensor_tensor(td, s0, wsb, ALU.mult))
                    lk(V.tensor_tensor(cosT[:, :, m:2 * m], ta, td, ALU.subtract))
                    lk(V.tensor_tensor(ta, c0, wsb, ALU.mult))
                    lk(V.tensor_tensor(td, s0, wcb, ALU.mult))
                    lk(V.tensor_tensor(sinT[:, :, m:2 * m], ta, td, ALU.add))
                if m < CH:
                    lk(V.tensor_tensor(u1, wc, wc, ALU.mult))
                    lk(V.tensor_tensor(u2, ws, ws, ALU.mult))
                    lk(V.tensor_tensor(u3, wc, ws, ALU.mult))
                    lk(V.tensor_tensor(wc, u1, u2, ALU.subtract))
                    lk(V.tensor_scalar(ws, u3, 2.0, None, ALU.mult))
                m *= 2
            for q in range(4):
                dq = dec_s.rearrange("p (q i j) -> p q j i", q=4, i=2)[:, q]
                lk(V.tensor_copy(decayT[:, q], dq.unsqueeze(3).to_broadcast([P, 4, 2, CH])))
            lk(V.memset(decayT[:].rearrange("p q j i t -> p (q j i) t")[:, :, 0:1], 0.0))
            wre, wim = sc[:, 6, :], sc[:, 7, :]
            lk(V.tensor_tensor(wre, wc, dec_s, ALU.mult))
            lk(V.tensor_tensor(wim, ws, dec_s, ALU.mult))
            zre, zim, cre, cim = (sc[:, j, :] for j in (8, 9, 10, 11))

            def quarter(ap, q):
                return ap.rearrange("p (q i j) -> p q j i", q=4, i=2)[:, q]

            def loc(ap):
                return ap.rearrange("p (j i t) -> p j i t", j=4, i=2)

            for k in range(NCH):
                for q in range(4):
                    n = 4 * k + q
                    dve.wait_ge(bu_done, n + 1)
                    bu = ps[:, 0:4, 0:4 * CH].rearrange("p j (i r t) -> p j i r t", i=2, r=2)
                    co = cosT[:, 8 * q:8 * q + 8, :].rearrange("p (i j) t -> p j i t", i=2)
                    si = sinT[:, 8 * q:8 * q + 8, :].rearrange("p (i j) t -> p j i t", i=2)
                    dre, dim = db[:, 0, :], db[:, 1, :]
                    V.tensor_tensor(loc(tb[:, 0, :]), bu[:, :, :, 0, :], co, ALU.mult)
                    V.tensor_tensor(loc(tb[:, 2, :]), bu[:, :, :, 1, :], co, ALU.mult)
                    V.tensor_tensor(loc(tb[:, 3, :]), bu[:, :, :, 0, :], si, ALU.mult)
                    lk(V.tensor_tensor(loc(zb[:, 0, :]), bu[:, :, :, 1, :], si, ALU.mult))
                    V.tensor_tensor(dre, tb[:, 0, :], zb[:, 0, :], ALU.add).then_inc(bu_used, 1)
                    lk(V.tensor_tensor(dim, tb[:, 2, :], tb[:, 3, :], ALU.subtract))
                    dve.wait_ge(bu_used, n + 1)
                    if k:
                        h = loc(dre)[:, :, :, 0]
                        lk(V.tensor_tensor(h, h, quarter(cre, q), ALU.add))
                        h = loc(dim)[:, :, :, 0]
                        lk(V.tensor_tensor(h, h, quarter(cim, q), ALU.add))
                    dq = decayT[:, q].rearrange("p j i t -> p (j i t)")
                    V.tensor_tensor_scan(zb[:, 0, :], dq, dre, 0.0, ALU.mult, ALU.add)
                    lk(V.tensor_tensor_scan(zb[:, 1, :], dq, dim, 0.0, ALU.mult, ALU.add))
                    if n:
                        dve.wait_ge(q_used, n)
                    zr, zi = loc(zb[:, 0, :]), loc(zb[:, 1, :])
                    V.tensor_tensor(loc(qb[:, 0, :]), zr, co, ALU.mult)
                    V.tensor_tensor(loc(qb[:, 1, :]), zi, si, ALU.mult)
                    V.tensor_tensor(loc(qb[:, 2, :]), zi, co, ALU.mult)
                    V.tensor_tensor(loc(qb[:, 3, :]), zr, si, ALU.mult).then_inc(q_ready, 1)
                    V.tensor_copy(quarter(zre, q), zr[:, :, :, CH - 1])
                    lk(V.tensor_copy(quarter(zim, q), zi[:, :, :, CH - 1]))
                if k < NCH - 1:
                    lk(V.tensor_tensor(u1, wre, zre, ALU.mult))
                    lk(V.tensor_tensor(u2, wim, zim, ALU.mult))
                    lk(V.tensor_tensor(cre, u1, u2, ALU.subtract))
                    lk(V.tensor_tensor(u1, wre, zim, ALU.mult))
                    lk(V.tensor_tensor(u2, wim, zre, ALU.mult))
                    lk(V.tensor_tensor(cim, u1, u2, ALU.add))
                if k:
                    dve.wait_ge(gelu_done, k)
                lk(V.tensor_tensor(tb[:, 0, :].rearrange("p (i t) -> p i t", i=KT), xnT[:, :, k * CH:(k + 1) * CH],
                                   dskip[:].unsqueeze(2).to_broadcast([P, KT, CH]), ALU.mult))
                dve.wait_ge(y_done, k + 1)
                V.tensor_tensor(tb[:, 1, :], tb[:, 0, :], ps[:, 4 + k % 2, :], ALU.add).then_inc(gelu_in, 1)
                dve.wait_ge(gelu_in, k + 1)

            for u in range(2 * RING):
                s, tt = divmod(u, 2)
                dve.wait_ge(sig_done, u + 1)
                xs = x[:, tt, s * WCOL:(s + 1) * WCOL]
                lk(V.tensor_tensor(sig[:, u % 2, :], sig[:, u % 2, :], ps[:, u % 2, 0:WCOL], ALU.mult))
                V.tensor_tensor(xs, xs, sig[:, u % 2, :], ALU.add).then_inc(glu_added, 1)
            dve.wait_ge(glu_added, 2 * RING)
            layer_moe(1)
            norm(4)

        @block.tensor
        def _(pe):
            mm = nc.tensor.matmul

            def turn(i):
                pe.wait_ge(xn_ready, 2 * i + 2)
                for g in range(4):
                    if g >= 2:
                        pe.wait_ge(tr_evac, 4 * i + g - 1)
                    for k in range(2):
                        for tt in range(TT):
                            kt = 2 * g + k
                            ins = nc.tensor.transpose(ps[:, g % 2, (2 * k + tt) * P:(2 * k + tt + 1) * P],
                                                      xn[:, tt, kt * P:(kt + 1) * P], ident[:])
                    ins.then_inc(tr_done, 1)
                pe.wait_ge(tr_evac, 4 * i + 4)

            pe.wait_ge(const_ready, 8)
            turn(0)

            def qkv(u0, u1):
                for u in range(u0, u1):
                    if u >= 3:
                        pe.wait_ge(qkv_evac, u - 2)
                    if u < 16:
                        s, c = divmod(u, 6)
                        pe.wait_ge(slot_full[s], 16)
                        w = ring[:, s, :].rearrange("p (k n) -> p k n", k=KT)
                        for kt in range(KT):
                            ins = mm(ps[:, u % 3, 0:T], w[:, kt, c * P:(c + 1) * P], xnT[:, kt, :],
                                     start=(kt == 0), stop=(kt == KT - 1))
                    else:
                        c, tt = divmod(u - 16, 2)
                        s, col = divmod(2 * D + c * VCOL, QCOL)
                        pe.wait_ge(slot_full[s], 16)
                        w = ring[:, s, :].rearrange("p (k n) -> p k n", k=KT)
                        for kt in range(KT):
                            ins = mm(ps[:, u % 3, 0:VCOL], xnT[:, kt, tt * P:(tt + 1) * P], w[:, kt, col:col + VCOL],
                                     start=(kt == 0), stop=(kt == KT - 1))
                    ins.then_inc(qkv_done, 1)
                    if u % 6 == 5:
                        pe.wait_ge(qkv_done, u + 1)
                        pe.sem_inc(slot_free[u // 6], 1)

            qkv(0, 6)
            pe.wait_ge(craw_loaded, 64)
            for r in range(2):
                for i in range(KT):
                    ins = nc.tensor.transpose(ps[:, 4 + 2 * r + i // 4, (i % 4) * P:(i % 4 + 1) * P],
                                              c_raw[:, r, i].rearrange("p u n -> p (u n)"), ident[:])
            ins.then_inc(c_turned, 1)
            qkv(6, 12)
            pe.wait_ge(par_ready, 1)
            for j, src in enumerate((18, 19, 2, 9, 8)):
                ins = nc.tensor.transpose(ps[:, 3, j * ST:(j + 1) * ST], disc[:, src, :],
                                          ident[0:ST, 0:ST])
            ins.then_inc(par_turned, 1)
            qkv(12, 14)
            pe.wait_ge(b_ready, 1)
            for r in range(2):
                for i in range(KT):
                    ins = nc.tensor.transpose(ps[:, 4 + 2 * r + i // 4, (i % 4) * P:(i % 4 + 1) * P],
                                              b_blk[:, r, 4 * i:4 * i + 4].rearrange("p s c -> p (s c)"), ident[:])
            ins.then_inc(b_turned, 1)
            qkv(14, 24)

            pe.wait_ge(qkv_evac, 24)
            pe.wait_ge(prep_done, 1)

            def scores(hp):
                if hp >= 2:
                    pe.wait_ge(nmax_ready, hp - 1)
                for h in range(2):
                    rows = slice(HD * h, HD * (h + 1))
                    q, kk = qkT[rows, hp, :], qkT[rows, HP + hp, :]
                    b = 2 * (hp % 2) + h
                    mm(ps[:, b, 0:P], q[:, 0:P], kk[:, 0:P], start=True, stop=True)
                    ins = mm(ps[:, b, P:3 * P], q[:, P:T], kk[:, 0:T], start=True, stop=True)
                ins.then_inc(s_done, 1)

            def attend(hp):
                pe.wait_ge(p_ready, 2 * hp + 2)
                if hp:
                    pe.wait_ge(pt_evac_a, hp)
                for h in range(2):
                    for j in range(3):
                        ins = nc.tensor.transpose(ps[:, 4 + h, j * P:(j + 1) * P],
                                                  s_sb[:, hp % 2, h, j * P:(j + 1) * P], ident[:])
                ins.then_inc(pt_done, 1)
                pe.wait_ge(pt_evac_a, hp + 1)
                if hp >= 2:
                    pe.wait_ge(o_evac, hp - 1)
                for h in range(2):
                    rows = slice(HD * h, HD * (h + 1))
                    cols = slice(HD * (2 * hp + h), HD * (2 * hp + h + 1))
                    b = 6 + hp % 2
                    mm(ps[rows, b, 0:P], v[:, 0, cols], pT[:, h, 0:P], start=True, stop=True)
                    mm(ps[rows, b, P:T], v[:, 0, cols], pT[:, h, P:2 * P], start=True, stop=False)
                    ins = mm(ps[rows, b, P:T], v[:, 1, cols], pT[:, h, 2 * P:3 * P], start=False, stop=True)
                ins.then_inc(o_done, 1)

            scores(0)
            for hp in range(HP):
                if hp + 1 < HP:
                    scores(hp + 1)
                attend(hp)

            pe.wait_ge(o_evac, HP)
            for u in range(2 * RING):
                s, tt = divmod(u, 2)
                pe.wait_ge(slot_full[s], 32)
                if u >= 2:
                    pe.wait_ge(proj_added, u - 1)
                w = ring[:, s, 0:KT * WCOL].rearrange("p (k n) -> p k n", k=KT)
                for kt in range(KT):
                    ins = mm(ps[:, u % 2, 0:WCOL], oT[:, kt, tt * P:(tt + 1) * P], w[:, kt, :],
                             start=(kt == 0), stop=(kt == KT - 1))
                ins.then_inc(proj_done, 1)
                if tt == 1:
                    pe.wait_ge(proj_done, u + 1)
                    pe.sem_inc(slot_free[s], 1)

            def router(layer):
                pe.wait_ge(small_loaded, 16 * 18)
                for tt in range(TT):
                    for kt in range(KT):
                        ins = mm(ps[:, 2, tt * NR:(tt + 1) * NR], xnT[:, kt, tt * P:(tt + 1) * P],
                                 router_w[:, layer, kt, :], start=(kt == 0), stop=(kt == KT - 1))
                ins.then_inc(logit_done, 1)
                pe.wait_ge(sel_ready, layer + 1)
                mm(ps[:, 3, 0:E], before[:], sel[:, 0, :], start=True, stop=True)
                mm(ps[:, 3, E:2 * E], before[:], sel[:, 1, :], start=True, stop=False)
                mm(ps[:, 3, E:2 * E], ones[:], sel[:, 0, :], start=False, stop=True)
                mm(ps[:, 3, 2 * E:3 * E], ones[:], sel[:, 0, :], start=True, stop=False)
                mm(ps[:, 3, 2 * E:3 * E], ones[:], sel[:, 1, :], start=False, stop=True).then_inc(rank_done, 1)

            def moe_pe(S, n, full, start):
                pe.wait_ge(S.pick_ready, 2 * n + 2)
                xs = [t[:].rearrange("p t (q c) -> p t q c", c=KT) for t in (xh, xl)]
                for u in range(4):
                    if u >= 2:
                        pe.wait_ge(S.xg_evac, 4 * n + u - 1)
                    for c in range(2):
                        for i in range(2 * TT):
                            part, tt = divmod(i, TT)
                            ins = mm(ps[:, u % 2, c * QS:(c + 1) * QS], xs[part][:, tt, :, 2 * u + c],
                                     pick[:, tt].rearrange("p e s -> p (e s)"), start=(i == 0), stop=(i == 2 * TT - 1))
                    ins.then_inc(S.gath_done, 1)
                for r in range(2):
                    for tt in range(TT):
                        nc.tensor.transpose(ps[:, 5, (2 * r + tt) * P:(2 * r + tt + 1) * P],
                                            pick[:, tt, 2 * r:2 * r + 2].rearrange("p e s -> p (e s)").bitcast(F32), ident[:])
                for r in range(2):
                    for tt in range(TT):
                        ins = mm(ps[:, 4, 256 + QUAD * r:256 + QUAD * (r + 1)],
                                 pick[:, tt, 2 * r:2 * r + 2].rearrange("p e s -> p (e s)").bitcast(F32), gq[:, tt, :],
                                 start=(tt == 0), stop=(tt == TT - 1))
                ins.then_inc(S.turn_done, 1)
                pe.wait_ge(S.xg_evac, 4 * n + 4)
                pe.wait_ge(S.gslot_ready, 2 * n + 2)
                for r in range(2):
                    for h in range(2):
                        pe.wait_ge(full[2 * r + h], start + 48 * (n + 1))
                    for c in range(KT):
                        for h in range(2):
                            s = 2 * r + h
                            w = ring[:, s, 0:2 * KT * F].rearrange("p (u c f) -> p u c f", u=2, c=KT)[:, :, c, :]
                            ins = mm(ps[CAP * h:CAP * (h + 1), 2 + r, :], xg[:, c, CAP * s:CAP * (s + 1)], w,
                                     start=(c == 0), stop=(c == KT - 1))
                    ins.then_inc(S.gu_done, 1)
                for r in range(2):
                    pe.wait_ge(S.hid_ready, 2 * n + r + 1)
                    for j in range(FT):
                        ins = nc.tensor.transpose(ps[:, 4, j * P:(j + 1) * P], hid[:, r, j:F:FT], ident[:])
                    ins.then_inc(S.hT_done, 1)
                    pe.wait_ge(S.hT_evac, 2 * n + r + 1)
                    if r:
                        pe.wait_ge(S.yl_done, 2 * n + 1)
                    for j in range(FT):
                        for b in range(2):
                            for h in range(2):
                                s = 2 * r + h
                                w = ring[:, s, 2 * KT * F:].rearrange("p (j d) -> p j d", j=FT)[:, j, 512 * b:512 * (b + 1)]
                                ins = mm(ps[CAP * h:CAP * (h + 1), 6 + b, :], hidT[:, r, j, CAP * h:CAP * (h + 1)], w,
                                         start=(j == 0), stop=(j == FT - 1))
                    ins.then_inc(S.down_done, 1)
                pe.wait_ge(S.yl_done, 2 * n + 2)
                pe.wait_ge(S.pt_evac, n + 1)
                for u in range(4):
                    tt, b = divmod(u, 2)
                    if u >= 2:
                        pe.wait_ge(S.x_added, 4 * n + u - 1)
                    for i in range(4):
                        r, y = i // 2, (yh, yl)[i % 2]
                        ins = mm(ps[:, u % 2, :], pickT[:, r, tt * P:(tt + 1) * P], y[:, r, 512 * b:512 * (b + 1)],
                                 start=(i == 0), stop=(i == 3))
                    ins.then_inc(S.comb_done, 1)

            def layer_moe(layer):
                turn(2 * layer + 1)
                router(layer)
                pe.wait_ge(xl_ready, 2 * layer + 2)
                with pe.Fori(0, NQ) as it:
                    moe_pe(main[layer], it, slot_full, full_before(layer))
                pe.wait_ge(count_ready, layer + 1)
                most = pe.value_load(count_i[0:1, layer:layer + 1], min_val=0, max_val=T)
                with pe.If(most > CAP):
                    pe.sem_inc(more[layer].ring_passed, 1)
                    with pe.Fori(0, WINDOWS - 1) as w:
                        with pe.Fori(0, NQ) as it:
                            n = w * NQ + it
                            moe_pe(more[layer], n, more[layer].full, 0)
                            pe.wait_ge(more[layer].down_done, 2 * n + 2)
                            pe.sem_inc(more[layer].ring_passed, 1)
                pe.nop()

            layer_moe(0)

            turn(2)

            def inputs(n):
                k, q = divmod(n, 4)
                if n:
                    pe.wait_ge(bu_used, n)
                for i in range(2):
                    for r in range(2):
                        for j in range(4):
                            rows = slice(32 * j, 32 * (j + 1))
                            o = (2 * i + r) * CH
                            ins = mm(ps[:, j, o:o + CH], bT[rows, r, 2 * q + i, :], xnT[rows, 2 * q + i, k * CH:(k + 1) * CH],
                                     start=True, stop=True, tile_position=(32 * j, 0))
                ins.then_inc(bu_done, 1)

            inputs(0)
            for n in range(4 * NCH):
                k, q = divmod(n, 4)
                if n + 1 < 4 * NCH:
                    inputs(n + 1)
                pe.wait_ge(q_ready, n + 1)
                if q == 0 and k >= 2:
                    pe.wait_ge(gelu_in, k - 1)
                for i in range(2):
                    for m, c in enumerate((0, 1, 2, 2)):
                        for j in range(4):
                            rows = slice(32 * j, 32 * (j + 1))
                            ins = mm(ps[rows, 4 + k % 2, (2 * q + i) * CH:(2 * q + i + 1) * CH],
                                     cT[:, c, 8 * q + 4 * i + j, :],
                                     qb[:, m, :].rearrange("p (j i t) -> p j i t", j=4, i=2)[:, j, i, :],
                                     start=(m == 0), stop=(m == 3), tile_position=(0, 32 * j))
                ins.then_inc(q_used, 1)
                if q == 3:
                    pe.wait_ge(q_used, n + 1)
                    pe.sem_inc(y_done, 1)

            pe.wait_ge(gelu_done, NCH)
            for u in range(2 * RING):
                s, tt = divmod(u, 2)
                pe.wait_ge(slot_full[s], full_before(1))
                if u >= 2:
                    pe.wait_ge(glu_added, u - 1)
                w = ring[:, s, 0:KT * 2 * WCOL].rearrange("p (k n) -> p k n", k=KT)
                for kt in range(KT):
                    ins = mm(ps[:, u % 2, :], yT[:, kt, tt * P:(tt + 1) * P], w[:, kt, :],
                             start=(kt == 0), stop=(kt == KT - 1))
                ins.then_inc(glu_done, 1)
                if tt == 1:
                    pe.wait_ge(glu_done, u + 1)
                    pe.sem_inc(slot_free[s], 1)
            layer_moe(1)


_INS = ["x", "norm_mix", "norm_ffn", "norm_final", "attn_w_qkv", "attn_w_o", "attn_rel_bias", "ssm_lambda_re",
        "ssm_lambda_im", "ssm_log_step", "ssm_b_re", "ssm_b_im", "ssm_c_re", "ssm_c_im", "ssm_d", "ssm_w_out",
        "moe_w_group_router", "moe_b_group_router", "moe_w_expert_router", "moe_b_expert_router", "moe_w_gate",
        "moe_w_up", "moe_w_down"]


def kernel(**inputs):
    import concourse.bacc as bacc
    from concourse.bass_utils import run_bass_kernel_spmd

    nc = bacc.Bacc("TRN2", target_bir_lowering=False, num_devices=1)
    arrays, aps = {}, {}
    for name in _INS:
        arr = np.ascontiguousarray(inputs[name])
        arrays[f"in_{name}"] = arr
        aps[name] = nc.dram_tensor(f"in_{name}", arr.shape, mybir.dt.from_np(arr.dtype), kind="ExternalInput").ap()
    out = nc.dram_tensor("out_0", (1, T, D), F32, kind="ExternalOutput").ap()
    trunk_program(nc, aps, out)
    r = run_bass_kernel_spmd(nc, [arrays], core_ids=[0])
    return r.results[0]["out_0"]
```

```python
from contextlib import ExitStack

import numpy as np

import concourse.bass as bass
from concourse import mybir

F32 = mybir.dt.float32
F32R = mybir.dt.float32r
I32 = mybir.dt.int32
ALU = mybir.AluOpType
ACT = mybir.ActivationFunctionType
AX = mybir.AxisListType

P = 128
D = 1024
T = 256
TT = T // P
KT = D // P
H, HD = 16, 64
HP = H // 2
CH = 64
MAXREL = 128
NREL = 2 * MAXREL + 1
G, GC, NS = 64, 16, 64
ST = G * NS // P
NCH = T // CH
EG, EPG = 4, 8
E = EG * EPG
F = D // 4
FT = F // P
CAP = 64
WINDOWS = T // CAP
QUAD = 4
QS = QUAD * CAP
NQ = E // QUAD
NR = EG + E
EPS = 1e-6
NEG = -1e30
RING = 4
SLOT = 3 * D * F // P
REV = 2 * T - 1 - P
WCOL = D // RING
HPS = WCOL // P
UNITS = 6
GU = 2 * D * F // P
BREAKS = (3, 6)


def trunk_program(nc, a, out):
    ctx = ExitStack()
    with ctx:
        base = (nc.sbuf_base + 63) // 64 * 64
        where = [base]

        def fixed(name, shape, dt=F32):
            n = int(np.prod(shape[1:])) * 4
            t = nc.alloc_sbuf_tensor_at(name, shape, dt, offset=where[0])
            where[0] += (n + 63) // 64 * 64
            return t

        def sem(name):
            return ctx.enter_context(nc.semaphore(name))

        ring = fixed("ring", [P, RING, SLOT])
        x = fixed("x", [P, TT, D])
        normw = fixed("normw", [P, D])
        xnT_at = where[0]
        xnT = fixed("xnT", [P, KT, T])
        bT = fixed("bT", [P, 2, KT, P])
        cT = fixed("cT", [P, 3, ST, 2 * GC])
        par = fixed("par", [P, 5, ST])
        router_w = fixed("router_w", [P, 2, KT, NR])
        router_b = fixed("router_b", [P, 2, NR])
        ident = fixed("ident", [P, P])
        before = fixed("before", [P, P])
        ones = fixed("ones", [P, P])
        slot_iota = fixed("slot_iota", [P, CAP])
        rev_e = fixed("rev_e", [P, E])
        rev_g = fixed("rev_g", [P, EG])
        small = fixed("small", [P, 12, TT])
        lam = fixed("lam", [ST, 2, P])
        logstep = fixed("logstep", [ST, 2])
        dskip = fixed("dskip", [P, KT])
        rank = fixed("rank", [P, TT, E])
        gates = fixed("gates", [P, TT, E])
        route = fixed("route", [P, 6, TT, E])
        glog = fixed("glog", [P, TT, NR])
        sel = fixed("sel", [P, TT, E])
        count_i = fixed("count_i", [P, 2], I32)
        sc = fixed("sc", [P, 14, ST])
        arena = where[0]

        def at(name, shape, off, dt=F32):
            return nc.alloc_sbuf_tensor_at(name, shape, dt, offset=arena + 4 * off)

        qk = at("qk", [P, 2, 4, T], 0)
        v = at("v", [P, 2, TT, WCOL], 2048)
        oT = at("oT", [P, KT, T], 3072)
        bias = at("bias", [P, H, 3 * P], 5120)
        s_sb = at("s_sb", [P, 2, 2, 3 * P], 11264)
        pT = at("pT", [P, 2, 3 * P], 12800)
        stat = at("stat", [P, 3, 2, 2, 2], 13568)
        rb_row = at("rb_row", [H, NREL], 13632)
        rb_rev = at("rb_rev", [H, REV], 13952)
        xn = at("xn", [P, TT, D], 0)
        xg = at("xg", [P, KT, QS], 0)
        xh = at("xh", [P, TT, D], 2048, F32R)
        xl = at("xl", [P, TT, D], 4096, F32R)
        yh = at("yh", [P, 2, D], 6144, F32R)
        yl = nc.alloc_sbuf_tensor_at("yl", [P, 2, D], F32R, offset=xnT_at)
        pick = at("pick", [P, TT, QUAD, CAP], 10240, F32R)
        pickT = at("pickT", [P, 2, T], 10752, F32R)
        sg = at("sg", [P, 2, F], 11264)
        hid = at("hid", [P, 2, F], 11776)
        hidT = at("hidT", [P, 2, FT, P], 12288)
        gq = at("gq", [P, TT, QUAD], 12800)
        gslot = at("gslot", [P, 2], 12816)
        disc = at("disc", [ST, 16, P], 0)
        b_blk = at("b_blk", [P, 2, ST, 2 * GC], 6144)
        c_raw = at("c_raw", [P, 2, KT, 2, NS], 8192)
        b_raw = at("b_raw", [P, 2, ST, GC], 12832)
        b_tmp = at("b_tmp", [P, 2, ST, GC], 12832 + 1024)
        t_tmp = at("t_tmp", [P, 2, ST * CH // 2], 6144)
        cosT = at("cosT", [P, ST, CH], 8192)
        sinT = at("sinT", [P, ST, CH], 12832)
        yT = at("yT", [P, KT, T], 0)
        decayT = at("decayT", [P, 4, 4, 2, CH], 2048)
        tb = at("tb", [P, 4, 512], 4096)
        qb = at("qb", [P, 4, 512], 6144)
        zb = at("zb", [P, 2, 2, 512], 10240)
        sig = at("sig", [P, 2, WCOL], 14880)
        yb = at("yb", [P, 512], 12288)
        assert arena + 4 * 15392 <= nc.sbuf_usable_end, (arena, nc.sbuf_usable_end)

        ps = ctx.enter_context(nc.psum_tensor("ps", [P, 8, 512], F32))
        rev_dram = nc.dram_tensor("rev_bias", (H, REV), F32).ap()

        x_loaded, small_loaded = sem("x_loaded"), sem("small_loaded")
        braw_loaded, craw_loaded = sem("braw_loaded"), sem("craw_loaded")
        rb_loaded, rev_ready, rev_stored, bias_loaded = (sem(n) for n in ("rb_loaded", "rev_ready", "rev_stored", "bias_loaded"))
        normw_loaded = sem("normw_loaded")
        const_ready, pool_chain = sem("const_ready"), sem("pool_chain")
        dve_chain = sem("dve_chain")
        slot_full = [sem(f"slot_full{s}") for s in range(RING)]
        down_full = [sem(f"down_full{s}") for s in range(RING)]
        slot_free = [sem(f"slot_free{s}") for s in range(RING)]
        ms_ready, rms_ready, xn_ready = sem("ms_ready"), sem("rms_ready"), sem("xn_ready")
        xh_ready, xl_ready = sem("xh_ready"), sem("xl_ready")
        tr_done, tr_evac = sem("tr_done"), sem("tr_evac")
        qkv_done, qkv_evac = sem("qkv_done"), sem("qkv_evac")
        step_ready, step_exp, ang_ready, ang_sin = (sem(n) for n in ("step_ready", "step_exp", "ang_ready", "ang_sin"))
        par_ready, par_turned, c_turned, b_ready, b_turned, prep_done = (
            sem(n) for n in ("par_ready", "par_turned", "c_turned", "b_ready", "b_turned", "prep_done"))
        s_done, nmax_ready, exp_done, p_ready, pt_done, pt_evac_a = (
            sem(n) for n in ("s_done", "nmax_ready", "exp_done", "p_ready", "pt_done", "pt_evac_a"))
        o_done, o_evac = sem("o_done"), sem("o_evac")
        proj_done, proj_added = sem("proj_done"), sem("proj_added")
        logit_done, sel_ready, rank_done = (sem(n) for n in ("logit_done", "sel_ready", "rank_done"))
        glog_ready, gexp_done, e2_ready, e2_done = (sem(n) for n in ("glog_ready", "gexp_done", "e2_ready", "e2_done"))
        count_ready = sem("count_ready")
        bu_done, bu_used, q_ready, q_used, y_done, y_used, gelu_in, gelu_done = (
            sem(n) for n in ("bu_done", "bu_used", "q_ready", "q_used", "y_done", "y_used", "gelu_in", "gelu_done"))
        glu_done, sig_done, glu_added = sem("glu_done"), sem("sig_done"), sem("glu_added")
        out_stored = sem("out_stored")
        raw_ready, z_ready, tables_ready = sem("raw_ready"), sem("z_ready"), sem("tables_ready")

        class MoeSems:

            def __init__(self, tag):
                self.pick_ready = sem(f"pick_ready_{tag}")
                self.gath_done = sem(f"gath_done_{tag}")
                self.xg_evac = sem(f"xg_evac_{tag}")
                self.turn_done = sem(f"turn_done_{tag}")
                self.pt_evac = sem(f"pt_evac_{tag}")
                self.gslot_ready = sem(f"gslot_ready_{tag}")
                self.gu_done = sem(f"gu_done_{tag}")
                self.silu_done = sem(f"silu_done_{tag}")
                self.hid_ready = sem(f"hid_ready_{tag}")
                self.hT_done = sem(f"hT_done_{tag}")
                self.hT_evac = sem(f"hT_evac_{tag}")
                self.down_done = sem(f"down_done_{tag}")
                self.yh_done = sem(f"yh_done_{tag}")
                self.yl_done = sem(f"yl_done_{tag}")
                self.comb_done = sem(f"comb_done_{tag}")
                self.x_added = sem(f"x_added_{tag}")
                self.chain = sem(f"chain_{tag}")
                self.full = None
                self.dfull = None

        main = [MoeSems(f"l{i}") for i in range(2)]
        more = [MoeSems(f"more{i}") for i in range(2)]
        for i in range(2):
            more[i].window = sem(f"window_{i}")
            more[i].ring_passed = sem(f"ring_passed_{i}")
            more[i].full = more[i].dfull = [sem(f"more_full{i}")] * RING
            main[i].full, main[i].dfull = slot_full, down_full

        def full_before(layer):
            return 48 + 16 + layer * (NQ * 32 + 32)

        block = ctx.enter_context(nc.Block())

        class Chain:

            def __init__(self, eng, s, start=0):
                self.eng, self.s, self.start, self.n = eng, s, start, 0

            def __call__(self, ins):
                self.n += 1
                ins.then_inc(self.s, 1)
                self.eng.wait_ge(self.s, self.start + self.n)

        @block.sync
        def _(sp):
            sp.dma_start(x[:], a["x"][0].rearrange("(t p) d -> p t d", p=P)).then_inc(x_loaded, 16)
            wqkv = a["attn_w_qkv"][0].rearrange("(k p) n -> p k n", p=P)
            wo = a["attn_w_o"][0].rearrange("(k p) n -> p k n", p=P)
            wout = a["ssm_w_out"][0].rearrange("(k p) n -> p k n", p=P)
            for s in range(RING):
                for i in range(3):
                    sp.dma_start(ring[:, s, :].rearrange("p (i k n) -> p i k n", i=3, k=KT)[:, i],
                                 wqkv[:, :, i * D + s * WCOL:i * D + (s + 1) * WCOL]).then_inc(slot_full[s], 16)

            n_mat = D * F // P
            wg = a["moe_w_gate"].rearrange("l e (p c) f -> p (l e) (c f)", p=P)
            wu = a["moe_w_up"].rearrange("l e (p c) f -> p (l e) (c f)", p=P)
            wd = a["moe_w_down"].rearrange("l e (p j) d -> p (l e) (j d)", p=P)

            def gate_up(layer, e, s, full):
                for i, w in enumerate((wg, wu)):
                    src = w[:, bass.ds(E * layer + e, 1), :].rearrange("p o n -> p (o n)")
                    sp.dma_start(ring[:, s, i * n_mat:(i + 1) * n_mat], src).then_inc(full[s], 16)

            def down(layer, e, s, full):
                src = wd[:, bass.ds(E * layer + e, 1), :].rearrange("p o n -> p (o n)")
                sp.dma_start(ring[:, s, GU:SLOT], src).then_inc(full[s], 16)

            def experts(layer):
                S = main[layer]
                for s in range(QUAD):
                    sp.wait_ge(slot_free[s], 2 + layer)
                    gate_up(layer, s, s, slot_full)
                with sp.Fori(1, NQ) as it:
                    for s in range(QUAD):
                        sp.wait_ge(S.gu_done, 2 * it - 1 + s // 2)
                        gate_up(layer, QUAD * it + s, s, slot_full)
                    for s in range(QUAD):
                        sp.wait_ge(S.down_done, 2 * it - 1 + s // 2)
                        down(layer, QUAD * it + s, s, down_full)
                sp.wait_ge(count_ready, layer + 1)
                most = sp.value_load(count_i[0:1, layer:layer + 1], min_val=0, max_val=T)
                R = more[layer]
                with sp.If(most > CAP):
                    sp.wait_ge(S.down_done, 2 * NQ)
                    with sp.Fori(0, WINDOWS - 1) as w:
                        with sp.Fori(0, NQ) as it:
                            sp.wait_ge(R.ring_passed, NQ * w + it + 1)
                            for s in range(QUAD):
                                gate_up(layer, QUAD * it + s, s, R.full)
                                down(layer, QUAD * it + s, s, R.dfull)
                    sp.wait_ge(R.down_done, 2 * NQ * (WINDOWS - 1))
                sp.nop()

            for s in range(RING):
                sp.wait_ge(slot_free[s], 1)
                sp.dma_start(ring[:, s, 0:KT * WCOL].rearrange("p (k n) -> p k n", k=KT),
                             wo[:, :, s * WCOL:(s + 1) * WCOL]).then_inc(slot_full[s], 16)
                down(0, s, s, down_full)
            experts(0)
            for s in range(RING):
                sp.wait_ge(main[0].gu_done, 2 * NQ - 1 + s // 2)
                dst = ring[:, s, 0:KT * 2 * WCOL].rearrange("p (k h n) -> p k h n", k=KT, h=2)
                for h in range(2):
                    sp.dma_start(dst[:, :, h, :], wout[:, :, h * D + s * WCOL:h * D + (s + 1) * WCOL])\
                      .then_inc(slot_full[s], 16)
            for s in range(RING):
                sp.wait_ge(main[0].down_done, 2 * NQ - 1 + s // 2)
                down(1, s, s, down_full)
            experts(1)
            for tt in range(TT):
                sp.wait_ge(xn_ready, 2 * 4 + tt + 1)
                sp.dma_start(out[0, tt * P:(tt + 1) * P, :], xn[:, tt, :]).then_inc(out_stored, 16)
            sp.wait_ge(out_stored, 16 * TT)

        @block.gpsimd
        def _(pool):
            pc = Chain(pool, pool_chain)
            norms = [a["norm_mix"][0], a["norm_ffn"][0], a["norm_mix"][1], a["norm_ffn"][1], a["norm_final"]]

            def load_normw(i):
                if i:
                    pool.wait_ge(xn_ready, 2 * i)
                pool.dma_start(normw[:], norms[i].rearrange("(o d) -> o d", o=1).to_broadcast([P, D]))\
                    .then_inc(normw_loaded, 16)

            load_normw(0)
            nc.gpsimd.memset(ones[:], 1.0).then_inc(const_ready, 1)
            pc(nc.gpsimd.memset(ident[:], 0.0))
            pc(nc.gpsimd.memset(before[:], 1.0))
            nc.gpsimd.affine_select(out=ident[:], in_=ident[:], compare_op=ALU.not_equal, fill=1.0, base=0,
                                    pattern=[[-1, P]], channel_multiplier=1).then_inc(const_ready, 1)
            nc.gpsimd.affine_select(out=before[:], in_=before[:], compare_op=ALU.is_gt, fill=0.0, base=0,
                                    pattern=[[1, P]], channel_multiplier=-1).then_inc(const_ready, 1)
            nc.gpsimd.iota(slot_iota[:], pattern=[[1, CAP]], base=0, channel_multiplier=0,
                           allow_small_or_imprecise_dtypes=True).then_inc(const_ready, 1)
            nc.gpsimd.iota(rev_e[:], pattern=[[-1, E]], base=E, channel_multiplier=0,
                           allow_small_or_imprecise_dtypes=True).then_inc(const_ready, 1)
            nc.gpsimd.iota(rev_g[:], pattern=[[-1, EG]], base=EG, channel_multiplier=0,
                           allow_small_or_imprecise_dtypes=True).then_inc(const_ready, 1)
            nc.gpsimd.memset(cT[:], 0.0).then_inc(const_ready, 1)
            pool.wait_ge(rev_ready, 1)
            pool.dma_start(rev_dram, rb_rev[:]).then_inc(rev_stored, 16)
            pool.wait_ge(rev_stored, 16)
            ap = rev_dram
            lo = bass.AP(tensor=ap.tensor, offset=T - P, ap=[[1, P], [REV, H], [1, P]])
            hi = bass.AP(tensor=ap.tensor, offset=0, ap=[[1, P], [REV, H], [1, 2 * P]])
            pool.dma_start(bias[:, :, 0:P], lo).then_inc(bias_loaded, 16)
            pool.dma_start(bias[:, :, P:3 * P], hi).then_inc(bias_loaded, 16)
            load_normw(1)
            pool.wait_ge(xn_ready, 2 + 2)
            for r, name in enumerate(("ssm_c_re", "ssm_c_im")):
                for dup in range(2):
                    pool.dma_start(c_raw[:, r, :, dup, :], a[name][0].rearrange("(i g) c p -> (g c) i p", g=P // GC))\
                        .then_inc(craw_loaded, 16)
            for r, name in enumerate(("ssm_b_re", "ssm_b_im")):
                for g2 in range(2):
                    src = a[name][0].rearrange("(s g) p c -> g p s c", g=2)[g2]
                    pool.dma_start(b_raw[NS * g2:NS * (g2 + 1), r], src).then_inc(braw_loaded, 16)
            load_normw(2)
            pool.wait_ge(tables_ready, 1)
            for n in range(4 * NCH):
                q = n % 4
                pool.wait_ge(z_ready, n + 1)
                if n:
                    pool.wait_ge(q_used, n)
                co = cosT[:, 8 * q:8 * q + 8, :].rearrange("p (i j) t -> p j i t", i=2)
                si = sinT[:, 8 * q:8 * q + 8, :].rearrange("p (i j) t -> p j i t", i=2)
                zr, zi = (zb[:, n % 2, r, :].rearrange("p (j i t) -> p j i t", j=4, i=2) for r in range(2))
                for m, (z, w) in enumerate(((zr, co), (zi, si), (zi, co), (zr, si))):
                    nc.gpsimd.tensor_tensor(qb[:, m, :].rearrange("p (j i t) -> p j i t", j=4, i=2), z, w, ALU.mult)\
                        .then_inc(q_ready, 1)
            for i in range(3, 5):
                load_normw(i)

        @block.scalar
        def _(act):
            n = 0
            lre = a["ssm_lambda_re"][0].rearrange("(s g) p -> s (g p)", g=2)
            lim = a["ssm_lambda_im"][0].rearrange("(s g) p -> s (g p)", g=2)
            act.dma_start(lam[:, 0, :], lre).then_inc(small_loaded, 16)
            act.dma_start(lam[:, 1, :], lim).then_inc(small_loaded, 16)
            act.dma_start(logstep[:], a["ssm_log_step"][0].rearrange("(s g) -> s g", g=2)).then_inc(small_loaded, 16)
            act.dma_start(rb_row[:], a["attn_rel_bias"][0]).then_inc(rb_loaded, 16)
            for layer in range(2):
                wr = router_w[:, layer]
                act.dma_start(wr[:, :, 0:EG], a["moe_w_group_router"][layer].rearrange("(k p) g -> p k g", p=P))\
                   .then_inc(small_loaded, 16)
                for g in range(EG):
                    act.dma_start(wr[:, :, EG + g * EPG:EG + (g + 1) * EPG],
                                  a["moe_w_expert_router"][layer, g].rearrange("(k p) e -> p k e", p=P))\
                       .then_inc(small_loaded, 16)
                act.dma_start(router_b[:, layer, 0:EG],
                              a["moe_b_group_router"][layer].rearrange("(o g) -> o g", o=1).to_broadcast([P, EG]))\
                   .then_inc(small_loaded, 16)
                act.dma_start(router_b[:, layer, EG:],
                              a["moe_b_expert_router"][layer].rearrange("(o g) e -> o (g e)", o=1).to_broadcast([P, E]))\
                   .then_inc(small_loaded, 16)
            act.dma_start(dskip[:], a["ssm_d"][0].rearrange("(k p) -> p k", p=P),
                          allow_slow_non_contiguous=True).then_inc(small_loaded, 16)

            def norm_root(i):
                act.wait_ge(ms_ready, i + 1)
                nc.scalar.activation(small[:, 2, :], small[:, 1, :], ACT.Sqrt).then_inc(rms_ready, 1)

            def turn_evac(i):
                for g in range(4):
                    act.wait_ge(tr_done, 4 * i + g + 1)
                    nc.scalar.copy(xnT[:, 2 * g:2 * g + 2, :], ps[:, g % 2, :].rearrange("p (k t) -> p k t", k=2))\
                      .then_inc(tr_evac, 1)

            norm_root(0)
            turn_evac(0)

            def evac_qkv(u):
                s, c = divmod(u, UNITS)
                act.wait_ge(qkv_done, u + 1)
                src = ps[:, u % 3, 0:WCOL]
                dst = qk[:, s % 2, c, :] if c < 4 else v[:, s % 2, c - 4, :]
                if c < HPS:
                    dst = dst.rearrange("p (t q) -> p t q", t=TT)
                    src = src.rearrange("p (t q) -> p t q", t=TT)[:, :, ::-1]
                nc.scalar.copy(dst, src).then_inc(qkv_evac, 1)

            def exps(hp):
                act.wait_ge(nmax_ready, hp + 1)
                for h in range(2):
                    for qt in range(2):
                        w = slice(0, P) if qt == 0 else slice(P, 3 * P)
                        sl = s_sb[:, hp % 2, h, w]
                        nc.scalar.activation(sl, sl, ACT.Exp, bias=stat[:, 0, hp % 2, h, qt:qt + 1],
                                             accum_out=stat[:, 1, hp % 2, h, qt:qt + 1]).then_inc(exp_done, 1)

            def evac_pT(hp):
                act.wait_ge(pt_done, hp + 1)
                nc.scalar.copy(pT[:], ps[:, 5:7, 0:3 * P]).then_inc(pt_evac_a, 1)

            def evac_o(hp):
                act.wait_ge(o_done, hp + 1)
                nc.scalar.copy(oT[:, hp, :].rearrange("p (t q) -> p t q", t=TT),
                               ps[:, 7, 0:T].rearrange("p (t q) -> p t q", t=TT)[:, :, ::-1]).then_inc(o_evac, 1)

            for u in range(UNITS):
                evac_qkv(u)
            for s in range(1, RING + 1):
                u, hp = UNITS * s, HPS * (s - 1)
                more_units = s < RING
                steps = [(evac_qkv, u), (evac_qkv, u + 1), (exps, hp), (evac_qkv, u + 2), (evac_pT, hp),
                         (evac_qkv, u + 3), (evac_o, hp), (exps, hp + 1), (evac_qkv, u + 4), (evac_pT, hp + 1),
                         (evac_qkv, u + 5), (evac_o, hp + 1)]
                for step, arg in steps:
                    if more_units or step is not evac_qkv:
                        step(arg)

            def moe_act(S, n):
                for u in range(4):
                    act.wait_ge(S.gath_done, 4 * n + u + 1)
                    nc.scalar.copy(xg[:, 2 * u:2 * u + 2, :], ps[:, u % 2, :].rearrange("p (c s) -> p c s", c=2))\
                      .then_inc(S.xg_evac, 1)
                act.wait_ge(S.turn_done, n + 1)
                nc.scalar.copy(pickT[:], ps[:, 5, :].rearrange("p (r t) -> p r t", r=2)).then_inc(S.pt_evac, 1)
                for r in range(2):
                    act.wait_ge(S.gu_done, 2 * n + r + 1)
                    nc.scalar.activation(sg[:, r, :], ps[:, 2 + r, 0:F], ACT.Silu).then_inc(S.silu_done, 1)
                for r in range(2):
                    act.wait_ge(S.hT_done, 2 * n + r + 1)
                    nc.scalar.copy(hidT[:, r], ps[:, 4, 0:F].rearrange("p (j s) -> p j s", j=FT)).then_inc(S.hT_evac, 1)
                    act.wait_ge(S.down_done, 2 * n + r + 1)
                    act.wait_ge(S.gslot_ready, 2 * n + 2)
                    nc.scalar.activation(yh[:, r, :].rearrange("p (b n) -> p b n", b=2), ps[:, 6:8, :], ACT.Copy,
                                         scale=gslot[:, r:r + 1]).then_inc(S.yh_done, 1)

            def layer_moe(layer):
                i = 2 * layer + 1
                norm_root(i)
                for tt in range(TT):
                    act.wait_ge(xn_ready, 2 * i + tt + 1)
                    nc.scalar.copy(xh[:, tt, :], xn[:, tt, :]).then_inc(xh_ready, 1)
                turn_evac(i)
                act.wait_ge(glog_ready, layer + 1)
                nc.scalar.activation(route[:, 0, :, 0:EG], route[:, 1, :, 0:EG], ACT.Exp).then_inc(gexp_done, 1)
                act.wait_ge(e2_ready, layer + 1)
                nc.scalar.activation(small[:, 9, :], small[:, 8, :], ACT.Exp).then_inc(e2_done, 1)
                if layer == 0:
                    with act.Fori(0, BREAKS[0]) as it:
                        moe_act(main[layer], it)
                    act.wait_ge(step_ready, 1)
                    nc.scalar.activation(disc[:, 0, 0:2], logstep[:], ACT.Exp).then_inc(step_exp, 1)
                    act.wait_ge(step_ready, 2)
                    nc.scalar.activation(disc[:, 2, :], disc[:, 1, :], ACT.Exp).then_inc(step_exp, 1)
                    act.wait_ge(ang_ready, 1)
                    nc.scalar.activation(disc[:, 8:10, :], disc[:, 6:8, :], ACT.Sin).then_inc(ang_sin, 1)
                    with act.Fori(BREAKS[0], NQ) as it:
                        moe_act(main[layer], it)
                else:
                    with act.Fori(0, NQ) as it:
                        moe_act(main[layer], it)
                act.wait_ge(count_ready, layer + 1)
                most = act.value_load(count_i[0:1, layer:layer + 1], min_val=0, max_val=T)
                with act.If(most > CAP):
                    with act.Fori(0, WINDOWS - 1) as w:
                        with act.Fori(0, NQ) as it:
                            moe_act(more[layer], w * NQ + it)
                act.nop()

            layer_moe(0)
            norm_root(2)
            turn_evac(2)
            def gelu(k):
                act.wait_ge(gelu_in, k + 1)
                nc.scalar.activation(yT[:, :, k * CH:(k + 1) * CH], yb[:].rearrange("p (i t) -> p i t", i=KT),
                                     ACT.Gelu_apprx_tanh).then_inc(gelu_done, 1)

            def gate(u):
                act.wait_ge(glu_done, u + 1)
                if u >= 2:
                    act.wait_ge(glu_added, u - 1)
                nc.scalar.activation(sig[:, u % 2, :], ps[:, 6 + u % 2, WCOL:2 * WCOL], ACT.Sigmoid).then_inc(sig_done, 1)

            gelu(0)
            gelu(1)
            gate(0)
            gate(1)
            gelu(2)
            gate(2)
            gate(3)
            gelu(3)
            for u in range(RING, 2 * RING):
                gate(u)
            layer_moe(1)
            norm_root(4)

        @block.vector
        def _(dve):
            lk = Chain(dve, dve_chain)
            V = nc.vector

            def norm(i):
                ss, ms, rt, r0, t0, t1, rs = (small[:, j, :] for j in (0, 1, 2, 3, 4, 5, 6))
                for tt in range(TT):
                    lk(V.tensor_tensor_reduce(out=xn[:, tt, :], in0=x[:, tt, :], in1=x[:, tt, :], scale=1.0, scalar=0.0,
                                              op0=ALU.mult, op1=ALU.add, accum_out=ss[:, tt:tt + 1]))
                V.tensor_scalar(ms, ss, 1.0 / D, EPS, ALU.mult, ALU.add).then_inc(ms_ready, 1)
                dve.wait_ge(rms_ready, i + 1)
                lk(V.reciprocal(r0, rt))
                lk(V.tensor_tensor(t0, r0, r0, ALU.mult))
                lk(V.tensor_tensor(t1, t0, ms, ALU.mult))
                lk(V.tensor_scalar(t0, t1, -0.5, 1.5, ALU.mult, ALU.add))
                lk(V.tensor_tensor(rs, r0, t0, ALU.mult))
                dve.wait_ge(normw_loaded, 16 * (i + 1))
                for tt in range(TT):
                    V.scalar_tensor_tensor(out=xn[:, tt, :], in0=x[:, tt, :], scalar=rs[:, tt:tt + 1], in1=normw[:],
                                           op0=ALU.mult, op1=ALU.mult).then_inc(xn_ready, 1)

            dve.wait_ge(x_loaded, 16)
            norm(0)

            dve.wait_ge(rb_loaded, 16)
            far = REV - 2 * MAXREL
            lk(V.tensor_copy(rb_rev[:, far:], rb_row[:, NREL - 1:0:-1]))
            V.tensor_copy(rb_rev[:, 0:far], rb_row[:, NREL - 1:NREL].to_broadcast([H, far])).then_inc(rev_ready, 1)

            def constants():
                dve.wait_ge(small_loaded, 16 * 18)
                d = disc
                step = d[:, 0, 0:2]
                lr, li, dec = d[:, 3, :], lam[:, 1, :], d[:, 2, :]

                def by_group(ap):
                    return ap.rearrange("s (g p) -> s g p", g=2)

                lk(V.tensor_scalar(lr, lam[:, 0, :], -1e-4, None, ALU.min))
                V.memset(d[:, 0, 2:4], 0.0).then_inc(step_ready, 1)
                dve.wait_ge(step_exp, 1)
                stepb = step.unsqueeze(2).to_broadcast([ST, 2, NS])
                V.tensor_tensor(by_group(d[:, 1, :]), by_group(lr), stepb, ALU.mult).then_inc(step_ready, 1)
                ang, cyc, t1, t2 = d[:, 4, :], d[:, 5, :], d[:, 10, :], d[:, 11, :]
                lk(V.tensor_tensor(by_group(ang), by_group(li), stepb, ALU.mult))
                MAGIC = float(1.5 * 2 ** 23)
                c1 = 6.28125
                c2 = float(np.float32(np.round((2 * np.pi - c1) * 2 ** 24) / 2 ** 24))
                c3 = float(2 * np.pi - c1 - c2)
                lk(V.tensor_scalar(cyc, ang, float(1 / (2 * np.pi)), None, ALU.mult))
                lk(V.tensor_scalar(t1, cyc, MAGIC, None, ALU.add))
                lk(V.tensor_scalar(cyc, t1, MAGIC, None, ALU.subtract))
                lk(V.scalar_tensor_tensor(out=t1, in0=cyc, scalar=-c1, in1=ang, op0=ALU.mult, op1=ALU.add))
                lk(V.scalar_tensor_tensor(out=t2, in0=cyc, scalar=-c2, in1=t1, op0=ALU.mult, op1=ALU.add))
                lk(V.scalar_tensor_tensor(out=t1, in0=cyc, scalar=-c3, in1=t2, op0=ALU.mult, op1=ALU.add))
                PI = float(np.nextafter(np.float32(np.pi), np.float32(0)))
                lk(V.tensor_scalar(d[:, 6, :], t1, -PI, PI, ALU.max, ALU.min))
                lk(V.tensor_scalar(t2, d[:, 6, :], -1.0, None, ALU.mult))
                lk(V.tensor_tensor(t1, d[:, 6, :], t2, ALU.max))
                V.tensor_scalar(d[:, 7, :], t1, -1.0, float(np.pi / 2), ALU.mult, ALU.add).then_inc(ang_ready, 1)
                dve.wait_ge(ang_sin, 1)
                dve.wait_ge(step_exp, 2)
                sin, cos = d[:, 8, :], d[:, 9, :]
                are, aim, den, nre = d[:, 12, :], d[:, 13, :], d[:, 5, :], d[:, 14, :]
                lk(V.tensor_tensor(are, dec, cos, ALU.mult))
                lk(V.tensor_tensor(aim, dec, sin, ALU.mult))
                lk(V.tensor_scalar(nre, are, -1.0, None, ALU.add))
                lk(V.tensor_tensor(t1, lr, lr, ALU.mult))
                lk(V.tensor_tensor(t2, li, li, ALU.mult))
                lk(V.tensor_tensor(den, t1, t2, ALU.add))
                lk(V.reciprocal(d[:, 15, :], den))
                lk(V.tensor_tensor(t1, nre, lr, ALU.mult))
                lk(V.tensor_tensor(t2, aim, li, ALU.mult))
                lk(V.tensor_tensor(den, t1, t2, ALU.add))
                lk(V.tensor_tensor(d[:, 4, :], den, d[:, 15, :], ALU.mult))
                lk(V.tensor_tensor(t1, aim, lr, ALU.mult))
                lk(V.tensor_tensor(t2, nre, li, ALU.mult))
                lk(V.tensor_tensor(den, t1, t2, ALU.subtract))
                V.tensor_tensor(d[:, 1, :], den, d[:, 15, :], ALU.mult).then_inc(par_ready, 1)

                dve.wait_ge(const_ready, 7)
                dve.wait_ge(c_turned, 1)
                for r in range(2):
                    for half in range(2):
                        for g2 in range(2):
                            part = slice(NS * g2, NS * (g2 + 1))
                            src = ps[part, 4 + 2 * r + half, :].rearrange("p (s g c) -> p s g c", g=2, c=GC)[:, :, g2, :]
                            rows = slice(16 * half, 16 * (half + 1))
                            cols = slice(GC * g2, GC * (g2 + 1))
                            if r == 0:
                                V.tensor_copy(cT[part, 0, rows, cols], src)
                                lk(V.tensor_scalar(cT[part, 1, rows, cols], src, -1.0, None, ALU.mult))
                            else:
                                lk(V.tensor_scalar(cT[part, 2, rows, cols], src, -1.0, None, ALU.mult))
                dve.wait_ge(par_turned, 1)
                lk(V.tensor_copy(par[:], ps[:, 3, 0:5 * ST].rearrange("p (j s) -> p j s", j=5)))
                dve.wait_ge(braw_loaded, 64)
                lk(V.memset(b_blk[:], 0.0))
                fre = par[:, 0, :].unsqueeze(2).to_broadcast([P, ST, GC])
                fim = par[:, 1, :].unsqueeze(2).to_broadcast([P, ST, GC])
                for r, (fa, fb, op) in enumerate(((fre, fim, ALU.subtract), (fim, fre, ALU.add))):
                    lk(V.tensor_tensor(b_tmp[:, 0], b_raw[:, 0], fa, ALU.mult))
                    lk(V.tensor_tensor(b_tmp[:, 1], b_raw[:, 1], fb, ALU.mult))
                    for g2 in range(2):
                        part = slice(NS * g2, NS * (g2 + 1))
                        ins = V.tensor_tensor(b_blk[part, r, :, GC * g2:GC * (g2 + 1)], b_tmp[part, 0], b_tmp[part, 1], op)
                        if r == 1 and g2 == 1:
                            ins.then_inc(b_ready, 1)
                        else:
                            lk(ins)
                dve.wait_ge(b_turned, 1)
                lk(V.tensor_copy(bT[:], ps[:, 4:8, :].rearrange("p (r h) (i q) -> p r (h i) q", r=2, q=P)))

            def tables():
                c1s, s1s = par[:, 3, :], par[:, 4, :]
                wc, ws, u1, u2, u3 = (sc[:, j, :] for j in range(5))
                lk(V.memset(cosT[:, :, 0:1], 1.0))
                lk(V.memset(sinT[:, :, 0:1], 0.0))
                lk(V.tensor_copy(wc, c1s))
                lk(V.tensor_copy(ws, s1s))
                m = 1
                while m < CH:
                    n_el = ST * m
                    ta = t_tmp[:, 0, 0:n_el].rearrange("p (s m) -> p s m", m=m)
                    td = t_tmp[:, 1, 0:n_el].rearrange("p (s m) -> p s m", m=m)
                    wcb = wc.unsqueeze(2).to_broadcast([P, ST, m])
                    wsb = ws.unsqueeze(2).to_broadcast([P, ST, m])
                    c0, s0 = cosT[:, :, 0:m], sinT[:, :, 0:m]
                    lk(V.tensor_tensor(ta, c0, wcb, ALU.mult))
                    lk(V.tensor_tensor(td, s0, wsb, ALU.mult))
                    lk(V.tensor_tensor(cosT[:, :, m:2 * m], ta, td, ALU.subtract))
                    lk(V.tensor_tensor(ta, c0, wsb, ALU.mult))
                    lk(V.tensor_tensor(td, s0, wcb, ALU.mult))
                    lk(V.tensor_tensor(sinT[:, :, m:2 * m], ta, td, ALU.add))
                    lk(V.tensor_tensor(u1, wc, wc, ALU.mult))
                    lk(V.tensor_tensor(u2, ws, ws, ALU.mult))
                    lk(V.tensor_tensor(u3, wc, ws, ALU.mult))
                    lk(V.tensor_tensor(wc, u1, u2, ALU.subtract))
                    lk(V.tensor_scalar(ws, u3, 2.0, None, ALU.mult))
                    m *= 2
                V.tensor_copy(u1, wc).then_inc(tables_ready, 1)

            dve.wait_ge(bias_loaded, 32)
            for col in (P - CH, 3 * P - CH):
                lk(V.memset(bias[P - CH:P, :, col:col + CH], NEG))

            def att_norm(hp):
                b = hp % 2
                dve.wait_ge(exp_done, 4 * hp + 4)
                lk(V.reciprocal(stat[:, 2, b], stat[:, 1, b]))
                for qt, w in ((0, slice(0, P)), (1, slice(P, 3 * P))):
                    n = w.stop - w.start
                    V.tensor_tensor(s_sb[:, b, :, w], s_sb[:, b, :, w],
                                    stat[:, 2, b, :, qt:qt + 1].to_broadcast([P, 2, n]), ALU.mult).then_inc(p_ready, 1)

            def att_max(hp):
                b = hp % 2
                dve.wait_ge(s_done, hp + 1)
                if hp >= 2:
                    dve.wait_ge(pt_done, hp - 1)
                lk(V.scalar_tensor_tensor(out=s_sb[:, b], in0=ps[:, 3:5, 0:3 * P], scalar=HD ** -0.5,
                                          in1=bias[:, 2 * hp:2 * hp + 2, :], op0=ALU.mult, op1=ALU.add))
                lk(V.tensor_reduce(stat[:, 0, b, :, 0:1], s_sb[:, b, :, 0:P], AX.X, ALU.max, negate=True))
                V.tensor_reduce(stat[:, 0, b, :, 1:2], s_sb[:, b, :, P:3 * P], AX.X, ALU.max, negate=True)\
                 .then_inc(nmax_ready, 1)

            for hp in range(0, HP, HPS):
                att_max(hp)
                att_max(hp + 1)
                att_norm(hp)
                att_norm(hp + 1)

            for u in range(2 * RING):
                s, tt = divmod(u, 2)
                dve.wait_ge(proj_done, u + 1)
                xs = x[:, tt, s * WCOL:(s + 1) * WCOL]
                V.tensor_tensor(xs, xs, ps[:, u % 2, 0:WCOL], ALU.add).then_inc(proj_added, 1)
            dve.wait_ge(proj_added, 2 * RING)

            def routing(layer):
                def bc(ap, n):
                    return ap.unsqueeze(2).to_broadcast([P, TT, n])

                r0, r1, r2, r3, r4, r5 = (route[:, j] for j in range(6))
                v0, v1, v2, v3 = (small[:, j, :] for j in (7, 8, 9, 10))
                m1 = small[:, 11, :]
                gl, el = glog[:, :, 0:EG], glog[:, :, EG:]
                dve.wait_ge(logit_done, layer + 1)
                lk(V.tensor_tensor(glog[:], ps[:, 2, 0:TT * NR].rearrange("p (t n) -> p t n", t=TT),
                                   router_b[:, layer].unsqueeze(1).to_broadcast([P, TT, NR]), ALU.add))
                lk(V.tensor_reduce(v0.unsqueeze(2), gl, AX.X, ALU.max))
                V.tensor_tensor(r1[:, :, 0:EG], gl, bc(v0, EG), ALU.subtract).then_inc(glog_ready, 1)
                lk(V.tensor_tensor(r2[:, :, 0:EG], gl, bc(v0, EG), ALU.is_equal))
                lk(V.tensor_tensor(r3[:, :, 0:EG], r2[:, :, 0:EG], rev_g[:].unsqueeze(1).to_broadcast([P, TT, EG]), ALU.mult))
                lk(V.tensor_reduce(v1.unsqueeze(2), r3[:, :, 0:EG], AX.X, ALU.max))
                lk(V.tensor_tensor(r2[:, :, 0:EG], rev_g[:].unsqueeze(1).to_broadcast([P, TT, EG]), bc(v1, EG), ALU.is_equal))
                dve.wait_ge(gexp_done, layer + 1)
                lk(V.tensor_reduce(v1.unsqueeze(2), r0[:, :, 0:EG], AX.X, ALU.add))
                lk(V.reciprocal(v3, v1))
                lk(V.tensor_scalar(r3[:, :, 0:EG], r2[:, :, 0:EG], 1.0, -NEG, ALU.subtract, ALU.mult))
                for tt in range(TT):
                    hot = r2[:, tt, 0:EG].unsqueeze(2).to_broadcast([P, EG, EPG])
                    low = r3[:, tt, 0:EG].unsqueeze(2).to_broadcast([P, EG, EPG])
                    e4 = r4[:, tt, :].rearrange("p (g e) -> p g e", g=EG)
                    lk(V.tensor_tensor(e4, el[:, tt, :].rearrange("p (g e) -> p g e", g=EG), hot, ALU.mult))
                    lk(V.tensor_tensor(e4, e4, low, ALU.add))
                reve = rev_e[:].unsqueeze(1).to_broadcast([P, TT, E])

                def first_max(src, top, hot):
                    lk(V.tensor_reduce(top.unsqueeze(2), src, AX.X, ALU.max))
                    lk(V.tensor_tensor(r3, src, bc(top, E), ALU.is_equal))
                    lk(V.tensor_tensor(r1, r3, reve, ALU.mult))
                    lk(V.tensor_reduce(v0.unsqueeze(2), r1, AX.X, ALU.max))
                    lk(V.tensor_tensor(hot, reve, bc(v0, E), ALU.is_equal))

                first_max(r4, m1, r5)
                lk(V.scalar_tensor_tensor(out=r0, in0=r5, scalar=2.0 * NEG, in1=r4, op0=ALU.mult, op1=ALU.add))
                first_max(r0, v2, r2)
                V.tensor_tensor(v1, v2, m1, ALU.subtract).then_inc(e2_ready, 1)
                V.tensor_tensor(sel[:], r5, r2, ALU.add).then_inc(sel_ready, 1)
                dve.wait_ge(e2_done, layer + 1)
                lk(V.tensor_scalar(v0, v2, 1.0, None, ALU.add))
                lk(V.reciprocal(m1, v0))
                lk(V.tensor_tensor(v0, m1, v3, ALU.mult))
                lk(V.tensor_tensor(v1, v0, v2, ALU.mult))
                lk(V.tensor_tensor(r0, r5, bc(v0, E), ALU.mult))
                lk(V.tensor_tensor(r1, r2, bc(v1, E), ALU.mult))
                lk(V.tensor_tensor(gates[:], r0, r1, ALU.add))
                dve.wait_ge(rank_done, layer + 1)
                lk(V.tensor_scalar(r0, ps[:, 3, 0:TT * E].rearrange("p (t e) -> p t e", t=TT), 1.0, None, ALU.add))
                lk(V.tensor_tensor(r1, r0, sel[:], ALU.mult))
                lk(V.tensor_scalar(rank[:], r1, -1.0, None, ALU.add))
                lk(V.tensor_reduce(r0[:, 0, 0:1], ps[:, 3, TT * E:(TT + 1) * E], AX.X, ALU.max))
                V.tensor_copy(count_i[:, layer:layer + 1], r0[:, 0, 0:1]).then_inc(count_ready, 1)
                dve.wait_ge(count_ready, layer + 1)

            def moe_dve(S, n, it, w=None):
                CHAIN = 2
                c = Chain(dve, S.chain, CHAIN * n)
                c(V.tensor_copy(gq[:], gates[:, :, bass.ds(QUAD * it, QUAD)]))
                if w is not None:
                    dve.wait_ge(S.window, w + 1)
                for tt in range(TT):
                    rk = rank[:, tt, bass.ds(QUAD * it, QUAD)].unsqueeze(2).to_broadcast([P, QUAD, CAP])
                    V.tensor_tensor(pick[:, tt], slot_iota[:].unsqueeze(1).to_broadcast([P, QUAD, CAP]), rk,
                                    ALU.is_equal).then_inc(S.pick_ready, 1)
                dve.wait_ge(S.turn_done, n + 1)
                for h in range(2):
                    part = slice(CAP * h, CAP * (h + 1))
                    V.tensor_copy(gslot[part, :], ps[part, 4, 256:256 + 2 * QUAD].rearrange("p (r e) -> p r e", r=2)
                                  [:, :, :].rearrange("p r e -> p (r e)")[:, h:h + 7:6]).then_inc(S.gslot_ready, 1)
                for r in range(2):
                    dve.wait_ge(S.silu_done, 2 * n + r + 1)
                    V.tensor_tensor(hid[:, r, :], sg[:, r, :], ps[:, 2 + r, F:2 * F], ALU.mult).then_inc(S.hid_ready, 1)
                for r in range(2):
                    dve.wait_ge(S.yh_done, 2 * n + r + 1)
                    dve.wait_ge(S.gslot_ready, 2 * n + 2)
                    V.scalar_tensor_tensor(out=yl[:, r, :].rearrange("p (b n) -> p b n", b=2), in0=ps[:, 6:8, :],
                                           scalar=gslot[:, r:r + 1],
                                           in1=yh[:, r, :].bitcast(F32).rearrange("p (b n) -> p b n", b=2),
                                           op0=ALU.mult, op1=ALU.subtract).then_inc(S.yl_done, 1)
                for u in range(4):
                    tt, h = divmod(u, 2)
                    dve.wait_ge(S.comb_done, 4 * n + u + 1)
                    xs = x[:, tt, 512 * h:512 * (h + 1)]
                    V.tensor_tensor(xs, xs, ps[:, u % 2, :], ALU.add).then_inc(S.x_added, 1)
                c(V.tensor_copy(small[:, 7, :], small[:, 6, :]))
                dve.wait_ge(S.x_added, 4 * n + 4)
                assert c.n == CHAIN

            def layer_moe(layer):
                i = 2 * layer + 1
                norm(i)
                for tt in range(TT):
                    dve.wait_ge(xh_ready, 2 * layer + tt + 1)
                    V.tensor_tensor(xl[:, tt, :], xn[:, tt, :], xh[:, tt, :].bitcast(F32), ALU.subtract).then_inc(xl_ready, 1)
                routing(layer)
                if layer == 0:
                    with dve.Fori(0, BREAKS[0]) as it:
                        moe_dve(main[layer], it, it)
                    constants()
                    with dve.Fori(BREAKS[0], BREAKS[1]) as it:
                        moe_dve(main[layer], it, it)
                    tables()
                    with dve.Fori(BREAKS[1], NQ) as it:
                        moe_dve(main[layer], it, it)
                else:
                    with dve.Fori(0, NQ) as it:
                        moe_dve(main[layer], it, it)
                most = dve.value_load(count_i[0:1, layer:layer + 1], min_val=0, max_val=T)
                with dve.If(most > CAP):
                    with dve.Fori(0, WINDOWS - 1) as w:
                        V.tensor_scalar(rank[:], rank[:], float(CAP), None, ALU.subtract)\
                         .then_inc(more[layer].window, 1)
                        with dve.Fori(0, NQ) as it:
                            moe_dve(more[layer], w * NQ + it, it, w)
                dve.nop()

            layer_moe(0)

            norm(2)
            dec_s = par[:, 2, :]
            wc, ws, u1, u2 = (sc[:, j, :] for j in range(4))
            for q in range(4):
                dq = dec_s.rearrange("p (q i j) -> p q j i", q=4, i=2)[:, q]
                lk(V.tensor_copy(decayT[:, q], dq.unsqueeze(3).to_broadcast([P, 4, 2, CH])))
            lk(V.memset(decayT[:].rearrange("p q j i t -> p (q j i) t")[:, :, 0:1], 0.0))
            wre, wim = sc[:, 6, :], sc[:, 7, :]
            for w, src in ((wre, wc), (wim, ws)):
                lk(V.tensor_tensor(u1, src, dec_s, ALU.mult))
                for q in range(4):
                    lk(V.tensor_copy(w[:, 8 * q:8 * q + 8].rearrange("p (j i) -> p j i", j=4),
                                     u1.rearrange("p (q i j) -> p q j i", q=4, i=2)[:, q]))
            zre, zim, cre, cim = (sc[:, j, :] for j in (8, 9, 10, 11))

            def loc(ap):
                return ap.rearrange("p (j i t) -> p j i t", j=4, i=2)

            def step(n):
                k, q = divmod(n, 4)
                mine = slice(8 * q, 8 * q + 8)
                dve.wait_ge(bu_done, n + 1)
                bu = ps[:, 0:4, 0:4 * CH].rearrange("p j (i r t) -> p j i r t", i=2, r=2)
                co = cosT[:, mine, :].rearrange("p (i j) t -> p j i t", i=2)
                si = sinT[:, mine, :].rearrange("p (i j) t -> p j i t", i=2)
                V.tensor_tensor(loc(tb[:, 0, :]), bu[:, :, :, 0, :], co, ALU.mult)
                V.tensor_tensor(loc(tb[:, 1, :]), bu[:, :, :, 1, :], si, ALU.mult)
                V.tensor_tensor(loc(tb[:, 2, :]), bu[:, :, :, 1, :], co, ALU.mult)
                V.tensor_tensor(loc(tb[:, 3, :]), bu[:, :, :, 0, :], si, ALU.mult).then_inc(bu_used, 1)
                dve.wait_ge(bu_used, n + 1)
                V.tensor_tensor(tb[:, 0, :], tb[:, 0, :], tb[:, 1, :], ALU.add)
                lk(V.tensor_tensor(tb[:, 2, :], tb[:, 2, :], tb[:, 3, :], ALU.subtract))
                if k:
                    head = tb[:, 0:3:2, :].rearrange("p r (s t) -> p r s t", t=CH)[:, :, :, 0]
                    lk(V.tensor_tensor(head, head, sc[:, 10:12, mine], ALU.add))
                if n >= 2:
                    dve.wait_ge(q_ready, 4 * (n - 1))
                dq = decayT[:, q].rearrange("p j i t -> p (j i t)")
                V.tensor_tensor_scan(zb[:, n % 2, 0, :], dq, tb[:, 0, :], 0.0, ALU.mult, ALU.add)
                V.tensor_tensor_scan(zb[:, n % 2, 1, :], dq, tb[:, 2, :], 0.0, ALU.mult, ALU.add).then_inc(z_ready, 1)
                dve.wait_ge(z_ready, n + 1)
                if k < NCH - 1:
                    last = zb[:, n % 2].rearrange("p r (s t) -> p r s t", t=CH)[:, :, :, CH - 1]
                    lk(V.tensor_copy(sc[:, 8:10, mine], last))
                    if q == 3:
                        lk(V.tensor_tensor(u1, wre, zre, ALU.mult))
                        lk(V.tensor_tensor(u2, wim, zim, ALU.mult))
                        lk(V.tensor_tensor(cre, u1, u2, ALU.subtract))
                        lk(V.tensor_tensor(u1, wre, zim, ALU.mult))
                        lk(V.tensor_tensor(u2, wim, zre, ALU.mult))
                        lk(V.tensor_tensor(cim, u1, u2, ALU.add))

            def finish(k):
                if k:
                    dve.wait_ge(gelu_done, k)
                lk(V.tensor_tensor(yb[:].rearrange("p (i t) -> p i t", i=KT), xnT[:, :, k * CH:(k + 1) * CH],
                                   dskip[:].unsqueeze(2).to_broadcast([P, KT, CH]), ALU.mult))
                dve.wait_ge(y_done, k + 1)
                V.tensor_tensor(yb[:], yb[:], ps[:, 4 + k % 2, :], ALU.add).then_inc(gelu_in, 1)

            def glu(u):
                tt, s = divmod(u, RING)
                dve.wait_ge(sig_done, u + 1)
                xs = x[:, tt, s * WCOL:(s + 1) * WCOL]
                lk(V.tensor_tensor(sig[:, u % 2, :], sig[:, u % 2, :], ps[:, 6 + u % 2, 0:WCOL], ALU.mult))
                V.tensor_tensor(xs, xs, sig[:, u % 2, :], ALU.add).then_inc(glu_added, 1)

            for n in range(4 * NCH):
                step(n)
                if n % 4 == 1 and n > 4:
                    finish(n // 4 - 1)
                if n == 14:
                    glu(0)
            glu(1)
            finish(NCH - 1)
            for u in range(2, 2 * RING):
                glu(u)
            dve.wait_ge(glu_added, 2 * RING)
            layer_moe(1)
            norm(4)

        @block.tensor
        def _(pe):
            mm = nc.tensor.matmul

            def turn(i):
                pe.wait_ge(xn_ready, 2 * i + 2)
                for g in range(4):
                    if g >= 2:
                        pe.wait_ge(tr_evac, 4 * i + g - 1)
                    for k in range(2):
                        for tt in range(TT):
                            kt = 2 * g + k
                            ins = nc.tensor.transpose(ps[:, g % 2, (2 * k + tt) * P:(2 * k + tt + 1) * P],
                                                      xn[:, tt, kt * P:(kt + 1) * P], ident[:])
                    ins.then_inc(tr_done, 1)
                pe.wait_ge(tr_evac, 4 * i + 4)

            pe.wait_ge(const_ready, 7)
            turn(0)

            def qkv(u):
                s, c = divmod(u, UNITS)
                if u >= 3:
                    pe.wait_ge(qkv_evac, u - 2)
                if c == 0:
                    pe.wait_ge(slot_full[s], 48)
                w = ring[:, s, :].rearrange("p (i k n) -> p i k n", i=3, k=KT)
                for kt in range(KT):
                    if c < 4:
                        ins = mm(ps[:, u % 3, 0:T], w[:, c // HPS, kt, (c % HPS) * P:(c % HPS + 1) * P], xnT[:, kt, :],
                                 start=(kt == 0), stop=(kt == KT - 1))
                    else:
                        ins = mm(ps[:, u % 3, 0:WCOL], xnT[:, kt, (c - 4) * P:(c - 3) * P], w[:, 2, kt, :],
                                 start=(kt == 0), stop=(kt == KT - 1))
                ins.then_inc(qkv_done, 1)
                if c == UNITS - 1:
                    pe.wait_ge(qkv_done, u + 1)
                    pe.sem_inc(slot_free[s], 1)

            def scores(hp):
                if hp:
                    pe.wait_ge(nmax_ready, hp)
                else:
                    pe.wait_ge(qkv_evac, 4)
                pe.wait_ge(qkv_evac, UNITS * (hp // HPS) + UNITS)
                for h in range(2):
                    rows = slice(HD * h, HD * (h + 1))
                    par_s, pair = (hp // HPS) % 2, hp % HPS
                    q, kk = qk[rows, par_s, pair, :], qk[rows, par_s, HPS + pair, :]
                    mm(ps[:, 3 + h, 0:P], q[:, 0:P], kk[:, 0:P], start=True, stop=True)
                    ins = mm(ps[:, 3 + h, P:3 * P], q[:, P:T], kk[:, 0:T], start=True, stop=True)
                ins.then_inc(s_done, 1)

            def turn_p(hp):
                pe.wait_ge(p_ready, 2 * hp + 2)
                if hp:
                    pe.wait_ge(pt_evac_a, hp)
                for h in range(2):
                    for j in range(3):
                        ins = nc.tensor.transpose(ps[:, 5 + h, j * P:(j + 1) * P],
                                                  s_sb[:, hp % 2, h, j * P:(j + 1) * P], ident[:])
                ins.then_inc(pt_done, 1)

            def mix(hp):
                pe.wait_ge(pt_evac_a, hp + 1)
                if hp:
                    pe.wait_ge(o_evac, hp)
                for h in range(2):
                    rows = slice(HD * h, HD * (h + 1))
                    vv = v[:, (hp // HPS) % 2]
                    cols = slice(HD * (2 * (hp % HPS) + h), HD * (2 * (hp % HPS) + h + 1))
                    mm(ps[rows, 7, 0:P], vv[:, 0, cols], pT[:, h, 0:P], start=True, stop=True)
                    mm(ps[rows, 7, P:T], vv[:, 0, cols], pT[:, h, P:2 * P], start=True, stop=False)
                    ins = mm(ps[rows, 7, P:T], vv[:, 1, cols], pT[:, h, 2 * P:3 * P], start=False, stop=True)
                ins.then_inc(o_done, 1)

            for u in range(UNITS):
                qkv(u)
            for s in range(1, RING + 1):
                u, hp = UNITS * s, HPS * (s - 1)
                steps = [(qkv, u), (scores, hp), (qkv, u + 1), (scores, hp + 1), (qkv, u + 2), (turn_p, hp),
                         (qkv, u + 3), (mix, hp), (qkv, u + 4), (turn_p, hp + 1), (qkv, u + 5), (mix, hp + 1)]
                for step, arg in steps:
                    if s < RING or step is not qkv:
                        step(arg)

            pe.wait_ge(o_evac, HP)
            for u in range(2 * RING):
                s, tt = divmod(u, 2)
                pe.wait_ge(slot_full[s], 64)
                if u >= 2:
                    pe.wait_ge(proj_added, u - 1)
                w = ring[:, s, 0:KT * WCOL].rearrange("p (k n) -> p k n", k=KT)
                for kt in range(KT):
                    ins = mm(ps[:, u % 2, 0:WCOL], oT[:, kt, tt * P:(tt + 1) * P], w[:, kt, :],
                             start=(kt == 0), stop=(kt == KT - 1))
                ins.then_inc(proj_done, 1)
                if tt == 1:
                    pe.wait_ge(proj_done, u + 1)
                    pe.sem_inc(slot_free[s], 1)

            def router(layer):
                pe.wait_ge(small_loaded, 16 * 18)
                for tt in range(TT):
                    for kt in range(KT):
                        ins = mm(ps[:, 2, tt * NR:(tt + 1) * NR], xnT[:, kt, tt * P:(tt + 1) * P],
                                 router_w[:, layer, kt, :], start=(kt == 0), stop=(kt == KT - 1))
                ins.then_inc(logit_done, 1)
                pe.wait_ge(sel_ready, layer + 1)
                mm(ps[:, 3, 0:E], before[:], sel[:, 0, :], start=True, stop=True)
                mm(ps[:, 3, E:2 * E], before[:], sel[:, 1, :], start=True, stop=False)
                mm(ps[:, 3, E:2 * E], ones[:], sel[:, 0, :], start=False, stop=True)
                mm(ps[:, 3, 2 * E:3 * E], ones[:], sel[:, 0, :], start=True, stop=False)
                mm(ps[:, 3, 2 * E:3 * E], ones[:], sel[:, 1, :], start=False, stop=True).then_inc(rank_done, 1)

            def moe_pe(S, n, start, dstart, per, dper):
                pe.wait_ge(S.pick_ready, 2 * n + 2)
                xs = [t[:].rearrange("p t (q c) -> p t q c", c=KT) for t in (xh, xl)]
                for u in range(4):
                    if u >= 2:
                        pe.wait_ge(S.xg_evac, 4 * n + u - 1)
                    for c in range(2):
                        for i in range(2 * TT):
                            part, tt = divmod(i, TT)
                            ins = mm(ps[:, u % 2, c * QS:(c + 1) * QS], xs[part][:, tt, :, 2 * u + c],
                                     pick[:, tt].rearrange("p e s -> p (e s)"), start=(i == 0), stop=(i == 2 * TT - 1))
                    ins.then_inc(S.gath_done, 1)
                for r in range(2):
                    for tt in range(TT):
                        nc.tensor.transpose(ps[:, 5, (2 * r + tt) * P:(2 * r + tt + 1) * P],
                                            pick[:, tt, 2 * r:2 * r + 2].rearrange("p e s -> p (e s)").bitcast(F32), ident[:])
                for r in range(2):
                    for tt in range(TT):
                        ins = mm(ps[:, 4, 256 + QUAD * r:256 + QUAD * (r + 1)],
                                 pick[:, tt, 2 * r:2 * r + 2].rearrange("p e s -> p (e s)").bitcast(F32), gq[:, tt, :],
                                 start=(tt == 0), stop=(tt == TT - 1))
                ins.then_inc(S.turn_done, 1)
                pe.wait_ge(S.xg_evac, 4 * n + 4)
                pe.wait_ge(S.gslot_ready, 2 * n + 2)
                for r in range(2):
                    for h in range(2):
                        pe.wait_ge(S.full[2 * r + h], start + per * (n + 1))
                    for c in range(KT):
                        for h in range(2):
                            s = 2 * r + h
                            w = ring[:, s, 0:GU].rearrange("p (u c f) -> p u c f", u=2, c=KT)[:, :, c, :]
                            ins = mm(ps[CAP * h:CAP * (h + 1), 2 + r, :], xg[:, c, CAP * s:CAP * (s + 1)], w,
                                     start=(c == 0), stop=(c == KT - 1))
                    ins.then_inc(S.gu_done, 1)
                for r in range(2):
                    pe.wait_ge(S.hid_ready, 2 * n + r + 1)
                    for j in range(FT):
                        ins = nc.tensor.transpose(ps[:, 4, j * P:(j + 1) * P], hid[:, r, j:F:FT], ident[:])
                    ins.then_inc(S.hT_done, 1)
                    pe.wait_ge(S.hT_evac, 2 * n + r + 1)
                    if r:
                        pe.wait_ge(S.yl_done, 2 * n + 1)
                    for h in range(2):
                        pe.wait_ge(S.dfull[2 * r + h], dstart + dper * (n + 1))
                    for j in range(FT):
                        for b in range(2):
                            for h in range(2):
                                s = 2 * r + h
                                w = ring[:, s, GU:SLOT].rearrange("p (j d) -> p j d", j=FT)[:, j, 512 * b:512 * (b + 1)]
                                ins = mm(ps[CAP * h:CAP * (h + 1), 6 + b, :], hidT[:, r, j, CAP * h:CAP * (h + 1)], w,
                                         start=(j == 0), stop=(j == FT - 1))
                    ins.then_inc(S.down_done, 1)
                pe.wait_ge(S.yl_done, 2 * n + 2)
                pe.wait_ge(S.pt_evac, n + 1)
                for u in range(4):
                    tt, b = divmod(u, 2)
                    if u >= 2:
                        pe.wait_ge(S.x_added, 4 * n + u - 1)
                    for i in range(4):
                        r, y = i // 2, (yh, yl)[i % 2]
                        ins = mm(ps[:, u % 2, :], pickT[:, r, tt * P:(tt + 1) * P], y[:, r, 512 * b:512 * (b + 1)],
                                 start=(i == 0), stop=(i == 3))
                    ins.then_inc(S.comb_done, 1)

            def turn_constants():
                pe.wait_ge(craw_loaded, 64)
                for r in range(2):
                    for i in range(KT):
                        ins = nc.tensor.transpose(ps[:, 4 + 2 * r + i // 4, (i % 4) * P:(i % 4 + 1) * P],
                                                  c_raw[:, r, i].rearrange("p u n -> p (u n)"), ident[:])
                ins.then_inc(c_turned, 1)
                pe.wait_ge(par_ready, 1)
                for j, src in enumerate((4, 1, 2, 9, 8)):
                    ins = nc.tensor.transpose(ps[:, 3, j * ST:(j + 1) * ST], disc[:, src, :], ident[0:ST, 0:ST])
                ins.then_inc(par_turned, 1)
                pe.wait_ge(b_ready, 1)
                for r in range(2):
                    for i in range(KT):
                        ins = nc.tensor.transpose(ps[:, 4 + 2 * r + i // 4, (i % 4) * P:(i % 4 + 1) * P],
                                                  b_blk[:, r, 4 * i:4 * i + 4].rearrange("p s c -> p (s c)"), ident[:])
                ins.then_inc(b_turned, 1)

            def layer_moe(layer):
                turn(2 * layer + 1)
                router(layer)
                pe.wait_ge(xl_ready, 2 * layer + 2)
                def passes(a, b):
                    with pe.Fori(a, b) as it:
                        moe_pe(main[layer], it, full_before(layer), 16 * NQ * layer, 32, 16)

                if layer == 0:
                    passes(0, BREAKS[0])
                    turn_constants()
                    passes(BREAKS[0], NQ)
                else:
                    passes(0, NQ)
                pe.wait_ge(count_ready, layer + 1)
                most = pe.value_load(count_i[0:1, layer:layer + 1], min_val=0, max_val=T)
                with pe.If(most > CAP):
                    pe.sem_inc(more[layer].ring_passed, 1)
                    with pe.Fori(0, WINDOWS - 1) as w:
                        with pe.Fori(0, NQ) as it:
                            n = w * NQ + it
                            moe_pe(more[layer], n, 0, 0, 192, 192)
                            pe.wait_ge(more[layer].down_done, 2 * n + 2)
                            pe.sem_inc(more[layer].ring_passed, 1)
                pe.nop()

            layer_moe(0)

            turn(2)

            def inputs(n):
                k, q = divmod(n, 4)
                if n:
                    pe.wait_ge(bu_used, n)
                for i in range(2):
                    for r in range(2):
                        for j in range(4):
                            rows = slice(32 * j, 32 * (j + 1))
                            o = (2 * i + r) * CH
                            ins = mm(ps[:, j, o:o + CH], bT[rows, r, 2 * q + i, :], xnT[rows, 2 * q + i, k * CH:(k + 1) * CH],
                                     start=True, stop=True, tile_position=(32 * j, 0))
                ins.then_inc(bu_done, 1)

            def half_unit(u2):
                u, half = divmod(u2, 2)
                tt, s = divmod(u, RING)
                if half == 0:
                    pe.wait_ge(gelu_done, 2 if tt == 0 else NCH)
                    pe.wait_ge(slot_full[s], full_before(1))
                    if u >= 2:
                        pe.wait_ge(glu_added, u - 1)
                w = ring[:, s, 0:KT * 2 * WCOL].rearrange("p (k n) -> p k n", k=KT)
                for kt in range(4 * half, 4 * half + 4):
                    ins = mm(ps[:, 6 + u % 2, :], yT[:, kt, tt * P:(tt + 1) * P], w[:, kt, :],
                             start=(kt == 0), stop=(kt == KT - 1))
                if half:
                    ins.then_inc(glu_done, 1)
                    if tt == 1:
                        pe.wait_ge(glu_done, u + 1)
                        pe.sem_inc(slot_free[s], 1)

            inputs(0)
            for n in range(4 * NCH):
                k, q = divmod(n, 4)
                if n + 1 < 4 * NCH:
                    inputs(n + 1)
                pe.wait_ge(q_ready, 4 * n + 4)
                if q == 0 and k >= 2:
                    pe.wait_ge(gelu_in, k - 1)
                for i in range(2):
                    for m, c in enumerate((0, 1, 2, 2)):
                        for j in range(4):
                            rows = slice(32 * j, 32 * (j + 1))
                            ins = mm(ps[rows, 4 + k % 2, (2 * q + i) * CH:(2 * q + i + 1) * CH],
                                     cT[:, c, 8 * q + 4 * i + j, :],
                                     qb[:, m, :].rearrange("p (j i t) -> p j i t", j=4, i=2)[:, j, i, :],
                                     start=(m == 0), stop=(m == 3), tile_position=(0, 32 * j))
                ins.then_inc(q_used, 1)
                if q == 3:
                    pe.wait_ge(q_used, n + 1)
                    pe.sem_inc(y_done, 1)
                if n >= 10:
                    half_unit(n - 10)
            for u2 in range(6, 4 * RING):
                half_unit(u2)
            layer_moe(1)


_INS = ["x", "norm_mix", "norm_ffn", "norm_final", "attn_w_qkv", "attn_w_o", "attn_rel_bias", "ssm_lambda_re",
        "ssm_lambda_im", "ssm_log_step", "ssm_b_re", "ssm_b_im", "ssm_c_re", "ssm_c_im", "ssm_d", "ssm_w_out",
        "moe_w_group_router", "moe_b_group_router", "moe_w_expert_router", "moe_b_expert_router", "moe_w_gate",
        "moe_w_up", "moe_w_down"]


def kernel(**inputs):
    import concourse.bacc as bacc
    from concourse.bass_utils import run_bass_kernel_spmd

    nc = bacc.Bacc("TRN2", target_bir_lowering=False, num_devices=1)
    arrays, aps = {}, {}
    for name in _INS:
        arr = np.ascontiguousarray(inputs[name])
        arrays[f"in_{name}"] = arr
        aps[name] = nc.dram_tensor(f"in_{name}", arr.shape, mybir.dt.from_np(arr.dtype), kind="ExternalInput").ap()
    out = nc.dram_tensor("out_0", (1, T, D), F32, kind="ExternalOutput").ap()
    trunk_program(nc, aps, out)
    r = run_bass_kernel_spmd(nc, [arrays], core_ids=[0])
    return r.results[0]["out_0"]
```

```python
from contextlib import ExitStack

import numpy as np

import concourse.bass as bass
from concourse import mybir

F32 = mybir.dt.float32
F32R = mybir.dt.float32r
I32 = mybir.dt.int32
ALU = mybir.AluOpType
ACT = mybir.ActivationFunctionType
AX = mybir.AxisListType

P = 128
D = 1024
T = 256
TT = T // P
KT = D // P
H, HD = 16, 64
HP = H // 2
CH = 64
MAXREL = 128
NREL = 2 * MAXREL + 1
G, GC, NS = 64, 16, 64
ST = G * NS // P
NCH = T // CH
EG, EPG = 4, 8
E = EG * EPG
F = D // 4
FT = F // P
CAP = 64
WINDOWS = T // CAP
QUAD = 4
QS = QUAD * CAP
NQ = E // QUAD
NR = EG + E
EPS = 1e-6
NEG = -1e30
RING = 4
SLOT = 3 * D * F // P
REV = 2 * T - 1 - P
WCOL = D // RING
HPS = WCOL // P
UNITS = 6
GU = 2 * D * F // P
WARM = {"start": 6, "norm": 7, "choice": 5, "ranks": 2, "state-space norm": 8, "last loads": 3}
TURNS = (2, 4)


def trunk_program(nc, a, out):
    ctx = ExitStack()
    with ctx:
        base = (nc.sbuf_base + 63) // 64 * 64
        where = [base]

        def fixed(name, shape, dt=F32):
            n = int(np.prod(shape[1:])) * 4
            t = nc.alloc_sbuf_tensor_at(name, shape, dt, offset=where[0])
            where[0] += (n + 63) // 64 * 64
            return t

        def sem(name):
            return ctx.enter_context(nc.semaphore(name))

        ring = fixed("ring", [P, RING, SLOT])
        x = fixed("x", [P, TT, D])
        normw = fixed("normw", [P, D])
        xnT_at = where[0]
        xnT = fixed("xnT", [P, KT, T])
        bT = fixed("bT", [P, 2, KT, P])
        cT = fixed("cT", [P, 2, ST, 2 * GC])
        q4 = fixed("q4", [P, 4 * T])
        par = fixed("par", [P, 5, ST])
        router_w = fixed("router_w", [P, 2, KT, NR])
        router_b = fixed("router_b", [P, 2, NR])
        ident = fixed("ident", [P, P])
        before = fixed("before", [P, P])
        ones = fixed("ones", [P, P])
        slot_iota = fixed("slot_iota", [P, CAP])
        rev_e = fixed("rev_e", [P, E])
        rev_g = fixed("rev_g", [P, EG])
        small = fixed("small", [P, 12, TT])
        lam = fixed("lam", [ST, 2, P])
        logstep = fixed("logstep", [ST, 2])
        dskip = fixed("dskip", [P, KT])
        rank = fixed("rank", [P, TT, E])
        gates = fixed("gates", [P, TT, E])
        route = fixed("route", [P, 6, TT, E])
        glog = fixed("glog", [P, TT, NR])
        gexp = fixed("gexp", [P, TT, EG])
        sel = fixed("sel", [P, TT, E])
        count_i = fixed("count_i", [P, 2], I32)
        sc = fixed("sc", [P, 14, ST])
        arena = where[0]

        def at(name, shape, off, dt=F32):
            return nc.alloc_sbuf_tensor_at(name, shape, dt, offset=arena + 4 * off)

        qk = at("qk", [P, 2, 4, T], 0)
        v = at("v", [P, 2, TT, WCOL], 2048)
        oT = at("oT", [P, KT, T], 3072)
        bias = at("bias", [P, H, 3 * P], 5120)
        s_sb = at("s_sb", [P, 2, 2, 3 * P], 11264)
        pT = at("pT", [P, 2, 3 * P], 12800)
        stat = at("stat", [P, 3, 2, 2, 2], 13568)
        rb_row = at("rb_row", [H, NREL], 13632)
        rb_rev = at("rb_rev", [H, REV], 13952)
        xn = at("xn", [P, TT, D], 0)
        xg = at("xg", [P, KT, QS], 0)
        xh = at("xh", [P, TT, D], 2048, F32R)
        xl = at("xl", [P, TT, D], 4096, F32R)
        yh = at("yh", [P, 2, D], 6144, F32R)
        yl = nc.alloc_sbuf_tensor_at("yl", [P, 2, D], F32R, offset=xnT_at)
        pick = at("pick", [P, TT, QUAD, CAP], 10240, F32R)
        pickT = at("pickT", [P, 2, T], 10752, F32R)
        sg = at("sg", [P, 2, F], 11264)
        logT = at("logT", [P, T], 11776)
        hid = at("hid", [P, 2, F], 11776)
        hidT = at("hidT", [P, 2, FT, P], 12288)
        gq = at("gq", [P, TT, QUAD], 12800)
        gslot = at("gslot", [P, 2], 12816)
        disc = at("disc", [ST, 12, P], 13856)
        b_blk = at("b_blk", [P, 2, ST, 2 * GC], 8192)
        c_raw = at("c_raw", [P, 2, KT, 2, NS], 8192)
        b_raw = at("b_raw", [P, 2, ST, GC], 12832)
        b_tmp = at("b_tmp", [P, 2, ST, GC], 13856)
        t_tmp = at("t_tmp", [P, ST * CH // 4], 14880)
        cosT = at("cosT", [P, ST, CH], 8192)
        sinT = at("sinT", [P, ST, CH], 12832)
        yT = at("yT", [P, KT, T], 0)
        decayT = at("decayT", [P, ST, CH], 2048)
        zb = at("zb", [P, 2, 2, 4 * T], 4096)
        qb = at("qb", [P, 2, 4 * T], 10240)
        sig = at("sig", [P, 2, WCOL], 14880)
        yb = at("yb", [P, 2, T], 12288)
        assert arena + 4 * 15392 <= nc.sbuf_usable_end, (arena, nc.sbuf_usable_end)

        def down_banks(r):
            return slice(2, 4) if r else slice(6, 8)

        def glu_bank(u):
            return (6, 7, 0, 1, 2, 3, 6, 7)[u]

        ps = ctx.enter_context(nc.psum_tensor("ps", [P, 8, 512], F32))
        rev_dram = nc.dram_tensor("rev_bias", (H, REV), F32).ap()

        x_loaded, small_loaded = sem("x_loaded"), sem("small_loaded")
        braw_loaded, craw_loaded = sem("braw_loaded"), sem("craw_loaded")
        rb_loaded, rev_ready, rev_stored, bias_loaded = (sem(n) for n in ("rb_loaded", "rev_ready", "rev_stored", "bias_loaded"))
        normw0_loaded, normw_loaded = sem("normw0_loaded"), sem("normw_loaded")
        const_ready, pool_chain = sem("const_ready"), sem("pool_chain")
        dve_chain = sem("dve_chain")
        slot_full = [sem(f"slot_full{s}") for s in range(RING)]
        down_full = [sem(f"down_full{s}") for s in range(RING)]
        slot_free = [sem(f"slot_free{s}") for s in range(RING)]
        ms_ready, rms_ready, xn_ready = sem("ms_ready"), sem("rms_ready"), sem("xn_ready")
        xh_ready, xl_ready = sem("xh_ready"), sem("xl_ready")
        tr_done, tr_evac = sem("tr_done"), sem("tr_evac")
        qkv_done, qkv_evac = sem("qkv_done"), sem("qkv_evac")
        step_ready, step_exp, ang_ready, ang_sin = (sem(n) for n in ("step_ready", "step_exp", "ang_ready", "ang_sin"))
        par_ready, par_turned, c_turned, b_ready, b_turned, par_evac = (
            sem(n) for n in ("par_ready", "par_turned", "c_turned", "b_ready", "b_turned", "par_evac"))
        den_ready, inv_ready, bT_evac = sem("den_ready"), sem("inv_ready"), sem("bT_evac")
        s_done, nmax_ready, exp_done, p_ready, pt_done, pt_evac_a = (
            sem(n) for n in ("s_done", "nmax_ready", "exp_done", "p_ready", "pt_done", "pt_evac_a"))
        o_done, o_evac = sem("o_done"), sem("o_evac")
        proj_done, proj_added = sem("proj_done"), sem("proj_added")
        logit_done, sel_ready, rank_done = (sem(n) for n in ("logit_done", "sel_ready", "rank_done"))
        logit_evac, logits_turned = sem("logit_evac"), sem("logits_turned")
        glog_ready, gexp_done, e2_ready, e2_done = (sem(n) for n in ("glog_ready", "gexp_done", "e2_ready", "e2_done"))
        count_ready = sem("count_ready")
        bu_done, bu_used, q_ready, q_used, y_done, gelu_in, gelu_done = (
            sem(n) for n in ("bu_done", "bu_used", "q_ready", "q_used", "y_done", "gelu_in", "gelu_done"))
        glu_done, sig_done, glu_added = sem("glu_done"), sem("sig_done"), sem("glu_added")
        out_stored = sem("out_stored")
        q4_ready, z_ready, tables_ready = sem("q4_ready"), sem("z_ready"), sem("tables_ready")

        class MoeSems:

            def __init__(self, tag):
                self.pick_ready = sem(f"pick_ready_{tag}")
                self.gath_done = sem(f"gath_done_{tag}")
                self.xg_evac = sem(f"xg_evac_{tag}")
                self.turn_done = sem(f"turn_done_{tag}")
                self.pt_evac = sem(f"pt_evac_{tag}")
                self.gslot_ready = sem(f"gslot_ready_{tag}")
                self.gu_done = sem(f"gu_done_{tag}")
                self.silu_done = sem(f"silu_done_{tag}")
                self.hid_ready = sem(f"hid_ready_{tag}")
                self.hT_done = sem(f"hT_done_{tag}")
                self.hT_evac = sem(f"hT_evac_{tag}")
                self.down_done = sem(f"down_done_{tag}")
                self.yh_done = sem(f"yh_done_{tag}")
                self.yl_done = sem(f"yl_done_{tag}")
                self.comb_done = sem(f"comb_done_{tag}")
                self.x_added = sem(f"x_added_{tag}")
                self.full = None
                self.dfull = None

        main = [MoeSems(f"l{i}") for i in range(2)]
        more = [MoeSems(f"more{i}") for i in range(2)]
        for i in range(2):
            more[i].window = sem(f"window_{i}")
            more[i].ring_passed = sem(f"ring_passed_{i}")
            more[i].full = more[i].dfull = [sem(f"more_full{i}")] * RING
            main[i].full, main[i].dfull = slot_full, down_full

        def full_before(layer):
            return 48 + 16 + layer * (NQ * 32 + 32)

        norms = [a["norm_mix"][0], a["norm_ffn"][0], a["norm_mix"][1], a["norm_ffn"][1], a["norm_final"]]
        block = ctx.enter_context(nc.Block())

        class Chain:

            def __init__(self, eng, s, start=0):
                self.eng, self.s, self.start, self.n = eng, s, start, 0

            def __call__(self, ins):
                self.n += 1
                ins.then_inc(self.s, 1)
                self.eng.wait_ge(self.s, self.start + self.n)

        @block.sync
        def _(sp):
            sp.dma_start(x[:], a["x"][0].rearrange("(t p) d -> p t d", p=P)).then_inc(x_loaded, 16)
            wqkv = a["attn_w_qkv"][0].rearrange("(k p) n -> p k n", p=P)
            wo = a["attn_w_o"][0].rearrange("(k p) n -> p k n", p=P)
            wout = a["ssm_w_out"][0].rearrange("(k p) n -> p k n", p=P)

            def load_qkv(s):
                for i in range(3):
                    sp.dma_start(ring[:, s, :].rearrange("p (i k n) -> p i k n", i=3, k=KT)[:, i],
                                 wqkv[:, :, i * D + s * WCOL:i * D + (s + 1) * WCOL]).then_inc(slot_full[s], 16)

            load_qkv(0)
            sp.wait_ge(rev_stored, 16)
            lo = bass.AP(tensor=rev_dram.tensor, offset=T - P, ap=[[1, P], [REV, H], [1, P]])
            hi = bass.AP(tensor=rev_dram.tensor, offset=0, ap=[[1, P], [REV, H], [1, 2 * P]])
            sp.dma_start(bias[:, :, 0:P], lo).then_inc(bias_loaded, 16)
            sp.dma_start(bias[:, :, P:3 * P], hi).then_inc(bias_loaded, 16)
            for s in range(1, RING):
                load_qkv(s)

            lre = a["ssm_lambda_re"][0].rearrange("(s g) p -> s (g p)", g=2)
            lim = a["ssm_lambda_im"][0].rearrange("(s g) p -> s (g p)", g=2)
            sp.dma_start(lam[:, 0, :], lre).then_inc(small_loaded, 16)
            sp.dma_start(lam[:, 1, :], lim).then_inc(small_loaded, 16)
            sp.dma_start(logstep[:], a["ssm_log_step"][0].rearrange("(s g) -> s g", g=2)).then_inc(small_loaded, 16)
            for layer in range(2):
                wr = router_w[:, layer]
                sp.dma_start(wr[:, :, 0:EG], a["moe_w_group_router"][layer].rearrange("(k p) g -> p k g", p=P))\
                 .then_inc(small_loaded, 16)
                for g in range(EG):
                    sp.dma_start(wr[:, :, EG + g * EPG:EG + (g + 1) * EPG],
                                  a["moe_w_expert_router"][layer, g].rearrange("(k p) e -> p k e", p=P))\
                     .then_inc(small_loaded, 16)
                sp.dma_start(router_b[:, layer, 0:EG],
                              a["moe_b_group_router"][layer].rearrange("(o g) -> o g", o=1).to_broadcast([P, EG]))\
                 .then_inc(small_loaded, 16)
                sp.dma_start(router_b[:, layer, EG:],
                              a["moe_b_expert_router"][layer].rearrange("(o g) e -> o (g e)", o=1).to_broadcast([P, E]))\
                 .then_inc(small_loaded, 16)
            sp.dma_start(dskip[:], a["ssm_d"][0].rearrange("(k p) -> p k", p=P),
                          allow_slow_non_contiguous=True).then_inc(small_loaded, 16)

            n_mat = D * F // P
            wg = a["moe_w_gate"].rearrange("l e (p c) f -> p (l e) (c f)", p=P)
            wu = a["moe_w_up"].rearrange("l e (p c) f -> p (l e) (c f)", p=P)
            wd = a["moe_w_down"].rearrange("l e (p j) d -> p (l e) (j d)", p=P)

            def gate_up(layer, e, s, full):
                for i, w in enumerate((wg, wu)):
                    src = w[:, bass.ds(E * layer + e, 1), :].rearrange("p o n -> p (o n)")
                    sp.dma_start(ring[:, s, i * n_mat:(i + 1) * n_mat], src).then_inc(full[s], 16)

            def down(layer, e, s, full):
                src = wd[:, bass.ds(E * layer + e, 1), :].rearrange("p o n -> p (o n)")
                sp.dma_start(ring[:, s, GU:SLOT], src).then_inc(full[s], 16)

            def experts(layer):
                S = main[layer]
                for s in range(QUAD):
                    sp.wait_ge(slot_free[s], 2 + layer)
                    gate_up(layer, s, s, slot_full)
                with sp.Fori(1, NQ) as it:
                    for s in range(QUAD):
                        sp.wait_ge(S.gu_done, 2 * it - 1 + s // 2)
                        gate_up(layer, QUAD * it + s, s, slot_full)
                    for s in range(QUAD):
                        sp.wait_ge(S.down_done, 2 * it - 1 + s // 2)
                        down(layer, QUAD * it + s, s, down_full)
                sp.wait_ge(count_ready, layer + 1)
                most = sp.value_load(count_i[0:1, layer:layer + 1], min_val=0, max_val=T)
                R = more[layer]
                with sp.If(most > CAP):
                    sp.wait_ge(S.down_done, 2 * NQ)
                    with sp.Fori(0, WINDOWS - 1) as w:
                        with sp.Fori(0, NQ) as it:
                            sp.wait_ge(R.ring_passed, NQ * w + it + 1)
                            for s in range(QUAD):
                                gate_up(layer, QUAD * it + s, s, R.full)
                                down(layer, QUAD * it + s, s, R.dfull)
                    sp.wait_ge(R.down_done, 2 * NQ * (WINDOWS - 1))
                sp.nop()

            for s in range(RING):
                sp.wait_ge(slot_free[s], 1)
                sp.dma_start(ring[:, s, 0:KT * WCOL].rearrange("p (k n) -> p k n", k=KT),
                             wo[:, :, s * WCOL:(s + 1) * WCOL]).then_inc(slot_full[s], 16)
                down(0, s, s, down_full)
            experts(0)
            for s in range(RING):
                sp.wait_ge(main[0].gu_done, 2 * NQ - 1 + s // 2)
                dst = ring[:, s, 0:KT * 2 * WCOL].rearrange("p (k h n) -> p k h n", k=KT, h=2)
                for h in range(2):
                    sp.dma_start(dst[:, :, h, :], wout[:, :, h * D + s * WCOL:h * D + (s + 1) * WCOL])\
                      .then_inc(slot_full[s], 16)
            for s in range(RING):
                sp.wait_ge(main[0].down_done, 2 * NQ - 1 + s // 2)
                down(1, s, s, down_full)
            experts(1)
            for tt in range(TT):
                sp.wait_ge(xn_ready, 2 * 4 + tt + 1)
                sp.dma_start(out[0, tt * P:(tt + 1) * P, :], xn[:, tt, :]).then_inc(out_stored, 16)
            sp.wait_ge(out_stored, 16 * TT)

        @block.gpsimd
        def _(pool):
            pc = Chain(pool, pool_chain)
            def load_normw(i):
                pool.wait_ge(xn_ready, 2 * i)
                pool.dma_start(normw[:], norms[i].rearrange("(o d) -> o d", o=1).to_broadcast([P, D]))\
                    .then_inc(normw_loaded, 16)

            G_ = nc.gpsimd

            def discretise():
                pool.wait_ge(small_loaded, 16 * 18)
                d = disc
                step = d[:, 0, 0:2]
                lr, li, dec = d[:, 3, :], lam[:, 1, :], d[:, 2, :]

                def by_group(ap):
                    return ap.rearrange("s (g p) -> s g p", g=2)

                pc(G_.tensor_scalar(lr, lam[:, 0, :], -1e-4, None, ALU.min))
                pool.wait_ge(step_exp, 1)
                stepb = step.unsqueeze(2).to_broadcast([ST, 2, NS])
                G_.tensor_tensor(by_group(d[:, 1, :]), by_group(lr), stepb, ALU.mult).then_inc(step_ready, 1)
                ang, cyc, t1, t2 = d[:, 4, :], d[:, 5, :], d[:, 10, :], d[:, 11, :]
                pc(G_.tensor_tensor(by_group(ang), by_group(li), stepb, ALU.mult))
                MAGIC = float(1.5 * 2 ** 23)
                c1 = 6.28125
                c2 = float(np.float32(np.round((2 * np.pi - c1) * 2 ** 24) / 2 ** 24))
                c3 = float(2 * np.pi - c1 - c2)
                pc(G_.tensor_scalar(cyc, ang, float(1 / (2 * np.pi)), None, ALU.mult))
                pc(G_.tensor_scalar(t1, cyc, MAGIC, None, ALU.add))
                pc(G_.tensor_scalar(cyc, t1, MAGIC, None, ALU.subtract))
                for part in (c1, c2, c3):
                    pc(G_.tensor_scalar(t1, cyc, part, None, ALU.mult))
                    pc(G_.tensor_tensor(ang, ang, t1, ALU.subtract))
                PI = float(np.nextafter(np.float32(np.pi), np.float32(0)))
                pc(G_.tensor_scalar(d[:, 6, :], ang, -PI, PI, ALU.max, ALU.min))
                pc(G_.tensor_scalar(t2, d[:, 6, :], 0.0, -2.0, ALU.min, ALU.mult))
                pc(G_.tensor_tensor(t1, d[:, 6, :], t2, ALU.add))
                G_.tensor_scalar(d[:, 7, :], t1, -1.0, float(np.pi / 2), ALU.mult, ALU.add).then_inc(ang_ready, 1)
                pool.wait_ge(ang_sin, 1)
                pool.wait_ge(step_exp, 2)
                sin, cos = d[:, 8, :], d[:, 9, :]
                nre, aim, den, inv = d[:, 6, :], d[:, 7, :], d[:, 5, :], d[:, 0, :]
                pc(G_.tensor_tensor(t1, dec, cos, ALU.mult))
                pc(G_.tensor_tensor(aim, dec, sin, ALU.mult))
                pc(G_.tensor_scalar(nre, t1, -1.0, None, ALU.add))
                pc(G_.tensor_tensor(t1, lr, lr, ALU.mult))
                pc(G_.tensor_tensor(t2, li, li, ALU.mult))
                G_.tensor_tensor(den, t1, t2, ALU.add).then_inc(den_ready, 1)
                pool.wait_ge(inv_ready, 1)
                pc(G_.tensor_tensor(t1, nre, lr, ALU.mult))
                pc(G_.tensor_tensor(t2, aim, li, ALU.mult))
                pc(G_.tensor_tensor(t1, t1, t2, ALU.add))
                pc(G_.tensor_tensor(d[:, 4, :], t1, inv, ALU.mult))
                pc(G_.tensor_tensor(t1, aim, lr, ALU.mult))
                pc(G_.tensor_tensor(t2, nre, li, ALU.mult))
                pc(G_.tensor_tensor(t1, t1, t2, ALU.subtract))
                G_.tensor_tensor(d[:, 1, :], t1, inv, ALU.mult).then_inc(par_ready, 1)

            def block_inputs():
                pool.wait_ge(par_evac, 1)
                pool.wait_ge(braw_loaded, 64)
                pc(G_.memset(b_blk[:], 0.0))
                fre = par[:, 0, :].unsqueeze(2).to_broadcast([P, ST, GC])
                fim = par[:, 1, :].unsqueeze(2).to_broadcast([P, ST, GC])
                for r, (fa, fb, op) in enumerate(((fre, fim, ALU.subtract), (fim, fre, ALU.add))):
                    pc(G_.tensor_tensor(b_tmp[:, 0], b_raw[:, 0], fa, ALU.mult))
                    pc(G_.tensor_tensor(b_tmp[:, 1], b_raw[:, 1], fb, ALU.mult))
                    for g2 in range(2):
                        part = slice(NS * g2, NS * (g2 + 1))
                        ins = G_.tensor_tensor(b_blk[part, r, :, GC * g2:GC * (g2 + 1)], b_tmp[part, 0], b_tmp[part, 1], op)
                        if r == 1 and g2 == 1:
                            ins.then_inc(b_ready, 1)
                        else:
                            pc(ins)

            def tables():
                pool.wait_ge(b_ready, 1)
                pool.wait_ge(b_turned, 1)
                wc, ws, u1, u2, u3 = (sc[:, j, :] for j in range(5))
                pc(G_.memset(cosT[:, :, 0:1], 1.0))
                pc(G_.memset(sinT[:, :, 0:1], 0.0))
                pc(G_.tensor_copy(wc, par[:, 3, :]))
                pc(G_.tensor_copy(ws, par[:, 4, :]))
                m = 1
                while m < CH:
                    parts = 2 if 2 * m == CH else 1
                    k = ST // parts
                    for h in range(parts):
                        mine = slice(k * h, k * (h + 1))
                        t = t_tmp[:, 0:k * m].rearrange("p (s m) -> p s m", m=m)
                        wcb = wc[:, mine].unsqueeze(2).to_broadcast([P, k, m])
                        wsb = ws[:, mine].unsqueeze(2).to_broadcast([P, k, m])
                        c0, s0 = cosT[:, mine, 0:m], sinT[:, mine, 0:m]
                        c1, s1 = cosT[:, mine, m:2 * m], sinT[:, mine, m:2 * m]
                        G_.tensor_tensor(c1, c0, wcb, ALU.mult).then_inc(pool_chain, 1)
                        G_.tensor_tensor(s1, s0, wcb, ALU.mult).then_inc(pool_chain, 1)
                        pc.n += 2
                        pc(G_.tensor_tensor(t, s0, wsb, ALU.mult))
                        pc(G_.tensor_tensor(c1, c1, t, ALU.subtract))
                        pc(G_.tensor_tensor(t, c0, wsb, ALU.mult))
                        pc(G_.tensor_tensor(s1, s1, t, ALU.add))
                    pc(G_.tensor_tensor(u1, wc, wc, ALU.mult))
                    pc(G_.tensor_tensor(u2, ws, ws, ALU.mult))
                    pc(G_.tensor_tensor(u3, wc, ws, ALU.mult))
                    pc(G_.tensor_tensor(wc, u1, u2, ALU.subtract))
                    pc(G_.tensor_scalar(ws, u3, 2.0, None, ALU.mult))
                    m *= 2
                G_.tensor_copy(u1, wc).then_inc(tables_ready, 1)
                pool.wait_ge(tables_ready, 1)

            nc.gpsimd.memset(ones[:], 1.0).then_inc(const_ready, 1)
            pc(nc.gpsimd.memset(ident[:], 0.0))
            pc(nc.gpsimd.memset(before[:], 1.0))
            nc.gpsimd.affine_select(out=ident[:], in_=ident[:], compare_op=ALU.not_equal, fill=1.0, base=0,
                                    pattern=[[-1, P]], channel_multiplier=1).then_inc(const_ready, 1)
            nc.gpsimd.affine_select(out=before[:], in_=before[:], compare_op=ALU.is_gt, fill=0.0, base=0,
                                    pattern=[[1, P]], channel_multiplier=-1).then_inc(const_ready, 1)
            nc.gpsimd.iota(slot_iota[:], pattern=[[1, CAP]], base=0, channel_multiplier=0,
                           allow_small_or_imprecise_dtypes=True).then_inc(const_ready, 1)
            nc.gpsimd.iota(rev_e[:], pattern=[[-1, E]], base=E, channel_multiplier=0,
                           allow_small_or_imprecise_dtypes=True).then_inc(const_ready, 1)
            nc.gpsimd.iota(rev_g[:], pattern=[[-1, EG]], base=EG, channel_multiplier=0,
                           allow_small_or_imprecise_dtypes=True).then_inc(const_ready, 1)
            nc.gpsimd.memset(cT[:], 0.0).then_inc(const_ready, 1)
            load_normw(1)
            discretise()
            pool.wait_ge(xn_ready, 2 + 2)
            for r, name in enumerate(("ssm_c_re", "ssm_c_im")):
                for dup in range(2):
                    pool.dma_start(c_raw[:, r, :, dup, :], a[name][0].rearrange("(i g) c p -> (g c) i p", g=P // GC))\
                        .then_inc(craw_loaded, 16)
            for r, name in enumerate(("ssm_b_re", "ssm_b_im")):
                for g2 in range(2):
                    src = a[name][0].rearrange("(s g) p c -> g p s c", g=2)[g2]
                    pool.dma_start(b_raw[NS * g2:NS * (g2 + 1), r], src).then_inc(braw_loaded, 16)
            load_normw(2)
            block_inputs()
            tables()
            for o in range(KT):
                pool.wait_ge(z_ready, o + 1)

                def by_tile(ap):
                    return ap.rearrange("p (k j t) -> p j k t", k=NCH, t=CH)

                co, si = (t[:, 4 * o:4 * o + 4, :].unsqueeze(2).to_broadcast([P, 4, NCH, CH]) for t in (cosT, sinT))
                zr, zi = (by_tile(zb[:, o % 2, r, :]) for r in range(2))
                q0, q1 = qb[:, 0, :], qb[:, 1, :]
                if o:
                    pool.wait_ge(q_used, 2 * o - 1)
                nc.gpsimd.tensor_tensor(by_tile(q0), zr, co, ALU.mult).then_inc(pool_chain, 1)
                pc.n += 1
                if o:
                    pool.wait_ge(q_used, 2 * o)
                pc(nc.gpsimd.tensor_tensor(by_tile(q1), zi, si, ALU.mult))
                nc.gpsimd.tensor_tensor(q0, q0, q1, ALU.subtract).then_inc(q_ready, 1)
                pool.wait_ge(q_ready, 2 * o + 1)
                pc(nc.gpsimd.tensor_tensor(by_tile(q1), zi, co, ALU.mult))
                late = slice(NCH // 2, NCH)
                pc(nc.gpsimd.tensor_tensor(by_tile(q4[:])[:, :, late], zr[:, :, late], si[:, :, late], ALU.mult))
                pool.wait_ge(q4_ready, o + 1)
                nc.gpsimd.tensor_tensor(q1, q1, q4[:], ALU.add).then_inc(q_ready, 1)
            pool.wait_ge(bu_used, 2 * KT)
            pool.wait_ge(z_ready, KT)
            for i in range(3, 5):
                load_normw(i)

        @block.scalar
        def _(act):
            act.dma_start(rb_row[:], a["attn_rel_bias"][0]).then_inc(rb_loaded, 16)
            act.dma_start(normw[:], norms[0].rearrange("(o d) -> o d", o=1).to_broadcast([P, D]))\
               .then_inc(normw0_loaded, 16)
            def norm_root(i):
                act.wait_ge(ms_ready, i + 1)
                nc.scalar.activation(small[:, 2, :], small[:, 1, :], ACT.Sqrt).then_inc(rms_ready, 1)

            def turn_evac(i):
                for g in range(4):
                    act.wait_ge(tr_done, 4 * i + g + 1)
                    tt, half = divmod(g, 2)
                    nc.scalar.copy(xnT[:, 4 * half:4 * half + 4, tt * P:(tt + 1) * P],
                                   ps[:, g % 2, :].rearrange("p (k t) -> p k t", k=4))\
                      .then_inc(tr_evac, 1)

            norm_root(0)
            act.wait_ge(rev_ready, 1)
            act.dma_start(rev_dram, rb_rev[:]).then_inc(rev_stored, 16)
            turn_evac(0)

            def evac_qkv(u):
                s, c = divmod(u, UNITS)
                act.wait_ge(qkv_done, u + 1)
                src = ps[:, u % 3, 0:WCOL]
                dst = qk[:, s % 2, c, :] if c < 4 else v[:, s % 2, c - 4, :]
                if c < HPS:
                    dst = dst.rearrange("p (t q) -> p t q", t=TT)
                    src = src.rearrange("p (t q) -> p t q", t=TT)[:, :, ::-1]
                nc.scalar.copy(dst, src).then_inc(qkv_evac, 1)

            def exps(hp):
                act.wait_ge(nmax_ready, hp + 1)
                for h in range(2):
                    for qt in range(2):
                        w = slice(0, P) if qt == 0 else slice(P, 3 * P)
                        sl = s_sb[:, hp % 2, h, w]
                        nc.scalar.activation(sl, sl, ACT.Exp, bias=stat[:, 0, hp % 2, h, qt:qt + 1],
                                             accum_out=stat[:, 1, hp % 2, h, qt:qt + 1]).then_inc(exp_done, 1)

            def evac_pT(hp):
                act.wait_ge(pt_done, hp + 1)
                nc.scalar.copy(pT[:], ps[:, 5:7, 0:3 * P]).then_inc(pt_evac_a, 1)

            def evac_o(hp):
                act.wait_ge(o_done, hp + 1)
                nc.scalar.copy(oT[:, hp, :].rearrange("p (t q) -> p t q", t=TT),
                               ps[:, 7, 0:T].rearrange("p (t q) -> p t q", t=TT)[:, :, ::-1]).then_inc(o_evac, 1)

            for u in range(UNITS):
                evac_qkv(u)
            for s in range(1, RING + 1):
                u, hp = UNITS * s, HPS * (s - 1)
                more_units = s < RING
                steps = [(evac_qkv, u), (evac_qkv, u + 1), (exps, hp), (evac_qkv, u + 2), (evac_pT, hp),
                         (evac_qkv, u + 3), (evac_o, hp), (exps, hp + 1), (evac_qkv, u + 4), (evac_pT, hp + 1),
                         (evac_qkv, u + 5), (evac_o, hp + 1)]
                for step, arg in steps:
                    if more_units or step is not evac_qkv:
                        step(arg)
                if s == 2:
                    act.wait_ge(small_loaded, 16 * 18)
                    act.wait_ge(rev_stored, 16)
                    nc.scalar.activation(disc[:, 0, 0:2], logstep[:], ACT.Exp).then_inc(step_exp, 1)
                if s == 3:
                    act.wait_ge(step_ready, 1)
                    nc.scalar.activation(disc[:, 2, :], disc[:, 1, :], ACT.Exp).then_inc(step_exp, 1)
            act.wait_ge(ang_ready, 1)
            nc.scalar.activation(disc[:, 8:10, :], disc[:, 6:8, :], ACT.Sin).then_inc(ang_sin, 1)

            def take_gathered(S, n, us):
                for u in us:
                    act.wait_ge(S.gath_done, 4 * n + u + 1)
                    nc.scalar.copy(xg[:, 2 * u:2 * u + 2, :], ps[:, u % 2, :].rearrange("p (c s) -> p c s", c=2))\
                      .then_inc(S.xg_evac, 1)

            def take_turned(S, n):
                act.wait_ge(S.turn_done, n + 1)
                nc.scalar.copy(pickT[:], ps[:, 5, :].rearrange("p (r t) -> p r t", r=2)).then_inc(S.pt_evac, 1)

            def moe_act(S, n, last):
                for r in range(2):
                    act.wait_ge(S.gu_done, 2 * n + r + 1)
                    nc.scalar.activation(sg[:, r, :], ps[:, 2 + r, 0:F], ACT.Silu).then_inc(S.silu_done, 1)
                for r in range(2):
                    act.wait_ge(S.hT_done, 2 * n + r + 1)
                    nc.scalar.copy(hidT[:, r], ps[:, 4 + r, 0:F].rearrange("p (j s) -> p j s", j=FT)).then_inc(S.hT_evac, 1)
                    if r == 0 and not last:
                        take_gathered(S, n + 1, (0, 1))
                for r in range(2):
                    act.wait_ge(S.down_done, 2 * n + r + 1)
                    act.wait_ge(S.gslot_ready, 2 * n + 2)
                    nc.scalar.activation(yh[:, r, :].rearrange("p (b n) -> p b n", b=2), ps[:, down_banks(r), :], ACT.Copy,
                                         scale=gslot[:, r:r + 1]).then_inc(S.yh_done, 1)
                    if r == 0 and not last:
                        take_gathered(S, n + 1, (2, 3))
                act.wait_ge(S.comb_done, 4 * n + 4)
                if not last:
                    take_turned(S, n + 1)

            def moe_start(S, n):
                take_gathered(S, n, range(4))
                take_turned(S, n)

            def layer_moe(layer):
                i = 2 * layer + 1
                norm_root(i)
                turn_evac(i)
                for tt in range(TT):
                    act.wait_ge(xn_ready, 2 * i + tt + 1)
                    nc.scalar.copy(xh[:, tt, :], xn[:, tt, :]).then_inc(xh_ready, 1)
                act.wait_ge(logit_done, layer + 1)
                nc.scalar.copy(logT[0:NR, :], ps[0:NR, 2, 0:T]).then_inc(logit_evac, 1)
                act.wait_ge(glog_ready, layer + 1)
                nc.scalar.activation(gexp[:], gexp[:], ACT.Exp).then_inc(gexp_done, 1)
                act.wait_ge(e2_ready, layer + 1)
                nc.scalar.activation(small[:, 9, :], small[:, 8, :], ACT.Exp).then_inc(e2_done, 1)
                moe_start(main[layer], 0)
                with act.Fori(0, NQ - 1) as it:
                    moe_act(main[layer], it, False)
                moe_act(main[layer], NQ - 1, True)
                act.wait_ge(count_ready, layer + 1)
                most = act.value_load(count_i[0:1, layer:layer + 1], min_val=0, max_val=T)
                with act.If(most > CAP):
                    with act.Fori(0, WINDOWS - 1) as w:
                        moe_start(more[layer], w * NQ)
                        with act.Fori(0, NQ - 1) as it:
                            moe_act(more[layer], w * NQ + it, False)
                        moe_act(more[layer], w * NQ + NQ - 1, True)
                act.nop()

            layer_moe(0)
            norm_root(2)
            turn_evac(2)
            def gelu(o):
                act.wait_ge(gelu_in, o + 1)
                nc.scalar.activation(yT[:, o, :], yb[:, o % 2, :], ACT.Gelu_apprx_tanh).then_inc(gelu_done, 1)

            def gate(u):
                act.wait_ge(glu_done, u + 1)
                if u >= 2:
                    act.wait_ge(glu_added, u - 1)
                nc.scalar.activation(sig[:, u % 2, :], ps[:, glu_bank(u), WCOL:2 * WCOL], ACT.Sigmoid).then_inc(sig_done, 1)

            for o in range(KT):
                gelu(o)
            for u in range(2 * RING):
                gate(u)
            layer_moe(1)
            norm_root(4)

        @block.vector
        def _(dve):
            lk = Chain(dve, dve_chain)
            V = nc.vector

            def squares(tt):
                lk(V.tensor_tensor_reduce(out=q4[:], in0=x[:, tt, :], in1=x[:, tt, :], scale=1.0, scalar=0.0,
                                          op0=ALU.mult, op1=ALU.add, accum_out=small[:, 0, tt:tt + 1]))

            def norm(i, first=0, between=None):
                ss, ms, rt, r0, t0, t1, rs = (small[:, j, :] for j in (0, 1, 2, 3, 4, 5, 6))
                for tt in range(first, TT):
                    squares(tt)
                V.tensor_scalar(ms, ss, 1.0 / D, EPS, ALU.mult, ALU.add).then_inc(ms_ready, 1)
                if between:
                    between()
                dve.wait_ge(rms_ready, i + 1)
                lk(V.reciprocal(r0, rt))
                lk(V.tensor_tensor(t0, r0, r0, ALU.mult))
                lk(V.tensor_tensor(t1, t0, ms, ALU.mult))
                lk(V.tensor_scalar(t0, t1, -0.5, 1.5, ALU.mult, ALU.add))
                lk(V.tensor_tensor(rs, r0, t0, ALU.mult))
                if i:
                    dve.wait_ge(normw_loaded, 16 * i)
                else:
                    dve.wait_ge(normw0_loaded, 16)
                for tt in range(TT):
                    V.scalar_tensor_tensor(out=xn[:, tt, :], in0=x[:, tt, :], scalar=rs[:, tt:tt + 1], in1=normw[:],
                                           op0=ALU.mult, op1=ALU.mult).then_inc(xn_ready, 1)

            def reverse_bias():
                dve.wait_ge(rb_loaded, 16)
                far = REV - 2 * MAXREL
                lk(V.tensor_copy(rb_rev[:, far:], rb_row[:, NREL - 1:0:-1]))
                V.tensor_copy(rb_rev[:, 0:far], rb_row[:, NREL - 1:NREL].to_broadcast([H, far])).then_inc(rev_ready, 1)

            dve.wait_ge(x_loaded, 16)
            norm(0, between=reverse_bias)

            dve.wait_ge(bias_loaded, 32)
            for col in (P - CH, 3 * P - CH):
                lk(V.memset(bias[P - CH:P, :, col:col + CH], NEG))

            def att_norm(hp):
                b = hp % 2
                dve.wait_ge(exp_done, 4 * hp + 4)
                lk(V.reciprocal(stat[:, 2, b], stat[:, 1, b]))
                for qt, w in ((0, slice(0, P)), (1, slice(P, 3 * P))):
                    n = w.stop - w.start
                    V.tensor_tensor(s_sb[:, b, :, w], s_sb[:, b, :, w],
                                    stat[:, 2, b, :, qt:qt + 1].to_broadcast([P, 2, n]), ALU.mult).then_inc(p_ready, 1)

            def att_max(hp):
                b = hp % 2
                dve.wait_ge(s_done, hp + 1)
                if hp >= 2:
                    dve.wait_ge(pt_done, hp - 1)
                lk(V.scalar_tensor_tensor(out=s_sb[:, b], in0=ps[:, 3:5, 0:3 * P], scalar=HD ** -0.5,
                                          in1=bias[:, 2 * hp:2 * hp + 2, :], op0=ALU.mult, op1=ALU.add))
                lk(V.tensor_reduce(stat[:, 0, b, :, 0:1], s_sb[:, b, :, 0:P], AX.X, ALU.max, negate=True))
                V.tensor_reduce(stat[:, 0, b, :, 1:2], s_sb[:, b, :, P:3 * P], AX.X, ALU.max, negate=True)\
                 .then_inc(nmax_ready, 1)

            for hp in range(0, HP, HPS):
                att_max(hp)
                att_max(hp + 1)
                att_norm(hp)
                att_norm(hp + 1)

            for u in range(2 * RING):
                s, tt = divmod(u, 2)
                dve.wait_ge(proj_done, u + 1)
                xs = x[:, tt, s * WCOL:(s + 1) * WCOL]
                V.tensor_tensor(xs, xs, ps[:, u % 7, 0:WCOL], ALU.add).then_inc(proj_added, 1)
                if u == 2 * RING - 2:
                    dve.wait_ge(proj_added, u + 1)
                    squares(0)
            dve.wait_ge(proj_added, 2 * RING)
            dve.wait_ge(den_ready, 1)
            V.reciprocal(disc[:, 0, :], disc[:, 5, :]).then_inc(inv_ready, 1)

            def routing(layer):
                def bc(ap, n):
                    return ap.unsqueeze(2).to_broadcast([P, TT, n])

                r0, r1, r2, r3, r4, r5 = (route[:, j] for j in range(6))
                v0, v1, v2, v3 = (small[:, j, :] for j in (7, 8, 9, 10))
                m1 = small[:, 11, :]
                gl, el = glog[:, :, 0:EG], glog[:, :, EG:]
                for tt in range(TT):
                    dve.wait_ge(xh_ready, 2 * layer + tt + 1)
                    V.tensor_tensor(xl[:, tt, :], xn[:, tt, :], xh[:, tt, :].bitcast(F32), ALU.subtract).then_inc(xl_ready, 1)
                dve.wait_ge(logits_turned, layer + 1)
                lk(V.tensor_tensor(glog[:], ps[:, 4, 0:TT * NR].rearrange("p (t n) -> p t n", t=TT),
                                   router_b[:, layer].unsqueeze(1).to_broadcast([P, TT, NR]), ALU.add))
                lk(V.tensor_reduce(v0.unsqueeze(2), gl, AX.X, ALU.max))
                V.tensor_tensor(gexp[:], gl, bc(v0, EG), ALU.subtract).then_inc(glog_ready, 1)
                lk(V.tensor_tensor(r2[:, :, 0:EG], gl, bc(v0, EG), ALU.is_equal))
                lk(V.tensor_tensor(r3[:, :, 0:EG], r2[:, :, 0:EG], rev_g[:].unsqueeze(1).to_broadcast([P, TT, EG]), ALU.mult))
                lk(V.tensor_reduce(v1.unsqueeze(2), r3[:, :, 0:EG], AX.X, ALU.max))
                lk(V.tensor_tensor(r2[:, :, 0:EG], rev_g[:].unsqueeze(1).to_broadcast([P, TT, EG]), bc(v1, EG), ALU.is_equal))
                lk(V.tensor_scalar(r3[:, :, 0:EG], r2[:, :, 0:EG], 3e38, NEG, ALU.mult, ALU.add))
                lk(V.tensor_tensor(r4.rearrange("p t (g e) -> p t g e", g=EG), el.rearrange("p t (g e) -> p t g e", g=EG),
                                   r3[:, :, 0:EG].unsqueeze(3).to_broadcast([P, TT, EG, EPG]), ALU.min))
                reve = rev_e[:].unsqueeze(1).to_broadcast([P, TT, E])

                def first_max(src, top, hot):
                    lk(V.tensor_reduce(top.unsqueeze(2), src, AX.X, ALU.max))
                    lk(V.tensor_tensor(r3, src, bc(top, E), ALU.is_equal))
                    lk(V.tensor_tensor(r1, r3, reve, ALU.mult))
                    lk(V.tensor_reduce(v0.unsqueeze(2), r1, AX.X, ALU.max))
                    lk(V.tensor_tensor(hot, reve, bc(v0, E), ALU.is_equal))

                first_max(r4, m1, r5)
                lk(V.scalar_tensor_tensor(out=r0, in0=r5, scalar=2.0 * NEG, in1=r4, op0=ALU.mult, op1=ALU.add))
                first_max(r0, v2, r2)
                V.tensor_tensor(v1, v2, m1, ALU.subtract).then_inc(e2_ready, 1)
                V.tensor_tensor(sel[:], r5, r2, ALU.add).then_inc(sel_ready, 1)
                dve.wait_ge(gexp_done, layer + 1)
                lk(V.tensor_reduce(v3.unsqueeze(2), gexp[:], AX.X, ALU.add))
                lk(V.reciprocal(v3, v3))
                dve.wait_ge(e2_done, layer + 1)
                lk(V.tensor_scalar(v0, v2, 1.0, None, ALU.add))
                lk(V.reciprocal(m1, v0))
                lk(V.tensor_tensor(v0, m1, v3, ALU.mult))
                lk(V.tensor_tensor(v1, v0, v2, ALU.mult))
                lk(V.tensor_tensor(r0, r5, bc(v0, E), ALU.mult))
                lk(V.tensor_tensor(r1, r2, bc(v1, E), ALU.mult))
                lk(V.tensor_tensor(gates[:], r0, r1, ALU.add))
                dve.wait_ge(rank_done, layer + 1)
                lk(V.scalar_tensor_tensor(out=r1, in0=ps[:, 3, 0:TT * E].rearrange("p (t e) -> p t e", t=TT), scalar=1.0,
                                          in1=sel[:], op0=ALU.add, op1=ALU.mult))
                lk(V.tensor_scalar(rank[:], r1, -1.0, None, ALU.add))

            def make_pick(S, n, it):
                V.tensor_copy(gq[:], gates[:, :, bass.ds(QUAD * it, QUAD)]).then_inc(S.pick_ready, 1)
                for tt in range(TT):
                    rk = rank[:, tt, bass.ds(QUAD * it, QUAD)].unsqueeze(2).to_broadcast([P, QUAD, CAP])
                    V.tensor_tensor(pick[:, tt], slot_iota[:].unsqueeze(1).to_broadcast([P, QUAD, CAP]), rk,
                                    ALU.is_equal).then_inc(S.pick_ready, 1)

            def take_gslot(S, n):
                dve.wait_ge(S.turn_done, n + 1)
                for h in range(2):
                    part = slice(CAP * h, CAP * (h + 1))
                    V.tensor_copy(gslot[part, :], ps[part, 4, 256 + h:256 + h + 7:6]).then_inc(S.gslot_ready, 1)

            def moe_dve(S, n, it, last):
                if not last:
                    make_pick(S, n + 1, it + 1)
                for r in range(2):
                    dve.wait_ge(S.silu_done, 2 * n + r + 1)
                    V.tensor_tensor(hid[:, r, :], sg[:, r, :], ps[:, 2 + r, F:2 * F], ALU.mult).then_inc(S.hid_ready, 1)
                dve.wait_ge(S.gslot_ready, 2 * n + 2)
                for r in range(2):
                    dve.wait_ge(S.yh_done, 2 * n + r + 1)
                    V.scalar_tensor_tensor(out=yl[:, r, :].rearrange("p (b n) -> p b n", b=2), in0=ps[:, down_banks(r), :],
                                           scalar=gslot[:, r:r + 1],
                                           in1=yh[:, r, :].bitcast(F32).rearrange("p (b n) -> p b n", b=2),
                                           op0=ALU.mult, op1=ALU.subtract).then_inc(S.yl_done, 1)
                dve.wait_ge(S.yl_done, 2 * n + 2)
                if not last:
                    take_gslot(S, n + 1)
                for u in range(4):
                    tt, h = divmod(u, 2)
                    dve.wait_ge(S.comb_done, 4 * n + u + 1)
                    xs = x[:, tt, 512 * h:512 * (h + 1)]
                    V.tensor_tensor(xs, xs, ps[:, (0, 1, 6, 7)[u], :], ALU.add).then_inc(S.x_added, 1)
                dve.wait_ge(S.x_added, 4 * n + 8)

            def take_constants():
                dve.wait_ge(c_turned, 1)
                for r in range(2):
                    for half in range(2):
                        for g2 in range(2):
                            part = slice(NS * g2, NS * (g2 + 1))
                            src = ps[part, 2 * r + half, :].rearrange("p (s g c) -> p s g c", g=2, c=GC)[:, :, g2, :]
                            rows = slice(16 * half, 16 * (half + 1))
                            cols = slice(GC * g2, GC * (g2 + 1))
                            if r == 0:
                                lk(V.tensor_copy(cT[part, 0, rows, cols], src))
                            else:
                                lk(V.tensor_scalar(cT[part, 1, rows, cols], src, -1.0, None, ALU.mult))
                dve.wait_ge(par_turned, 1)
                V.tensor_copy(par[:], ps[:, 6, 0:5 * ST].rearrange("p (j s) -> p j s", j=5)).then_inc(par_evac, 1)

            def layer_moe(layer):
                i = 2 * layer + 1
                norm(i, first=1)
                routing(layer)
                S = main[layer]
                dve.sem_inc(S.x_added, 4)
                make_pick(S, 0, 0)
                lk(V.tensor_reduce(route[:, 0, 0, 0:1], ps[:, 3, TT * E:(TT + 1) * E], AX.X, ALU.max))
                V.tensor_copy(count_i[:, layer:layer + 1], route[:, 0, 0, 0:1]).then_inc(count_ready, 1)
                dve.wait_ge(count_ready, layer + 1)
                take_gslot(S, 0)
                if layer == 0:
                    with dve.Fori(0, TURNS[0]) as it:
                        moe_dve(S, it, it, False)
                    take_constants()
                    with dve.Fori(TURNS[0], TURNS[1]) as it:
                        moe_dve(S, it, it, False)
                    dve.wait_ge(b_turned, 1)
                    V.tensor_copy(bT[:], ps[:, 0:4, :].rearrange("p (r h) (i q) -> p r (h i) q", r=2, q=P))\
                     .then_inc(bT_evac, 1)
                    with dve.Fori(TURNS[1], NQ - 1) as it:
                        moe_dve(S, it, it, False)
                else:
                    with dve.Fori(0, NQ - 1) as it:
                        moe_dve(S, it, it, False)
                moe_dve(S, NQ - 1, NQ - 1, True)
                most = dve.value_load(count_i[0:1, layer:layer + 1], min_val=0, max_val=T)
                with dve.If(most > CAP):
                    dve.sem_inc(more[layer].x_added, 4)
                    with dve.Fori(0, WINDOWS - 1) as w:
                        V.tensor_scalar(rank[:], rank[:], float(CAP), None, ALU.subtract)\
                         .then_inc(more[layer].window, 1)
                        dve.wait_ge(more[layer].window, w + 1)
                        make_pick(more[layer], w * NQ, 0)
                        take_gslot(more[layer], w * NQ)
                        with dve.Fori(0, NQ - 1) as it:
                            moe_dve(more[layer], w * NQ + it, it, False)
                        moe_dve(more[layer], w * NQ + NQ - 1, NQ - 1, True)
                dve.nop()

            layer_moe(0)

            norm(2)
            dec_s = par[:, 2, :]
            wc, ws = sc[:, 0, :], sc[:, 1, :]
            lk(V.tensor_copy(decayT[:], dec_s.unsqueeze(2).to_broadcast([P, ST, CH])))
            lk(V.memset(decayT[:, :, 0:1], 0.0))
            dve.wait_ge(tables_ready, 1)
            wre, wsg = sc[:, 6, :], sc[:, 7:9, :]
            lk(V.tensor_tensor(wre, wc, dec_s, ALU.mult))
            lk(V.tensor_tensor(wsg[:, 1, :], ws, dec_s, ALU.mult))
            lk(V.tensor_scalar(wsg[:, 0, :], wsg[:, 1, :], -1.0, None, ALU.mult))
            tmp = normw

            def by_tile(ap):
                return ap.rearrange("p (k j t) -> p j k t", k=NCH, t=CH)

            def fourth(o):
                if o:
                    dve.wait_ge(q_ready, 2 * o)
                si = sinT[:, 4 * o:4 * o + 4, :].unsqueeze(2).to_broadcast([P, 4, NCH, CH])
                early = slice(0, NCH // 2)
                V.tensor_tensor(by_tile(q4[:])[:, :, early], by_tile(zb[:, o % 2, 0, :])[:, :, early], si[:, :, early],
                                ALU.mult).then_inc(q4_ready, 1)
                dve.wait_ge(q4_ready, o + 1)

            def step(o):
                mine = slice(4 * o, 4 * o + 4)
                zr, zi = zb[:, o % 2, 0, :], zb[:, o % 2, 1, :]

                if o >= 2:
                    dve.wait_ge(q_ready, 2 * (o - 1))
                for h in range(2):
                    dve.wait_ge(bu_done, 2 * o + h + 1)
                    bre, bim = (ps[:, 2 * h:2 * h + 2, T * r:T * (r + 1)].rearrange("p j (k t) -> p j k t", t=CH)
                                for r in range(2))
                    two = slice(4 * o + 2 * h, 4 * o + 2 * h + 2)
                    co, si = (t[:, two, :].unsqueeze(2).to_broadcast([P, 2, NCH, CH]) for t in (cosT, sinT))
                    zrh, zih = (by_tile(part)[:, 2 * h:2 * h + 2] for part in (zr, zi))
                    ta, tc = (tmp[:, 2 * T * i:2 * T * (i + 1)].rearrange("p (j k t) -> p j k t", j=2, t=CH) for i in range(2))
                    V.tensor_tensor(zrh, bre, co, ALU.mult)
                    V.tensor_tensor(ta, bim, si, ALU.mult)
                    V.tensor_tensor(zih, bim, co, ALU.mult)
                    V.tensor_tensor(tc, bre, si, ALU.mult).then_inc(bu_used, 1)
                    dve.wait_ge(bu_used, 2 * o + h + 1)
                    V.tensor_tensor(zrh, zrh, ta, ALU.add)
                    lk(V.tensor_tensor(zih, zih, tc, ALU.subtract))
                if o:
                    fourth(o - 1)
                if o >= 2:
                    finish(o - 2)
                dq = decayT[:, mine, :].rearrange("p j t -> p (j t)")
                z = zb[:, o % 2].rearrange("p r (k j t) -> p r k j t", k=NCH, t=CH)
                n = 4 * CH
                for k in range(NCH):
                    for r, part in enumerate((zr, zi)):
                        part = part[:, n * k:n * (k + 1)]
                        ins = V.tensor_tensor_scan(part, dq, part, 0.0, ALU.mult, ALU.add)
                        ins.then_inc(z_ready if (k == NCH - 1 and r) else dve_chain, 1)
                        if not (k == NCH - 1 and r):
                            lk.n += 1
                    if k < NCH - 1:
                        dve.wait_ge(dve_chain, lk.n)
                        last, swapped, head = z[:, :, k, :, CH - 1], z[:, ::-1, k, :, CH - 1], z[:, :, k + 1, :, 0]
                        c1, c2 = sc[:, 10:12, 0:4], sc[:, 12:14, 0:4]
                        V.tensor_tensor(c1, last, wre[:, mine].unsqueeze(1).to_broadcast([P, 2, 4]), ALU.mult)
                        lk(V.tensor_tensor(c2, swapped, wsg[:, :, mine], ALU.mult))
                        lk(V.tensor_tensor(c1, c1, c2, ALU.add))
                        lk(V.tensor_tensor(head, head, c1, ALU.add))

            def finish(o):
                dve.wait_ge(y_done, o + 1)
                if o >= 2:
                    dve.wait_ge(gelu_done, o - 1)
                V.scalar_tensor_tensor(out=yb[:, o % 2, :], in0=xnT[:, o, :], scalar=dskip[:, o:o + 1],
                                       in1=ps[:, 4 + o % 2, 0:T], op0=ALU.mult, op1=ALU.add).then_inc(gelu_in, 1)

            def glu(u):
                s, tt = divmod(u, TT)
                dve.wait_ge(sig_done, u + 1)
                xs = x[:, tt, s * WCOL:(s + 1) * WCOL]
                lk(V.tensor_tensor(sig[:, u % 2, :], sig[:, u % 2, :], ps[:, glu_bank(u), 0:WCOL], ALU.mult))
                V.tensor_tensor(xs, xs, sig[:, u % 2, :], ALU.add).then_inc(glu_added, 1)

            for o in range(KT):
                step(o)
            dve.wait_ge(dve_chain, lk.n)
            fourth(KT - 1)
            finish(KT - 2)
            finish(KT - 1)
            for u in range(2 * RING):
                glu(u)
                if u == 2 * RING - 2:
                    dve.wait_ge(glu_added, u + 1)
                    squares(0)
            dve.wait_ge(glu_added, 2 * RING)
            layer_moe(1)
            norm(4)

        @block.tensor
        def _(pe):
            mm = nc.tensor.matmul

            def turn(i):
                for g in range(4):
                    tt, half = divmod(g, 2)
                    pe.wait_ge(xn_ready, 2 * i + tt + 1)
                    if g >= 2:
                        pe.wait_ge(tr_evac, 4 * i + g - 1)
                    for k in range(4):
                        kt = 4 * half + k
                        ins = nc.tensor.transpose(ps[:, g % 2, k * P:(k + 1) * P],
                                                  xn[:, tt, kt * P:(kt + 1) * P], ident[:])
                    ins.then_inc(tr_done, 1)
                pe.wait_ge(tr_evac, 4 * i + 4)

            def keep_warm(bank, n):
                for _ in range(n):
                    mm(ps[:, bank, :], ones[:], ident[:].unsqueeze(1).to_broadcast([P, 4, P]), start=True, stop=True)

            pe.wait_ge(const_ready, 7)
            keep_warm(7, WARM["start"])
            turn(0)

            def qkv(u):
                s, c = divmod(u, UNITS)
                if u >= 3:
                    pe.wait_ge(qkv_evac, u - 2)
                if c == 0:
                    pe.wait_ge(slot_full[s], 48)
                w = ring[:, s, :].rearrange("p (i k n) -> p i k n", i=3, k=KT)
                for kt in range(KT):
                    if c < 4:
                        ins = mm(ps[:, u % 3, 0:T], w[:, c // HPS, kt, (c % HPS) * P:(c % HPS + 1) * P], xnT[:, kt, :],
                                 start=(kt == 0), stop=(kt == KT - 1))
                    else:
                        ins = mm(ps[:, u % 3, 0:WCOL], xnT[:, kt, (c - 4) * P:(c - 3) * P], w[:, 2, kt, :],
                                 start=(kt == 0), stop=(kt == KT - 1))
                ins.then_inc(qkv_done, 1)
                if c == UNITS - 1:
                    pe.wait_ge(qkv_done, u + 1)
                    pe.sem_inc(slot_free[s], 1)

            def scores(hp):
                if hp:
                    pe.wait_ge(nmax_ready, hp)
                pe.wait_ge(qkv_evac, UNITS * (hp // HPS) + 4)
                for h in range(2):
                    rows = slice(HD * h, HD * (h + 1))
                    par_s, pair = (hp // HPS) % 2, hp % HPS
                    q, kk = qk[rows, par_s, pair, :], qk[rows, par_s, HPS + pair, :]
                    mm(ps[:, 3 + h, 0:P], q[:, 0:P], kk[:, 0:P], start=True, stop=True)
                    ins = mm(ps[:, 3 + h, P:3 * P], q[:, P:T], kk[:, 0:T], start=True, stop=True)
                ins.then_inc(s_done, 1)

            def turn_p(hp):
                pe.wait_ge(p_ready, 2 * hp + 2)
                if hp:
                    pe.wait_ge(pt_evac_a, hp)
                for h in range(2):
                    for j in range(3):
                        ins = nc.tensor.transpose(ps[:, 5 + h, j * P:(j + 1) * P],
                                                  s_sb[:, hp % 2, h, j * P:(j + 1) * P], ident[:])
                ins.then_inc(pt_done, 1)

            def mix(hp):
                pe.wait_ge(qkv_evac, UNITS * (hp // HPS) + UNITS)
                pe.wait_ge(pt_evac_a, hp + 1)
                if hp:
                    pe.wait_ge(o_evac, hp)
                for h in range(2):
                    rows = slice(HD * h, HD * (h + 1))
                    vv = v[:, (hp // HPS) % 2]
                    cols = slice(HD * (2 * (hp % HPS) + h), HD * (2 * (hp % HPS) + h + 1))
                    mm(ps[rows, 7, 0:P], vv[:, 0, cols], pT[:, h, 0:P], start=True, stop=True)
                    mm(ps[rows, 7, P:T], vv[:, 0, cols], pT[:, h, P:2 * P], start=True, stop=False)
                    ins = mm(ps[rows, 7, P:T], vv[:, 1, cols], pT[:, h, 2 * P:3 * P], start=False, stop=True)
                ins.then_inc(o_done, 1)

            def project(u, kts):
                s, tt = divmod(u, TT)
                if kts[0] == 0:
                    pe.wait_ge(slot_full[s], 64)
                    if u < 3:
                        pe.wait_ge(qkv_evac, UNITS * RING)
                        pe.wait_ge(o_evac, 3)
                    elif u < 5:
                        pe.wait_ge(nmax_ready, HP)
                    elif u < 7:
                        pe.wait_ge(pt_evac_a, HP)
                    else:
                        pe.wait_ge(proj_added, 1)
                elif kts[0] == 3:
                    pe.wait_ge(o_evac, 6)
                w = ring[:, s, 0:KT * WCOL].rearrange("p (k n) -> p k n", k=KT)
                for kt in kts:
                    ins = mm(ps[:, u % 7, 0:WCOL], oT[:, kt, tt * P:(tt + 1) * P], w[:, kt, :],
                             start=(kt == 0), stop=(kt == KT - 1))
                if kts[-1] == KT - 1:
                    ins.then_inc(proj_done, 1)
                    if tt == 1:
                        pe.wait_ge(proj_done, u + 1)
                        pe.sem_inc(slot_free[s], 1)

            for u in range(UNITS - 1):
                qkv(u)
            scores(0)
            qkv(UNITS - 1)
            for s in range(1, RING + 1):
                u, hp = UNITS * s, HPS * (s - 1)
                steps = [(qkv, u), (qkv, u + 1), (scores, hp + 1), (qkv, u + 2), (turn_p, hp),
                         (qkv, u + 3), (mix, hp), (qkv, u + 4), (turn_p, hp + 1), (scores, hp + 2),
                         (qkv, u + 5), (mix, hp + 1)]
                for step, arg in steps:
                    if step is qkv and s == RING:
                        part, unit_o = divmod(arg - u, 3)
                        project(unit_o, range(3 * part, 3 * part + 3))
                    elif step is not scores or arg < HP:
                        if s == RING and arg == HP - 1 and step in (turn_p, mix):
                            project(3 if step is turn_p else 4, range(6))
                        step(arg)

            pe.wait_ge(o_evac, HP)
            for u in range(2 * RING):
                project(u, range(6 if u < 5 else 0, KT))

            def router(layer):
                pe.wait_ge(small_loaded, 16 * 18)
                for kt in range(KT):
                    ins = mm(ps[0:NR, 2, 0:T], router_w[:, layer, kt, :], xnT[:, kt, :], start=(kt == 0), stop=(kt == KT - 1))
                ins.then_inc(logit_done, 1)
                pe.wait_ge(logit_evac, layer + 1)
                for tt in range(TT):
                    ins = nc.tensor.transpose(ps[:, 4, tt * NR:(tt + 1) * NR], logT[0:NR, tt * P:(tt + 1) * P],
                                              ident[0:NR, 0:NR])
                ins.then_inc(logits_turned, 1)
                keep_warm(5, WARM["choice"])
                pe.wait_ge(sel_ready, layer + 1)
                mm(ps[:, 3, 0:E], before[:], sel[:, 0, :], start=True, stop=True)
                mm(ps[:, 3, E:2 * E], before[:], sel[:, 1, :], start=True, stop=False)
                mm(ps[:, 3, E:2 * E], ones[:], sel[:, 0, :], start=False, stop=True)
                mm(ps[:, 3, 2 * E:3 * E], ones[:], sel[:, 0, :], start=True, stop=False)
                mm(ps[:, 3, 2 * E:3 * E], ones[:], sel[:, 1, :], start=False, stop=True).then_inc(rank_done, 1)
                keep_warm(5, WARM["ranks"])

            def gather(S, n, us):
                xs = [t[:].rearrange("p t (q c) -> p t q c", c=KT) for t in (xh, xl)]
                for u in us:
                    if u >= 2:
                        pe.wait_ge(S.xg_evac, 4 * n + u - 1)
                    for c in range(2):
                        for i in range(2 * TT):
                            part, tt = divmod(i, TT)
                            ins = mm(ps[:, u % 2, c * QS:(c + 1) * QS], xs[part][:, tt, :, 2 * u + c],
                                     pick[:, tt].rearrange("p e s -> p (e s)"), start=(i == 0), stop=(i == 2 * TT - 1))
                    ins.then_inc(S.gath_done, 1)

            def turn_pick(S, n):
                for r in range(2):
                    for tt in range(TT):
                        nc.tensor.transpose(ps[:, 5, (2 * r + tt) * P:(2 * r + tt + 1) * P],
                                            pick[:, tt, 2 * r:2 * r + 2].rearrange("p e s -> p (e s)").bitcast(F32), ident[:])
                for r in range(2):
                    for tt in range(TT):
                        ins = mm(ps[:, 4, 256 + QUAD * r:256 + QUAD * (r + 1)],
                                 pick[:, tt, 2 * r:2 * r + 2].rearrange("p e s -> p (e s)").bitcast(F32), gq[:, tt, :],
                                 start=(tt == 0), stop=(tt == TT - 1))
                ins.then_inc(S.turn_done, 1)

            def moe_start(S, n):
                pe.wait_ge(S.pick_ready, 3 * n + 3)
                pe.wait_ge(S.x_added, 4 * n + 4)
                gather(S, n, range(4))
                turn_pick(S, n)

            def moe_pe(S, n, start, dstart, per, dper, last):
                pe.wait_ge(S.xg_evac, 4 * n + 4)
                for r in range(2):
                    for h in range(2):
                        pe.wait_ge(S.full[2 * r + h], start + per * (n + 1))
                    for c in range(KT):
                        for h in range(2):
                            s = 2 * r + h
                            w = ring[:, s, 0:GU].rearrange("p (u c f) -> p u c f", u=2, c=KT)[:, :, c, :]
                            ins = mm(ps[CAP * h:CAP * (h + 1), 2 + r, :], xg[:, c, CAP * s:CAP * (s + 1)], w,
                                     start=(c == 0), stop=(c == KT - 1))
                    ins.then_inc(S.gu_done, 1)
                    if r == 0:
                        pe.wait_ge(S.gslot_ready, 2 * n + 2)
                    if last and r == 0:
                        keep_warm(4, WARM["last loads"])

                def turn_hidden(r):
                    pe.wait_ge(S.hid_ready, 2 * n + r + 1)
                    for j in range(FT):
                        ins = nc.tensor.transpose(ps[:, 4 + r, j * P:(j + 1) * P], hid[:, r, j:F:FT], ident[:])
                    ins.then_inc(S.hT_done, 1)

                def down_product(r):
                    pe.wait_ge(S.hT_evac, 2 * n + r + 1)
                    for h in range(2):
                        pe.wait_ge(S.dfull[2 * r + h], dstart + dper * (n + 1))
                    for j in range(FT):
                        for b in range(2):
                            for h in range(2):
                                s = 2 * r + h
                                w = ring[:, s, GU:SLOT].rearrange("p (j d) -> p j d", j=FT)[:, j, 512 * b:512 * (b + 1)]
                                ins = mm(ps[CAP * h:CAP * (h + 1), down_banks(r).start + b, :], hidT[:, r, j, CAP * h:CAP * (h + 1)], w,
                                         start=(j == 0), stop=(j == FT - 1))
                    ins.then_inc(S.down_done, 1)

                def combine(us, parts):
                    for u in us:
                        tt, b = divmod(u, 2)
                        for i in parts:
                            r, y = i // 2, (yh, yl)[i % 2]
                            ins = mm(ps[:, (0, 1, 6, 7)[u], :], pickT[:, r, tt * P:(tt + 1) * P],
                                     y[:, r, 512 * b:512 * (b + 1)], start=(i == 0), stop=(i == 3))
                        if parts[-1] == 3:
                            ins.then_inc(S.comb_done, 1)

                pe.wait_ge(S.x_added, 4 * n + 4)
                turn_hidden(0)
                if not last:
                    pe.wait_ge(S.pick_ready, 3 * n + 6)
                    gather(S, n + 1, (0, 1))
                pe.wait_ge(S.pt_evac, n + 1)
                turn_hidden(1)
                down_product(0)
                if not last:
                    gather(S, n + 1, (2, 3))
                pe.wait_ge(S.hid_ready, 2 * n + 2)
                down_product(1)
                if not last:
                    turn_pick(S, n + 1)
                    pe.wait_ge(S.xg_evac, 4 * n + 8)
                pe.wait_ge(S.yl_done, 2 * n + 1)
                combine((0, 1), (0, 1))
                pe.wait_ge(S.yh_done, 2 * n + 2)
                combine((0, 1), (2,))
                pe.wait_ge(S.yl_done, 2 * n + 2)
                combine((0, 1), (3,))
                combine((2, 3), (0, 1, 2, 3))

            def banks_free(n):
                S = main[0]
                pe.wait_ge(S.x_added, 4 * n + 4)
                pe.wait_ge(S.xg_evac, 4 * n + 4)

            def turn_constants():
                banks_free(TURNS[0])
                pe.wait_ge(craw_loaded, 64)
                for r in range(2):
                    for i in range(KT):
                        ins = nc.tensor.transpose(ps[:, 2 * r + i // 4, (i % 4) * P:(i % 4 + 1) * P],
                                                  c_raw[:, r, i].rearrange("p u n -> p (u n)"), ident[:])
                ins.then_inc(c_turned, 1)
                pe.wait_ge(par_ready, 1)
                for j, src in enumerate((4, 1, 2, 9, 8)):
                    ins = nc.tensor.transpose(ps[:, 6, j * ST:(j + 1) * ST], disc[:, src, :], ident[0:ST, 0:ST])
                ins.then_inc(par_turned, 1)
                pe.wait_ge(par_evac, 1)

            def turn_inputs():
                banks_free(TURNS[1])
                pe.wait_ge(b_ready, 1)
                for r in range(2):
                    for i in range(KT):
                        ins = nc.tensor.transpose(ps[:, 2 * r + i // 4, (i % 4) * P:(i % 4 + 1) * P],
                                                  b_blk[:, r, 4 * i:4 * i + 4].rearrange("p s c -> p (s c)"), ident[:])
                ins.then_inc(b_turned, 1)
                pe.wait_ge(bT_evac, 1)

            def layer_moe(layer):
                keep_warm((7, 5)[layer], WARM["norm"])
                turn(2 * layer + 1)
                router(layer)
                pe.wait_ge(xl_ready, 2 * layer + 2)
                def one_pass(n, last):
                    moe_pe(main[layer], n, full_before(layer), 16 * NQ * layer, 32, 16, last)

                moe_start(main[layer], 0)
                if layer == 0:
                    with pe.Fori(0, TURNS[0]) as it:
                        one_pass(it, False)
                    turn_constants()
                    with pe.Fori(TURNS[0], TURNS[1]) as it:
                        one_pass(it, False)
                    turn_inputs()
                    with pe.Fori(TURNS[1], NQ - 1) as it:
                        one_pass(it, False)
                else:
                    with pe.Fori(0, NQ - 1) as it:
                        one_pass(it, False)
                one_pass(NQ - 1, True)
                pe.wait_ge(count_ready, layer + 1)
                most = pe.value_load(count_i[0:1, layer:layer + 1], min_val=0, max_val=T)
                with pe.If(most > CAP):
                    pe.sem_inc(more[layer].ring_passed, 1)
                    def one_more(n, last):
                        moe_pe(more[layer], n, 0, 0, 192, 192, last)
                        pe.wait_ge(more[layer].down_done, 2 * n + 2)
                        pe.sem_inc(more[layer].ring_passed, 1)

                    with pe.Fori(0, WINDOWS - 1) as w:
                        moe_start(more[layer], w * NQ)
                        with pe.Fori(0, NQ - 1) as it:
                            one_more(w * NQ + it, False)
                        one_more(w * NQ + NQ - 1, True)
                pe.nop()

            layer_moe(0)

            keep_warm(5, WARM["state-space norm"])
            turn(2)

            def inputs(o, h):
                if o:
                    pe.wait_ge(bu_used, 2 * (o - 1) + h + 1)
                for r in range(2):
                    for j in range(2 * h, 2 * h + 2):
                        rows = slice(32 * j, 32 * (j + 1))
                        ins = mm(ps[:, j, T * r:T * (r + 1)], bT[rows, r, o, :], xnT[rows, o, :],
                                 start=True, stop=True, tile_position=(32 * j, 0))
                ins.then_inc(bu_done, 1)

            def outputs(o, r):
                pe.wait_ge(q_ready, 2 * o + r + 1)
                if r == 0 and o >= 2:
                    pe.wait_ge(gelu_in, o - 1)
                for j in range(4):
                    rows = slice(32 * j, 32 * (j + 1))
                    ins = mm(ps[rows, 4 + o % 2, 0:T], cT[:, r, 4 * o + j, :],
                             qb[:, r, :].rearrange("p (k j t) -> p k j t", k=NCH, t=CH)[:, :, j, :],
                             start=(r == 0), stop=(r == 1), tile_position=(0, 32 * j))
                ins.then_inc(q_used, 1)
                if r:
                    pe.wait_ge(q_used, 2 * o + 2)
                    pe.sem_inc(y_done, 1)

            def unit(u, kts):
                s, tt = divmod(u, TT)
                if kts[0] == 0:
                    pe.wait_ge(slot_full[s], full_before(1))
                    if 2 <= u < 6:
                        pe.wait_ge(bu_used, 2 * KT)
                    elif u >= 6:
                        pe.wait_ge(glu_added, u - 5)
                pe.wait_ge(gelu_done, kts[-1] + 1)
                w = ring[:, s, 0:KT * 2 * WCOL].rearrange("p (k n) -> p k n", k=KT)
                for kt in kts:
                    ins = mm(ps[:, glu_bank(u), :], yT[:, kt, tt * P:(tt + 1) * P], w[:, kt, :],
                             start=(kt == 0), stop=(kt == KT - 1))
                if kts[-1] == KT - 1:
                    ins.then_inc(glu_done, 1)
                    if tt == 1:
                        pe.wait_ge(glu_done, u + 1)
                        pe.sem_inc(slot_free[s], 1)

            for o in range(2):
                for r in range(2):
                    inputs(o, r)
            for o in range(KT):
                if o + 2 < KT:
                    inputs(o + 2, 0)
                if o >= 2:
                    for u in range(2):
                        unit(u, (o - 2,))
                if o == KT - 1:
                    unit(2, range(KT - 4, KT - 2))
                    unit(3, range(KT - 2))
                outputs(o, 0)
                if o + 2 < KT:
                    inputs(o + 2, 1)
                if o == KT - 2:
                    unit(2, range(KT - 4))
                if o == KT - 1:
                    unit(4, range(KT - 2))
                outputs(o, 1)
            unit(5, range(KT - 2))
            for u in range(2 * RING):
                unit(u, range(KT - 2 if u < 6 else 0, KT))
            layer_moe(1)


_INS = ["x", "norm_mix", "norm_ffn", "norm_final", "attn_w_qkv", "attn_w_o", "attn_rel_bias", "ssm_lambda_re",
        "ssm_lambda_im", "ssm_log_step", "ssm_b_re", "ssm_b_im", "ssm_c_re", "ssm_c_im", "ssm_d", "ssm_w_out",
        "moe_w_group_router", "moe_b_group_router", "moe_w_expert_router", "moe_b_expert_router", "moe_w_gate",
        "moe_w_up", "moe_w_down"]


def kernel(**inputs):
    import concourse.bacc as bacc
    from concourse.bass_utils import run_bass_kernel_spmd

    nc = bacc.Bacc("TRN2", target_bir_lowering=False, num_devices=1)
    arrays, aps = {}, {}
    for name in _INS:
        arr = np.ascontiguousarray(inputs[name])
        arrays[f"in_{name}"] = arr
        aps[name] = nc.dram_tensor(f"in_{name}", arr.shape, mybir.dt.from_np(arr.dtype), kind="ExternalInput").ap()
    out = nc.dram_tensor("out_0", (1, T, D), F32, kind="ExternalOutput").ap()
    trunk_program(nc, aps, out)
    r = run_bass_kernel_spmd(nc, [arrays], core_ids=[0])
    return r.results[0]["out_0"]
```
